# Optimizing a Trainium2 kernel written in Bass

```python
import math
import jax, jax.numpy as jnp
from jax import lax
import numpy as np

D_MODEL = 1024
BATCH = 1
SEQ = 256
DEPTH = 2

N_META = 16
D_MIX = D_MODEL
ATTN_WIDTH = D_MIX // 2
CONV_CH = D_MIX - ATTN_WIDTH
N_ATTN_HEADS = 4
V_HEAD_DIM = ATTN_WIDTH // N_ATTN_HEADS
HEAD_DIM = V_HEAD_DIM // 2
QK_WIDTH = N_ATTN_HEADS * 2 * HEAD_DIM
IN_WIDTH = 2 * QK_WIDTH + ATTN_WIDTH + 2 * CONV_CH
CONV_WIDTH = 31
D_FF = -(-8 * D_MODEL // (3 * 256)) * 256
ROPE_THETA = 10000.0
Q_BLOCK = 128
NORM_EPS = 1e-5


def rmsnorm(x, g):
    x32 = x.astype(jnp.float32)
    y = x32 * lax.rsqrt(jnp.mean(x32 * x32, axis=-1, keepdims=True) + NORM_EPS)
    return (y * g.astype(jnp.float32)).astype(x.dtype)

def layer_norm(x, g, b):
    x32 = x.astype(jnp.float32)
    mu = jnp.mean(x32, axis=-1, keepdims=True)
    xc = x32 - mu
    y = xc * lax.rsqrt(jnp.mean(xc * xc, axis=-1, keepdims=True) + NORM_EPS)
    return (y * g.astype(jnp.float32) + b.astype(jnp.float32)).astype(x.dtype)

def rope_tables(length, dtype):
    pos = jnp.arange(length, dtype=jnp.float32)
    inv = ROPE_THETA ** (-jnp.arange(0, HEAD_DIM, 2, dtype=jnp.float32) / HEAD_DIM)
    ang = pos[:, None] * inv[None, :]
    ang = jnp.concatenate([ang, ang], axis=-1)
    return jnp.cos(ang).astype(dtype), jnp.sin(ang).astype(dtype)

def apply_rope(t, cos, sin):
    c = cos[None, :, None, None, :]
    s = sin[None, :, None, None, :]
    t1, t2 = jnp.split(t, 2, axis=-1)
    return t * c + jnp.concatenate([-t2, t1], axis=-1) * s

def diff_attention(q, k, v, lam, sub_g, lam_init):
    B, L = q.shape[0], q.shape[1]
    n_blk = -(-L // Q_BLOCK)
    L_pad = n_blk * Q_BLOCK
    pad = L_pad - L
    q = jnp.pad(q, ((0, 0), (0, pad), (0, 0), (0, 0), (0, 0)))
    k = jnp.pad(k, ((0, 0), (0, pad), (0, 0), (0, 0), (0, 0)))
    v = jnp.pad(v, ((0, 0), (0, pad), (0, 0), (0, 0)))
    qb = q.reshape(B, n_blk, Q_BLOCK, N_ATTN_HEADS, 2, HEAD_DIM).transpose(1, 0, 2, 3, 4, 5)
    k_pos = jnp.arange(L_pad)
    scale = HEAD_DIM ** -0.5

    def one_block(args):
        q_blk, start = args
        s = jnp.einsum('bqhcd,bkhcd->bhcqk', q_blk, k).astype(jnp.float32) * scale
        q_pos = start + jnp.arange(Q_BLOCK)
        mask = k_pos[None, :] <= q_pos[:, None]
        s = jnp.where(mask, s, -jnp.inf)
        p = jax.nn.softmax(s, axis=-1)
        a = p[:, :, 0] - lam * p[:, :, 1]
        return jnp.einsum('bhqk,bkhe->bqhe', a.astype(v.dtype), v)

    starts = jnp.arange(n_blk) * Q_BLOCK
    o = lax.map(one_block, (qb, starts))
    o = o.transpose(1, 0, 2, 3, 4).reshape(B, L_pad, N_ATTN_HEADS, V_HEAD_DIM)[:, :L]
    o = rmsnorm(o, sub_g) * (1.0 - lam_init)
    return o.reshape(B, L, ATTN_WIDTH)

def conformer_conv(u, conv_w, conv_b, ln_g, ln_b):
    a, gate = jnp.split(u, 2, axis=-1)
    z = a * jax.nn.sigmoid(gate)
    z = lax.conv_general_dilated(
        z, conv_w[:, None, :], window_strides=(1,), padding=((CONV_WIDTH - 1, 0),),
        dimension_numbers=('NWC', 'WIO', 'NWC'), feature_group_count=CONV_CH)
    z = z + conv_b
    z = layer_norm(z, ln_g, ln_b)
    return jax.nn.silu(z)

def first_inputs(seed: int = 0) -> dict:
    key = jax.random.key(seed)
    ks = jax.random.split(key, 20)
    f = jnp.float32
    nrm = lambda k, shape, s: jax.random.normal(k, shape, f) * s
    return {
        "x": nrm(ks[0], (BATCH, SEQ, D_MODEL), 1.0),
        "meta_tokens": nrm(ks[1], (N_META, D_MODEL), 1.0),
        "norm1_g": 1.0 + nrm(ks[2], (DEPTH, D_MODEL), 0.02),
        "w_in": nrm(ks[3], (DEPTH, D_MODEL, IN_WIDTH), D_MODEL ** -0.5),
        "b_glu": nrm(ks[4], (DEPTH, 2 * CONV_CH), 0.02),
        "conv_w": nrm(ks[5], (DEPTH, CONV_WIDTH, CONV_CH), CONV_WIDTH ** -0.5),
        "conv_b": nrm(ks[6], (DEPTH, CONV_CH), 0.02),
        "conv_ln_g": 1.0 + nrm(ks[7], (DEPTH, CONV_CH), 0.02),
        "conv_ln_b": nrm(ks[8], (DEPTH, CONV_CH), 0.02),
        "lam_q1": nrm(ks[9], (DEPTH, HEAD_DIM), 0.1),
        "lam_k1": nrm(ks[10], (DEPTH, HEAD_DIM), 0.1),
        "lam_q2": nrm(ks[11], (DEPTH, HEAD_DIM), 0.1),
        "lam_k2": nrm(ks[12], (DEPTH, HEAD_DIM), 0.1),
        "subln_g": 1.0 + nrm(ks[13], (DEPTH, V_HEAD_DIM), 0.02),
        "w_out": nrm(ks[14], (DEPTH, D_MIX, D_MODEL), D_MIX ** -0.5),
        "norm2_g": 1.0 + nrm(ks[15], (DEPTH, D_MODEL), 0.02),
        "w_gate_up": nrm(ks[16], (DEPTH, D_MODEL, 2 * D_FF), D_MODEL ** -0.5),
        "w_down": nrm(ks[17], (DEPTH, D_FF, D_MODEL), D_FF ** -0.5),
        "final_g": 1.0 + nrm(ks[18], (D_MODEL,), 0.02),
    }

def first_block(x, meta_tokens, norm1_g, w_in, b_glu, conv_w, conv_b, conv_ln_g, conv_ln_b,
              lam_q1, lam_k1, lam_q2, lam_k2, subln_g, w_out, norm2_g, w_gate_up, w_down,
              final_g):
    B, S, D = x.shape
    meta = jnp.broadcast_to(meta_tokens[None].astype(x.dtype), (B, N_META, D))
    h = jnp.concatenate([meta, x], axis=1)
    L = S + N_META
    cos, sin = rope_tables(L, x.dtype)
    for l in range(DEPTH):
        lam_init = 0.8 - 0.6 * math.exp(-0.3 * l)
        hn = rmsnorm(h, norm1_g[l])
        proj = hn @ w_in[l]
        q, k, v, u = jnp.split(proj, [QK_WIDTH, 2 * QK_WIDTH, 2 * QK_WIDTH + ATTN_WIDTH], axis=-1)
        q = apply_rope(q.reshape(B, L, N_ATTN_HEADS, 2, HEAD_DIM), cos, sin)
        k = apply_rope(k.reshape(B, L, N_ATTN_HEADS, 2, HEAD_DIM), cos, sin)
        v = v.reshape(B, L, N_ATTN_HEADS, V_HEAD_DIM)
        lam = (jnp.exp(jnp.sum(lam_q1[l].astype(jnp.float32) * lam_k1[l].astype(jnp.float32)))
               - jnp.exp(jnp.sum(lam_q2[l].astype(jnp.float32) * lam_k2[l].astype(jnp.float32)))
               + lam_init)
        attn_out = diff_attention(q, k, v, lam, subln_g[l], lam_init)
        conv_out = conformer_conv(u + b_glu[l], conv_w[l], conv_b[l],
                                  conv_ln_g[l], conv_ln_b[l])
        h = h + jnp.concatenate([attn_out, conv_out], axis=-1) @ w_out[l]
        hn = rmsnorm(h, norm2_g[l])
        gate, up = jnp.split(hn @ w_gate_up[l], 2, axis=-1)
        h = h + (jax.nn.silu(gate) * up) @ w_down[l]
    h = rmsnorm(h, final_g)
    return h[:, N_META:]


DEPTH_2 = 1

GDN_HEADS = 8
GDN_DK = 128
GDN_DV = 128
GDN_CONV = 4
GDN_CHUNK = 64
DIL_PATTERN = ((128, 1), (512, 4), (2048, 16))
DIL_HEADS_PER_GROUP = 4
DIL_HD = 128
DIL_BLOCK = 128
N_EXPERTS = 64
TOP_K = 8
N_GROUPS = 8
TOPK_GROUPS = 4
D_EXPERT = 256
D_SHARED = 256
ROUTE_SCALE = 2.5
MOE_TOKEN_BLOCK = 512
EPS = 1e-6

GDN_QK_W = GDN_HEADS * GDN_DK
GDN_V_W = GDN_HEADS * GDN_DV
N_DIL_GROUPS = len(DIL_PATTERN)
DIL_HEADS = N_DIL_GROUPS * DIL_HEADS_PER_GROUP
DIL_W = DIL_HEADS * DIL_HD
DIL_OUT_W = DIL_HEADS_PER_GROUP * DIL_HD
SPLIT_WIDTHS = (GDN_QK_W, GDN_QK_W, GDN_V_W, GDN_V_W, GDN_HEADS, GDN_HEADS,
                DIL_W, DIL_W, DIL_W, D_MODEL, D_MODEL)
IN_W = sum(SPLIT_WIDTHS)
SPLIT_OFFSETS = tuple(sum(SPLIT_WIDTHS[:i + 1]) for i in range(len(SPLIT_WIDTHS) - 1))


def _rms(t, g):
    t32 = t.astype(jnp.float32)
    return t32 * lax.rsqrt(jnp.mean(t32 * t32, axis=-1, keepdims=True) + EPS) * g.astype(jnp.float32)

def _l2norm(t):
    return t * lax.rsqrt(jnp.sum(t * t, axis=-1, keepdims=True) + EPS)

def causal_depthwise_conv(x, w):
    K, C = w.shape
    return lax.conv_general_dilated(x, w[:, None, :], window_strides=(1,), padding=((K - 1, 0),),
                                    dimension_numbers=('NWC', 'WIO', 'NWC'), feature_group_count=C)

def chunk_gated_delta_rule(q, k, v, g, beta):
    B, H, S, dk = q.shape
    dv = v.shape[-1]
    C = GDN_CHUNK
    N = S // C
    q = q.reshape(B, H, N, C, dk)
    k = k.reshape(B, H, N, C, dk)
    v = v.reshape(B, H, N, C, dv)
    g = g.reshape(B, H, N, C)
    beta = beta.reshape(B, H, N, C)
    gc = jnp.cumsum(g, axis=-1)
    incl = jnp.tril(jnp.ones((C, C), bool))
    strict = jnp.tril(jnp.ones((C, C), bool), -1)
    decay = jnp.exp(jnp.where(incl, gc[..., :, None] - gc[..., None, :], -jnp.inf))
    k_beta = k * beta[..., None]
    a_mat = jnp.where(strict, jnp.einsum('bhnid,bhnjd->bhnij', k_beta, k) * decay, 0.0)
    lmat = a_mat + jnp.eye(C, dtype=a_mat.dtype)
    rhs = jnp.concatenate([v * beta[..., None], k_beta * jnp.exp(gc)[..., None]], axis=-1)
    sol = lax.linalg.triangular_solve(lmat, rhs, left_side=True, lower=True, unit_diagonal=True)
    u, w = sol[..., :dv], sol[..., dv:]
    qk = jnp.einsum('bhnid,bhnjd->bhnij', q, k) * decay
    q_dec = q * jnp.exp(gc)[..., None]
    k_dec = k * jnp.exp(gc[..., -1:] - gc)[..., None]
    g_tot = jnp.exp(gc[..., -1])

    def step(state, xs):
        u_n, w_n, qk_n, qd_n, kd_n, gt_n = xs
        v_new = u_n - jnp.einsum('bhck,bhkv->bhcv', w_n, state)
        o_n = jnp.einsum('bhck,bhkv->bhcv', qd_n, state) + jnp.einsum('bhij,bhjv->bhiv', qk_n, v_new)
        state = state * gt_n[..., None, None] + jnp.einsum('bhck,bhcv->bhkv', kd_n, v_new)
        return state, o_n

    xs = tuple(jnp.moveaxis(t, 2, 0) for t in (u, w, qk, q_dec, k_dec, g_tot))
    state0 = jnp.zeros((B, H, dk, dv), q.dtype)
    _, o = lax.scan(step, state0, xs)
    return jnp.moveaxis(o, 0, 2).reshape(B, H, S, dv)

def gated_deltanet(q, k, v, z, b, a, conv_w, a_log, dt_bias, norm_g):
    B, S, _ = q.shape
    f32 = jnp.float32
    qkv = jnp.concatenate([q, k, v], axis=-1).astype(f32)
    qkv = jax.nn.silu(causal_depthwise_conv(qkv, conv_w.astype(f32)))
    q, k, v = jnp.split(qkv, [GDN_QK_W, 2 * GDN_QK_W], axis=-1)

    def heads(t, d):
        return t.reshape(B, S, GDN_HEADS, d).transpose(0, 2, 1, 3)

    q = _l2norm(heads(q, GDN_DK)) * (GDN_DK ** -0.5)
    k = _l2norm(heads(k, GDN_DK))
    v = heads(v, GDN_DV)
    beta = jax.nn.sigmoid(b.astype(f32)).transpose(0, 2, 1)
    g = (-jnp.exp(a_log.astype(f32)) * jax.nn.softplus(a.astype(f32) + dt_bias.astype(f32))).transpose(0, 2, 1)
    o = chunk_gated_delta_rule(q, k, v, g, beta).transpose(0, 2, 1, 3)
    zg = jax.nn.silu(z.astype(f32).reshape(B, S, GDN_HEADS, GDN_DV))
    o = _rms(o, norm_g) * zg
    return o.reshape(B, S, GDN_V_W)

def dilated_window_attention(q, k, v, window, dilation):
    B, S, h, e = q.shape
    L = S // dilation
    W = window // dilation
    blk = math.gcd(L, DIL_BLOCK)
    nb = L // blk

    def sub(t):
        return t.reshape(B, L, dilation, h, e).transpose(0, 2, 3, 1, 4)

    qs = sub(q).reshape(B, dilation, h, nb, blk, e)
    key_idx = np.arange(nb)[:, None] * blk + np.arange(blk + W)[None, :]
    pad = ((0, 0), (0, 0), (0, 0), (W, 0), (0, 0))
    ks = jnp.pad(sub(k), pad)[:, :, :, key_idx]
    vs = jnp.pad(sub(v), pad)[:, :, :, key_idx]
    dist = np.arange(blk)[:, None] + W - np.arange(blk + W)[None, :]
    valid = (dist >= 0) & (dist <= W) & ((key_idx[:, None, :] - W) >= 0)
    s = jnp.einsum('bdhnqe,bdhnke->bdhnqk', qs, ks) * (e ** -0.5)
    s = jnp.where(valid, s, -jnp.inf)
    m = jnp.max(s, axis=-1, keepdims=True)
    p = jnp.exp(s - m)
    den = jnp.sum(p, axis=-1, keepdims=True)
    o = jnp.einsum('bdhnqk,bdhnke->bdhnqe', p, vs) / den
    lse = (m + jnp.log(den))[..., 0]
    o = o.reshape(B, dilation, h, L, e).transpose(0, 3, 1, 2, 4).reshape(B, S, h, e)
    lse = lse.reshape(B, dilation, h, L).transpose(0, 3, 1, 2).reshape(B, S, h)
    return o, lse

def dilated_mixture(q, k, v, q_norm_g, k_norm_g):
    B, S, _ = q.shape
    q = _rms(q.reshape(B, S, DIL_HEADS, DIL_HD), q_norm_g)
    k = _rms(k.reshape(B, S, DIL_HEADS, DIL_HD), k_norm_g)
    v = v.reshape(B, S, DIL_HEADS, DIL_HD).astype(jnp.float32)
    outs, lses = [], []
    for gi, (win, dil) in enumerate(DIL_PATTERN):
        hs = slice(gi * DIL_HEADS_PER_GROUP, (gi + 1) * DIL_HEADS_PER_GROUP)
        o, lse = dilated_window_attention(q[:, :, hs], k[:, :, hs], v[:, :, hs], win, dil)
        outs.append(o)
        lses.append(lse)
    wts = jax.nn.softmax(jnp.stack(lses), axis=0)
    y = jnp.einsum('gbsh,gbshe->bshe', wts, jnp.stack(outs))
    return y.reshape(B, S, DIL_OUT_W)

def moe_ffn(h, w_router, router_bias, w_gate, w_up, w_down, ws_gate, ws_up, ws_down):
    B, S, D = h.shape
    T = B * S
    f32 = jnp.float32
    ht = h.reshape(T, D)
    scores = jax.nn.sigmoid(ht.astype(f32) @ w_router.astype(f32))
    sel = scores + router_bias.astype(f32)
    grp = sel.reshape(T, N_GROUPS, N_EXPERTS // N_GROUPS)
    grp_score = jnp.sum(lax.top_k(grp, 2)[0], axis=-1)
    _, gidx = lax.top_k(grp_score, TOPK_GROUPS)
    gmask = jnp.sum(jax.nn.one_hot(gidx, N_GROUPS, dtype=f32), axis=1)
    emask = jnp.repeat(gmask, N_EXPERTS // N_GROUPS, axis=1) > 0
    _, eidx = lax.top_k(jnp.where(emask, sel, -jnp.inf), TOP_K)
    wk = jnp.take_along_axis(scores, eidx, axis=-1)
    wk = wk / jnp.sum(wk, axis=-1, keepdims=True) * ROUTE_SCALE
    combine = jnp.einsum('tk,tke->te', wk, jax.nn.one_hot(eidx, N_EXPERTS, dtype=f32)).astype(h.dtype)
    tb = math.gcd(T, MOE_TOKEN_BLOCK)

    def block(args):
        hb, cb = args
        a = jnp.einsum('td,edf->tef', hb, w_gate)
        u = jnp.einsum('td,edf->tef', hb, w_up)
        return jnp.einsum('tef,efd->td', jax.nn.silu(a) * u * cb[..., None], w_down)

    routed = lax.map(block, (ht.reshape(T // tb, tb, D), combine.reshape(T // tb, tb, N_EXPERTS))).reshape(T, D)
    shared = (jax.nn.silu(ht @ ws_gate) * (ht @ ws_up)) @ ws_down
    return (routed + shared).reshape(B, S, D)

def second_inputs(seed: int = 0) -> dict:
    key = jax.random.key(seed)
    ks = jax.random.split(key, 24)
    L, D, E = DEPTH_2, D_MODEL, N_EXPERTS
    nrm = lambda k, shape, scale: jax.random.normal(k, shape, jnp.float32) * scale
    dt = jnp.exp(jax.random.uniform(ks[7], (L, GDN_HEADS), jnp.float32, math.log(1e-3), math.log(1e-1)))
    return {
        "x": nrm(ks[0], (BATCH, SEQ, D), 1.0),
        "c": nrm(ks[1], (BATCH, D), 1.0),
        "w_ada": nrm(ks[2], (L, D, 6 * D), 0.5 * D ** -0.5),
        "b_ada": nrm(ks[3], (L, 6 * D), 0.02),
        "g_mix": 1.0 + nrm(ks[4], (L, D), 0.05),
        "w_in": nrm(ks[5], (L, D, IN_W), D ** -0.5),
        "gdn_conv_w": nrm(ks[6], (L, GDN_CONV, 2 * GDN_QK_W + GDN_V_W), 0.5),
        "gdn_a_log": jnp.log(jax.random.uniform(ks[8], (L, GDN_HEADS), jnp.float32, 1.0, 16.0)),
        "gdn_dt_bias": dt + jnp.log(-jnp.expm1(-dt)),
        "gdn_norm_g": 1.0 + nrm(ks[9], (L, GDN_DV), 0.05),
        "dil_q_norm_g": 1.0 + nrm(ks[10], (L, DIL_HD), 0.05),
        "dil_k_norm_g": 1.0 + nrm(ks[11], (L, DIL_HD), 0.05),
        "w_up_gdn": nrm(ks[12], (L, GDN_V_W, D), GDN_V_W ** -0.5),
        "w_up_dil": nrm(ks[13], (L, DIL_OUT_W, D), DIL_OUT_W ** -0.5),
        "w_out": nrm(ks[14], (L, D, D), D ** -0.5),
        "g_ffn": 1.0 + nrm(ks[15], (L, D), 0.05),
        "w_router": nrm(ks[16], (L, D, E), D ** -0.5),
        "router_bias": nrm(ks[17], (L, E), 0.01),
        "w_exp_gate": nrm(ks[18], (L, E, D, D_EXPERT), D ** -0.5),
        "w_exp_up": nrm(ks[19], (L, E, D, D_EXPERT), D ** -0.5),
        "w_exp_down": nrm(ks[20], (L, E, D_EXPERT, D), D_EXPERT ** -0.5),
        "w_sh_gate": nrm(ks[21], (L, D, D_SHARED), D ** -0.5),
        "w_sh_up": nrm(ks[22], (L, D, D_SHARED), D ** -0.5),
        "w_sh_down": nrm(ks[23], (L, D_SHARED, D), D_SHARED ** -0.5),
    }

def second_block(x, c, w_ada, b_ada, g_mix, w_in, gdn_conv_w, gdn_a_log, gdn_dt_bias, gdn_norm_g,
              dil_q_norm_g, dil_k_norm_g, w_up_gdn, w_up_dil, w_out, g_ffn, w_router, router_bias,
              w_exp_gate, w_exp_up, w_exp_down, w_sh_gate, w_sh_up, w_sh_down):
    cs = jax.nn.silu(c)
    for l in range(DEPTH_2):
        mod = (cs @ w_ada[l] + b_ada[l])[:, None, :]
        sh1, sc1, gt1, sh2, sc2, gt2 = jnp.split(mod, 6, axis=-1)
        h = _rms(x, g_mix[l]).astype(x.dtype) * (1.0 + sc1) + sh1
        proj = h @ w_in[l]
        (gq, gk, gv, gz, gb, ga, dil_q, dil_k, dil_v, gate_a, gate_b) = jnp.split(proj, SPLIT_OFFSETS, axis=-1)
        y_a = gated_deltanet(gq, gk, gv, gz, gb, ga, gdn_conv_w[l], gdn_a_log[l], gdn_dt_bias[l],
                             gdn_norm_g[l]).astype(x.dtype)
        y_b = dilated_mixture(dil_q, dil_k, dil_v, dil_q_norm_g[l], dil_k_norm_g[l]).astype(x.dtype)
        merged = jax.nn.sigmoid(gate_a) * (y_a @ w_up_gdn[l]) + jax.nn.sigmoid(gate_b) * (y_b @ w_up_dil[l])
        x = x + gt1 * (merged @ w_out[l])
        h2 = _rms(x, g_ffn[l]).astype(x.dtype) * (1.0 + sc2) + sh2
        x = x + gt2 * moe_ffn(h2, w_router[l], router_bias[l], w_exp_gate[l], w_exp_up[l], w_exp_down[l],
                              w_sh_gate[l], w_sh_up[l], w_sh_down[l])
    return x


def setup_inputs(seed=0):
    out = dict(first_inputs(seed))
    for name, value in second_inputs(seed + 1).items():
        if name != "x":
            out[name + "_2"] = value
    return out


def reference(
    x, meta_tokens, norm1_g, w_in, b_glu, conv_w, conv_b, conv_ln_g, conv_ln_b, lam_q1, lam_k1,
    lam_q2, lam_k2, subln_g, w_out, norm2_g, w_gate_up, w_down, final_g, c_2, w_ada_2, b_ada_2,
    g_mix_2, w_in_2, gdn_conv_w_2, gdn_a_log_2, gdn_dt_bias_2, gdn_norm_g_2, dil_q_norm_g_2,
    dil_k_norm_g_2, w_up_gdn_2, w_up_dil_2, w_out_2, g_ffn_2, w_router_2, router_bias_2,
    w_exp_gate_2, w_exp_up_2, w_exp_down_2, w_sh_gate_2, w_sh_up_2, w_sh_down_2,
):
    x = first_block(
        x, meta_tokens, norm1_g, w_in, b_glu, conv_w, conv_b, conv_ln_g, conv_ln_b, lam_q1,
        lam_k1, lam_q2, lam_k2, subln_g, w_out, norm2_g, w_gate_up, w_down, final_g,
    )
    return second_block(
        x, c_2, w_ada_2, b_ada_2, g_mix_2, w_in_2, gdn_conv_w_2, gdn_a_log_2, gdn_dt_bias_2,
        gdn_norm_g_2, dil_q_norm_g_2, dil_k_norm_g_2, w_up_gdn_2, w_up_dil_2, w_out_2, g_ffn_2,
        w_router_2, router_bias_2, w_exp_gate_2, w_exp_up_2, w_exp_down_2, w_sh_gate_2,
        w_sh_up_2, w_sh_down_2,
    )


_drawn_inputs = setup_inputs


def setup_inputs(seed=0):
    import zlib

    import numpy as np

    out = dict(_drawn_inputs(seed))
    spreads = {}
    factors = {'gdn_norm_g_2': 3.454, 'dil_q_norm_g_2': 6.506, 'dil_k_norm_g_2': 4.086}
    for name, (base, spread) in spreads.items():
        noise = np.random.default_rng([zlib.crc32(name.encode()), seed]).standard_normal(out[name].shape)
        drawn = base * np.exp(spread * noise) if base else spread * noise
        out[name] = __import__('jax').numpy.asarray(drawn.astype(out[name].dtype))
    for name, factor in factors.items():
        out[name] = (out[name] * factor).astype(out[name].dtype)
    return out
```

```python
from contextlib import ExitStack
import math

import numpy as np
import concourse.bass as bass
from concourse import mybir

ALU = mybir.AluOpType
ACT = mybir.ActivationFunctionType
F32 = mybir.dt.float32
AX_X = mybir.AxisListType.X
ds = bass.ds

P = 128
D = 1024
DC = D // P

DEPTH = 2
SEQ = 256
META = 16
L = SEQ + META
HEADS = 4
HD = 64
FF = 2816
FC = FF // P
TAPS = 31
PAD = TAPS - 1
CC = 4
Q_TILES = [(0, 128), (128, 128), (256, 16)]
EPS1 = 1e-5
UNITS = [(h, t) for h in range(HEADS) for t in range(3)]

RING = 6
SLOT = 2048
IN_SLOTS, ADA_SLOTS, OUT_SLOTS, GU_SLOTS, DN_SLOTS = 10, 12, 4, FC, 12
OUT0 = IN_SLOTS + ADA_SLOTS
LAYER_SLOTS = OUT0 + OUT_SLOTS + GU_SLOTS + DN_SLOTS
assert LAYER_SLOTS % RING == 0

T = SEQ
GH = 8
CHUNK = 64
DG = 3
WINDOW_DILATION = ((128, 1), (512, 4), (2048, 16))
EXPERTS = 64
TOP = 8
GROUPS = 8
TOP_GROUPS = 4
EPS2 = 1e-6
NEG = -1e30
ROUTE_SCALE = 2.5
B2 = DEPTH * LAYER_SLOTS
DIL_SLOTS, GDN_SLOTS = 18, 12
Z0 = DIL_SLOTS + GDN_SLOTS
GATE0 = Z0 + 4
UP0 = GATE0 + 8
OUT2 = UP0 + 6
EX0 = B2 + OUT2 + 4
LOADS = 16 * 8

QMIX, QFFN, QADA, QC, QCW, QGN, QDQ, QDK, QAL, QDT, QRB = np.cumsum([0, 8, 8, 48, 8, 96, 1, 1, 1, 1, 1]).tolist()
NPAR2 = QRB + EXPERTS
KD0, KD1, KLEV, KLOW, KUP = np.cumsum([0, 3 * 128, 3 * 256, 6 * 128, 128]).tolist()
NCST2 = KUP + 128

PN1, PBG, PCW, PCB, PLG, PLB, PSG, PN2, PLAM, PLI, PLO = np.cumsum([0, 8, 8, CC * TAPS, CC, CC, CC, 1, 8, 4, 1]).tolist()
NPAR = PLO + 1


def build(nc, args, dbg=None):
    stream, xT, par1, consts, final_g, out = (args[k] for k in ("stream", "xT", "par1", "consts", "final_g", "out"))
    par2_d, consts2, w_ba_d, w_router_d = (args[k] for k in ("par2", "consts2", "w_ba", "w_router"))
    NSLOT = stream.shape[0]
    TURNS = -(-NSLOT // RING)

    with ExitStack() as ctx:
        def sb(name, shape, dt=F32):
            return ctx.enter_context(nc.sbuf_tensor(name, shape, dt))

        ring = sb("ring", [P, RING, SLOT])
        h = sb("h", [P, DC, L])
        hn = sb("hn", [P, DC, L])
        big = sb("big", [P, 30900])
        cst = sb("cst", [P, consts.shape[1]])
        ones, ident, rot = cst[:, 0:128], cst[:, 128:256], cst[:, 256:384]
        cos, sin = cst[:, 384:384 + L], cst[:, 384 + L:384 + 2 * L]
        o_tie = 384 + 5 * L
        o_mask = 384 + 2 * L
        causal = cst[:, o_mask:o_mask + 3 * L].rearrange("p (t k) -> p t k", t=3)
        par_all = sb("par_all", [P, DEPTH, NPAR])
        par = sb("par", [P, NPAR])
        fin_g = sb("fin_g", [P, DC])
        small = sb("small", [P, 64])
        root = sb("root", [P, HEADS, L])
        inv = sb("inv", [P, HEADS, L])

        at = [0]

        def carve(*shape):
            n = int(np.prod(shape))
            v = big[:, at[0]:at[0] + n]
            at[0] += n
            assert at[0] <= 30900, at
            if len(shape) == 2:
                v = v.rearrange("p (a b) -> p a b", a=shape[0])
            if len(shape) == 3:
                v = v.rearrange("p (a b c) -> p a b c", a=shape[0], b=shape[1])
            return v

        sq = carve(DC, L)
        zpad = carve(CC, PAD + L)
        conv = carve(CC, L)
        sgl = carve(CC, L)
        raw = carve(8, L)
        qk = carve(8, L)
        vT = carve(HEADS, L)
        V = carve(3, HEADS, P)
        rt1 = carve(2, L)
        rt2 = carve(2, L)
        after_w_in = at[0]
        Sm = carve(2, 2, L)
        Pr = carve(2, 2, L)
        Pt = carve(2, L)
        A = carve(2, L)
        aT = carve(2, 3, P)
        oraw = carve(HEADS, L)
        cat = carve(DC, L)
        xc = carve(CC, L)
        lsq = carve(CC, L)
        lnv = carve(CC, L)
        lns = carve(CC, L)
        attn_end = at[0]
        at[0] = PAD * CC + 2176 + CC * L
        hff = carve(FC, L)
        sgu = carve(2, L)
        at[0] = attn_end

        ps = ctx.enter_context(nc.psum_tensor("ps", [P, 8, 512], F32))
        par2 = sb("par2", [P, NPAR2])
        w_ba = sb("w_ba", [P, DC, 16])
        mod = sb("mod", [P, 48])
        cs = sb("cs", [P, DC])
        tiny = sb("tiny", [P, 192])

        def region(o, *shape):
            n = int(np.prod(shape))
            v = big[:, o:o + n]
            names = "abcd"[:len(shape)]
            if len(shape) > 1:
                v = v.rearrange(f"p ({' '.join(names)}) -> p {' '.join(names)}", **dict(zip(names[:-1], shape[:-1])))
            return v

        x = h[:, :, META:L]
        hm = hn[:, :, 0:T]
        sqx = region(0, DC, T)
        c2 = region(0, NCST2)
        yb = region(2176, 4, T)
        dqk = region(3200, 24, T)
        zs = region(3200, GH, T)
        MA = region(5248, 2, GH, P)
        MB = region(7296, 2, GH, P)
        dV = region(9344, 2, 12, P)
        dS = region(12416, 2, 3, T)
        dpT = region(13952, 2, 6, P)
        vst = region(15488, 2, 2, T)
        GB = region(9344, GH, T)
        WT = region(9344, 2, GH, P)
        MT = region(11392, 2, GH, P)
        yo = region(11392, GH, T)
        gt_ = region(11392, 8, T)
        St = region(13440, GH, P)
        vn = region(14464, GH, P)
        MU = region(15488, 2, GH, P)
        sga = region(15488, GH, T)
        gdiag = region(17536, GH, T)
        kbg = region(17536, 2, GH, P)
        sgb = region(17536, GH, T)
        gq = region(19584, GH, T)
        gk = region(21632, GH, T)
        gV = region(23680, 2, GH, P)
        gK = region(25728, 2, GH, P)
        gpad = region(27776, 2, 2, T + 3)
        gacc = region(28812, 2, 2, T)
        sqd = region(29836, 2, 512)
        Ms = region(27776, 2, 4, P)
        Wts = region(28800, 2, 4, P)
        root2 = root[:, :, :].rearrange("p a b -> p (a b)")[:, 0:1024].rearrange("p (a b) -> p a b", a=2)
        inv2 = inv[:, :, :].rearrange("p a b -> p (a b)")[:, 0:1024].rearrange("p (a b) -> p a b", a=2)
        w_r = region(19584, DC, EXPERTS)
        esil = region(9344, 2, 512)
        et = region(10368, 2, 512)
        hid = region(11392, 2, 2, T)
        combT = region(12416, T)
        rhs_e = region(12672, 2, T)
        rt = region(13440, 16, 128)
        flat = ps[:, :, :].rearrange("p a b -> p (a b)")

        COUNT = {}
        SEM = {}

        def sem(name, per_layer=0):
            SEM[name] = ctx.enter_context(nc.semaphore(name))
            COUNT[name] = per_layer
            return SEM[name]

        loaded = sem("loaded")
        stepped = sem("stepped")
        out_done = sem("out_done")
        ring_full = [sem(f"ring_full{j}") for j in range(RING)]
        slot_done = sem("slot_done", LAYER_SLOTS)
        zeroed = sem("zeroed")
        h_added = sem("h_added", 16)
        par_ready = sem("par_ready", 1)
        sq_ready = sem("sq_ready", 4)
        norm_sum = sem("norm_sum", 2)
        norm_root = sem("norm_root", 2)
        hn_ready = sem("hn_ready", 16)
        lam_prod = sem("lam_prod", 1)
        lam_sum = sem("lam_sum", 1)
        lam_exp = sem("lam_exp", 1)
        even_full = sem("even_full", IN_SLOTS + OUT_SLOTS)
        glu_sig = sem("glu_sig", 4)
        glu_done = sem("glu_done", 4)
        raw_ready = sem("raw_ready", 8)
        rot_full = sem("rot_full", 8)
        rot_used = sem("rot_used", 8)
        qk_ready = sem("qk_ready", 8)
        vT_ready = sem("vT_ready", 4)
        vt_full = sem("vt_full", 4)
        v_ready = sem("v_ready", 8)
        conv_ready = sem("conv_ready", 1)
        mu_sum = sem("mu_sum", 1)
        xc_ready = sem("xc_ready", 1)
        lsq_ready = sem("lsq_ready", 1)
        var_sum = sem("var_sum", 1)
        var_root = sem("var_root", 1)
        xn_ready = sem("xn_ready", 1)
        ln_act = sem("ln_act", 8)
        conv_out = sem("conv_out", 4)
        s_full = sem("s_full", 12)
        s_masked = sem("s_masked", 12)
        smax = sem("smax", 12)
        exp_done = sem("exp_done", 24)
        a_ready = sem("a_ready", 12)
        at_full = sem("at_full", 12)
        at_ready = sem("at_ready", 12)
        o_full = sem("o_full", 4)
        o_copied = sem("o_copied", 8)
        osq_ready = sem("osq_ready", 4)
        sub_sum = sem("sub_sum", 1)
        sub_root = sem("sub_root", 1)
        attn_out = sem("attn_out", 4)
        gate_act = sem("gate_act", FC)
        hff_ready = sem("hff_ready", FC)
        at_part = sem("at_part", 4)
        chain_v = sem("chain_v")
        chain_a = sem("chain_a")
        cs_ready = sem("cs_ready")
        x_ready = sem("x_ready")
        mod_ready = sem("mod_ready")
        hm_scaled = sem("hm_scaled")
        hm_ready = sem("hm_ready")
        loaded2 = sem("loaded2")
        padded = sem("padded")
        gemm_out = sem("gemm_out")
        msum = sem("msum")
        mroot = sem("mroot")
        mnorm = sem("mnorm")
        dv_full = sem("dv_full")
        dv_out = sem("dv_out")
        ba_full = sem("ba_full")
        ds_full = sem("ds_full")
        dmask = sem("dmask")
        dmax = sem("dmax")
        dexp = sem("dexp")
        dcoef = sem("dcoef")
        dtp = sem("dtp")
        dpt_ready = sem("dpt_ready")
        do_full = sem("do_full")
        yb_ready = sem("yb_ready")
        gconv = sem("gconv")
        gsilu = sem("gsilu")
        gsq = sem("gsq")
        x_full = sem("x_full")
        x_out = sem("x_out")
        gate_a1 = sem("gate_a1")
        gate_v1 = sem("gate_v1")
        gate_a2 = sem("gate_a2")
        gdiag_ready = sem("gdiag_ready")
        gb_full = sem("gb_full")
        gb_out = sem("gb_out")
        d_built = sem("d_built")
        d_exp = sem("d_exp")
        gcols = sem("gcols")
        kk_full = sem("kk_full")
        l_ready = sem("l_ready")
        qk_full = sem("qk_full")
        qkt_ready = sem("qkt_ready")
        tu_init = sem("tu_init")
        m_ready = sem("m_ready")
        wt_full = sem("wt_full")
        wt_copied = sem("wt_copied")
        tu_full = sem("tu_full")
        tu_done = sem("tu_done")
        pool_scaled = sem("pool_scaled")
        gtot_ready = sem("gtot_ready")
        u_full = sem("u_full")
        u_out = sem("u_out")
        w_full = sem("w_full")
        w_out = sem("w_out")
        vn_full = sem("vn_full")
        vn_ready = sem("vn_ready")
        oc_full = sem("oc_full")
        oc_out = sem("oc_out")
        su_full = sem("su_full")
        s_ready = sem("s_ready")
        ysq = sem("ysq")
        ysum = sem("ysum")
        yroot = sem("yroot")
        ya_ready = sem("ya_ready")
        up_out = sem("up_out")
        merged = sem("merged")
        out_add = sem("out_add")
        sc_full = sem("sc_full")
        sc_ready = sem("sc_ready")
        comb_ready = sem("comb_ready")
        ct_full = sem("ct_full")
        ct_out = sem("ct_out")
        row_ready = sem("row_ready")
        e_silu = sem("e_silu")
        e_prod = sem("e_prod")
        cb_full = sem("cb_full")
        hid_ready = sem("hid_ready")
        y_full = sem("y_full")
        zero_ready = sem("zero_ready")
        hid_primed = sem("hid_primed")
        prod_primed = sem("prod_primed")
        zero_t = big[:, 15488:15616]
        MA_sq = region(5248, 4, 512)
        MB_rt = region(7296, 4, 512)

        block = ctx.enter_context(nc.Block())

        def W(eng, name, value, l=0):
            eng.wait_ge(SEM[name], l * COUNT[name] + value)

        def W_alone(eng, name, value, l=0):
            W(eng, name, value, l)
            eng.sem_inc(stepped, 1)

        def after_layers(name, value):
            return DEPTH * COUNT[name] + value

        @block.sync
        def _(sp):
            sp.dma_start(h[:, :, :], xT).then_inc(loaded, 16)
            sp.dma_start(cst[:, :], consts).then_inc(loaded, 16)
            sp.dma_start(par_all[:, :, :], par1).then_inc(loaded, 16)
            sp.dma_start(fin_g[:, :], final_g).then_inc(loaded, 16)
            sp.dma_start(par2[:, :], par2_d).then_inc(loaded, 16)
            sp.dma_start(w_ba[:, :, :], w_ba_d).then_inc(loaded, 16)
            sp.dma_start(cs[:, :], par2_d[:, QC:QC + DC]).then_inc(loaded, 16)
            sp.dma_start(small[:, 40:48], par2_d[:, QC:QC + DC]).then_inc(loaded, 16)
            for j in range(RING):
                sp.dma_start(ring[:, j, :], stream[j, :, :]).then_inc(ring_full[j], 16)

            def refill(i, j):
                sp.wait_ge(slot_done, i - RING + 1)
                src = stream[i, :, :] if isinstance(i, int) else stream[ds(i, 1), :, :].rearrange("a p n -> (a p) n")
                sp.dma_start(ring[:, j, :], src).then_inc(ring_full[j], 16)

            with sp.Fori(1, NSLOT // RING) as t:
                for j in range(RING):
                    refill(t * RING + j, j)
            for i in range(NSLOT // RING * RING, NSLOT):
                refill(i, i % RING)
            sp.wait_ge(x_ready, 24)
            sp.dma_start(out, x).then_inc(out_done, 16)
            sp.wait_ge(out_done, 16)


        @block.tensor
        def _(pe):
            mm = nc.tensor.matmul

            def slot(s, turn0):
                pe.wait_ge(ring_full[s % RING], (turn0 + s // RING + 1) * 16)
                return ring[:, s % RING, :]

            def norm_sums(l, which):
                for c in range(DC):
                    if c % 4 == 0:
                        W(pe, "sq_ready", 2 * which + c // 4 + 1, l)
                    m = mm(ps[:, 7, 0:L], ones, sq[:, c, :], start=c == 0, stop=c == DC - 1)
                m.then_inc(norm_sum, 1)

            def pair(w, rhs, banks, order=range(DC), cols=L, wait=None, even=True):
                for n in range(2):
                    for q, k in enumerate(order):
                        if n == 0 and wait:
                            wait(k)
                        m = mm(ps[:, banks[n], 0:cols], w[:, k, n, :], rhs[:, k, 0:cols],
                               start=q == 0, stop=q == DC - 1)
                    if n == 0 and even:
                        m.then_inc(even_full, 1)
                m.then_inc(slot_done, 1)

            pe.wait_ge(loaded, LOADS)
            pe.wait_ge(cs_ready, 1)
            with pe.Fori(0, DEPTH) as l:
                turn = l * (LAYER_SLOTS // RING)

                def weights(s, t0=0):
                    return slot(s, turn + t0).rearrange("p (k n c) -> p k n c", k=8, n=2)

                norm_sums(l, 0)
                W(pe, "lam_prod", 1, l)
                mm(ps[:, 6, 0:2], ones[0:HD, :], small[0:HD, 0:2], start=True, stop=True).then_inc(lam_sum, 1)

                def rotate(j):
                    W(pe, "raw_ready", j + 1, l)
                    if j >= 2:
                        W(pe, "rot_used", j - 1, l)
                    mm(ps[:, 4 + j % 2, 0:L], rot, raw[:, j, :], start=True, stop=True).then_inc(rot_full, 1)

                def turn_v(j):
                    W(pe, "vT_ready", j + 1, l)
                    if j >= 2:
                        W(pe, "v_ready", 2 * (j - 1), l)
                    for t, (k0, kn) in enumerate(Q_TILES):
                        m = nc.tensor.transpose(ps[0:kn, 6 + j % 2, t * P:t * P + P], vT[:, j, k0:k0 + kn], ident)
                    m.then_inc(vt_full, 1)

                for s in range(IN_SLOTS):
                    w = weights(s)
                    if 2 <= s < 6:
                        W(pe, "glu_done", s - 1, l)
                    if 6 <= s < 8:
                        W(pe, "raw_ready", 2 * (s - 6) + 2, l)
                    if s >= 8:
                        W(pe, "raw_ready", 2 * (s - 6) + 2, l)
                    pair(w, hn, (2 * (s % 2), 2 * (s % 2) + 1),
                         wait=(lambda k: W(pe, "hn_ready", k + 1, l)) if s == 0 else None)
                    if s >= 5:
                        if s < 9:
                            rotate(2 * (s - 5))
                            rotate(2 * (s - 5) + 1)
                        else:
                            turn_v(0)
                            turn_v(1)
                turn_v(2)
                turn_v(3)

                def scores(u):
                    head, t = UNITS[u]
                    q0, rows = Q_TILES[t]
                    keys = q0 + rows
                    b = 4 + 2 * (u % 2)
                    if u < 2:
                        W(pe, "v_ready", 8, l)
                        W_alone(pe, "qk_ready", 8, l)
                    else:
                        W_alone(pe, "s_masked", u - 1, l)
                    for c in range(2):
                        r = slice(64 * c, 64 * c + 64)
                        m = mm(ps[0:rows, b + c, 0:keys], qk[r, head, q0:q0 + rows], qk[r, HEADS + head, 0:keys],
                               start=True, stop=True)
                    m.then_inc(s_full, 1)

                def turn_probs(u):
                    head, t = UNITS[u]
                    q0, rows = Q_TILES[t]
                    if u >= 2:
                        W(pe, "at_ready", u - 1, l)
                    W_alone(pe, "a_ready", u + 1, l)
                    for kt in range(t + 1):
                        k0, kn = Q_TILES[kt]
                        m = nc.tensor.transpose(ps[0:kn, u % 2, kt * P:kt * P + rows], A[0:rows, u % 2, k0:k0 + kn],
                                                ident[0:rows, 0:rows])
                    m.then_inc(at_full, 1)

                def modulate(u):
                    head, t = UNITS[u]
                    w = weights(IN_SLOTS + u)
                    for n in range(2):
                        for k in range(DC):
                            m = mm(ps[:, 2 + head % 2, L + 2 * t + n:L + 2 * t + n + 1], w[:, k, n, :], cs[:, k:k + 1],
                                   start=k == 0, stop=k == DC - 1)
                    m.then_inc(slot_done, 1)

                def weigh(u):
                    head, t = UNITS[u]
                    q0, rows = Q_TILES[t]
                    if head >= 2 and t == 0:
                        W(pe, "osq_ready", head - 1, l)
                    modulate(u)
                    W(pe, "at_ready", u + 1, l)
                    for kt in range(t + 1):
                        kn = Q_TILES[kt][1]
                        m = mm(ps[:, 2 + head % 2, q0:q0 + rows], V[0:kn, kt, head, :], aT[0:kn, u % 2, kt, 0:rows],
                               start=kt == 0, stop=kt == t)
                    if t == 2:
                        m.then_inc(o_full, 1)

                W(pe, "vT_ready", 4, l)
                W(pe, "conv_ready", 1, l)
                for c in range(CC):
                    m = mm(ps[:, 0, 0:L], ones, conv[:, c, :], start=c == 0, stop=c == CC - 1)
                m.then_inc(mu_sum, 1)
                scores(0)
                scores(1)
                W(pe, "lsq_ready", 1, l)
                for c in range(CC):
                    m = mm(ps[:, 1, 0:L], ones, lsq[:, c, :], start=c == 0, stop=c == CC - 1)
                m.then_inc(var_sum, 1)
                W(pe, "var_root", 1, l)
                for u in range(12):
                    turn_probs(u)
                    if u + 2 < 12:
                        scores(u + 2)
                    if u >= 1:
                        weigh(u - 1)
                weigh(11)
                W(pe, "s_masked", 12, l)
                for head in range(HEADS):
                    W(pe, "osq_ready", head + 1, l)
                    m = mm(ps[:, 4 + head, 0:L], ones, sq[:, head, :], start=True, stop=True)
                m.then_inc(sub_sum, 1)

                W(pe, "conv_out", 4, l)
                W(pe, "at_ready", 12, l)
                for n in range(OUT_SLOTS):
                    w = weights(OUT0 + n)
                    if n >= 2:
                        W(pe, "h_added", 1 + 2 * (n - 1), l)
                    pair(w, cat, (2 * (n % 2), 2 * (n % 2) + 1), order=[4, 5, 6, 7, 0, 1, 2, 3],
                         wait=(lambda k: W(pe, "attn_out", k % 4 + 1, l) if k < 4 else None) if n == 0 else None)
                norm_sums(l, 1)

                g0 = OUT0 + OUT_SLOTS

                def gate_up(i, s, t0=0, wait=None, need=None):
                    w = slot(s, turn + t0).rearrange("p (k n c) -> p k n c", k=8, n=2)
                    if need is not None:
                        W(pe, "hff_ready", need, l)
                    pair(w, hn, (2 * (i % 2), 2 * (i % 2) + 1), wait=wait, even=False)

                for i in range(4):
                    gate_up(i, g0 + i, need=i - 1 if i >= 2 else None,
                            wait=(lambda k: W(pe, "hn_ready", 8 + k + 1, l)) if i == 0 else None)
                with pe.Fori(0, (GU_SLOTS - 4) // RING) as t:
                    for i in range(RING):
                        gate_up(i, g0 + 4 + i, t0=t, need=t * RING + i + 3)

                d0 = g0 + GU_SLOTS
                for half in range(2):
                    for g in range(6):
                        s = d0 + 6 * half + g
                        w = slot(s, turn).rearrange("p (k n c) -> p k n c", k=4, n=4)
                        if half == 0:
                            W(pe, "hff_ready", min(4 * g + 4, FC), l)
                        for k in range(min(4, FC - 4 * g)):
                            for n in range(4):
                                m = mm(ps[:, 4 - 4 * half + n, 0:L], w[:, k, n, :], hff[:, 4 * g + k, :],
                                       start=g + k == 0, stop=4 * g + k == FC - 1)
                        m.then_inc(slot_done, 1)
            norm_sums(DEPTH, 0)

            def token_sums(which):
                for c in range(DC):
                    if c % 4 == 0:
                        W(pe, "sq_ready", 2 * which + c // 4 + 1, DEPTH)
                    m = mm(ps[:, 7, 0:T], ones, sqx[:, c, :], start=c == 0, stop=c == DC - 1)
                m.then_inc(norm_sum, 1)

            token_sums(1)

            def project(i, wait=None):
                w = slot(B2 + i, 0).rearrange("p (k n c) -> p k n c", k=8, n=2)
                if i >= 2:
                    pe.wait_ge(gemm_out, i - 1)
                for n in range(2):
                    for k in range(DC):
                        if wait and n == 0:
                            pe.wait_ge(hm_ready, k + 1)
                        m = mm(ps[:, i % 2, n * T:(n + 1) * T], w[:, k, n, :], hm[:, k, :], start=k == 0, stop=k == DC - 1)
                m.then_inc(slot_done, 1)

            def square_sum(j, ready, value):
                pe.wait_ge(ready, value)
                if j >= 1:
                    pe.wait_ge(mroot, j)
                mm(ps[:, 2, :], ones, sqd[:, j % 2, :], start=True, stop=True).then_inc(msum, 1)

            def turn4(bank, src):
                for a in range(2):
                    for t in range(2):
                        m = nc.tensor.transpose(ps[:, bank, (2 * a + t) * P:(2 * a + t + 1) * P],
                                                src[:, a, t * P:(t + 1) * P], ident)
                return m

            def turn_dv(i):
                pe.wait_ge(gemm_out, i + 1)
                if i >= 14:
                    pe.wait_ge(dv_out, i - 13)
                turn4(4 + i % 2, vst[:, i % 2]).then_inc(dv_full, 1)

            for i in range(DIL_SLOTS):
                project(i, wait=i == 0)
                if 1 <= i <= 12:
                    square_sum(i - 1, gemm_out, i)
                if i >= 13:
                    turn_dv(i - 1)
            turn_dv(17)
            for o in range(2):
                for k in range(DC):
                    m = mm(ps[0:GH, 3, o * T:(o + 1) * T], w_ba[:, k, o * GH:(o + 1) * GH], hm[:, k, :],
                           start=k == 0, stop=k == DC - 1)
            m.then_inc(ba_full, 1)

            def dil_scores(d):
                hs, t = divmod(d, 2)
                if d == 0:
                    pe.wait_ge(dv_out, 6)
                    pe.wait_ge(mnorm, 12)
                else:
                    pe.wait_ge(dmask, d)
                for g in range(DG):
                    m = mm(flat[:, 4 * 512 + g * T:4 * 512 + g * T + (t + 1) * P],
                           dqk[:, 4 * g + hs, t * P:(t + 1) * P], dqk[:, 12 + 4 * g + hs, 0:(t + 1) * P],
                           start=True, stop=True)
                m.then_inc(ds_full, 1)

            def dil_turn(d):
                t = d % 2
                pe.wait_ge(dcoef, d + 1)
                if d >= 1:
                    pe.wait_ge(yb_ready, d)
                for g in range(DG):
                    for kt in range(t + 1):
                        o = 6 * 512 + (2 * g + kt) * P
                        m = nc.tensor.transpose(flat[:, o:o + P], dS[:, d % 2, g, kt * P:(kt + 1) * P], ident)
                m.then_inc(dtp, 1)

            def dil_out(d):
                hs, t = divmod(d, 2)
                pe.wait_ge(dpt_ready, d + 1)
                n = 0
                for g in range(DG):
                    for kt in range(t + 1):
                        n += 1
                        m = mm(ps[:, 6, 0:P], dV[:, kt, 4 * g + hs, :], dpT[:, d % 2, 2 * g + kt, :],
                               start=n == 1, stop=n == DG * (t + 1))
                m.then_inc(do_full, 1)

            def turn_kv(n):
                if n < 8:
                    pe.wait_ge(mnorm, 12 + n + 1)
                    src = gk[:, 2 * (n - 4):2 * (n - 4) + 2, :]
                else:
                    pe.wait_ge(gsilu, n + 1)
                    src = vst[:, n % 2]
                pe.wait_ge(gate_a1, 1)
                if n > 4:
                    pe.wait_ge(x_out, n - 4)
                turn4(3, src).then_inc(x_full, 1)

            for n in range(14):
                if n < 12:
                    project(DIL_SLOTS + n)
                if n < 8:
                    dil_scores(n)
                if 1 <= n <= 8:
                    square_sum(12 + n - 1, gsq, n)
                    dil_turn(n - 1)
                if 4 <= n - 2 < 12:
                    turn_kv(n - 2)
                if 1 <= n <= 8:
                    dil_out(n - 1)

            project(Z0)
            pe.wait_ge(x_out, 8)
            pe.wait_ge(gdiag_ready, 1)
            for o, src in enumerate((gt_[:, 5, :], gt_[:, 0, :])):
                for t in range(2):
                    nc.tensor.transpose(ps[:, 3, (2 * o + t) * GH:(2 * o + t + 1) * GH], src[0:GH, t * P:(t + 1) * P],
                                        ident[0:GH, 0:GH])
            pe.wait_ge(yb_ready, 8)
            for b in range(4):
                m = mm(ps[:, 4 + b, :], ones[0:GH, :], gdiag[0:GH, 2 * b:2 * b + 2, :], start=True, stop=True)
            m.then_inc(gb_full, 1)
            pe.wait_ge(gb_out, 2)
            pe.wait_ge(mnorm, 20)

            def batch(b):
                return b // 2, range(4 * (b % 2), 4 * (b % 2) + 4)

            for b in range(4):
                p, heads = batch(b)
                for hh in heads:
                    kT = gk[:, hh, p * P:(p + 1) * P]
                    m = mm(ps[:, 4 + b, (hh % 4) * P:(hh % 4 + 1) * P], kT, kT, start=True, stop=True)
                m.then_inc(kk_full, 1)
            for b in range(4):
                p, heads = batch(b)
                pe.wait_ge(l_ready, b + 1)
                for hh in heads:
                    m = mm(ps[:, 4 + b, (hh % 4) * P:(hh % 4 + 1) * P], gk[:, hh, p * P:(p + 1) * P],
                           gq[:, hh, p * P:(p + 1) * P], start=True, stop=True)
                m.then_inc(qk_full, 1)

            def inv_w(m_):
                s_, b = divmod(m_, 4)
                p, heads = batch(b)
                pe.wait_ge(m_ready, m_ + 1)
                if m_ == 0:
                    pe.wait_ge(tu_init, 2)
                    pe.wait_ge(qkt_ready, 4)
                if s_ >= 1:
                    pe.wait_ge(tu_done, 4 * (s_ - 1) + b + 1)
                if m_ >= 2:
                    pe.wait_ge(wt_copied, m_ - 1)
                for hh in heads:
                    m = mm(ps[:, 2 + 3 * (m_ % 2), (hh % 4) * P:(hh % 4 + 1) * P], Ms[:, m_ % 2, hh % 4, :],
                           MU[:, p, hh, :], start=True, stop=True)
                m.then_inc(wt_full, 1)

            def inv_tu(m_):
                s_, b = divmod(m_, 4)
                p, heads = batch(b)
                pe.wait_ge(wt_copied, m_ + 1)
                if m_ >= 2:
                    pe.wait_ge(tu_done, m_ - 1)
                for hh in heads:
                    c = slice((hh % 4) * P, (hh % 4 + 1) * P)
                    mm(ps[:, 3 + 3 * (m_ % 2), c], Wts[:, m_ % 2, hh % 4, :], MT[:, p, hh, :], start=True, stop=True)
                    m = mm(ps[:, 4 + 3 * (m_ % 2), c], MT[:, p, hh, :], Wts[:, m_ % 2, hh % 4, :], start=True, stop=True)
                m.then_inc(tu_full, 1)

            inv_w(0)
            for m_ in range(24):
                if m_ in (5, 11, 17):
                    project(Z0 + 1 + m_ // 6)
                if m_ + 1 < 24:
                    inv_w(m_ + 1)
                inv_tu(m_)
            pe.wait_ge(tu_done, 24)
            for b in range(4):
                p, heads = batch(b)
                if b == 0:
                    pe.wait_ge(pool_scaled, 2)
                for hh in heads:
                    m = mm(ps[:, 2 + b, (hh % 4) * P:(hh % 4 + 1) * P], MU[:, p, hh, :], gV[:, p, hh, :],
                           start=True, stop=True)
                m.then_inc(u_full, 1)
            for b in range(4):
                p, heads = batch(b)
                bank = (6, 7, 2, 3)[b]
                if b >= 2:
                    pe.wait_ge(u_out, b - 1)
                for hh in heads:
                    m = mm(ps[:, bank, (hh % 4) * P:(hh % 4 + 1) * P], kbg[:, p, hh, :], MU[:, p, hh, :],
                           start=True, stop=True)
                m.then_inc(w_full, 1)
            pe.wait_ge(w_out, 4)
            pe.wait_ge(u_out, 4)
            pe.wait_ge(pool_scaled, 4)
            for c in range(4):
                p, r = c // 2, slice(CHUNK * (c % 2), CHUNK * (c % 2) + CHUNK)
                pe.wait_ge(s_ready, c + 1)
                for hh in range(GH):
                    m = mm(ps[r, 2 + hh // 4, (hh % 4) * P:(hh % 4 + 1) * P], WT[:, p, hh, r], St[:, hh, :],
                           start=True, stop=True)
                m.then_inc(vn_full, 1)
                project(GATE0 + 2 * c)
                pe.wait_ge(vn_ready, c + 1)
                if c >= 2:
                    pe.wait_ge(oc_out, c - 1)
                for hh in range(GH):
                    o = ps[:, 4 + c % 2, hh * CHUNK:(hh + 1) * CHUNK]
                    mm(o, St[:, hh, :], gq[:, hh, c * CHUNK:(c + 1) * CHUNK], start=True, stop=False)
                    m = mm(o, vn[r, hh, :], MB[r, p, hh, r], start=False, stop=True)
                m.then_inc(oc_full, 1)
                if c < 3:
                    for hh in range(GH):
                        m = mm(ps[:, 6 + hh // 4, (hh % 4) * P:(hh % 4 + 1) * P], gK[r, p, hh, :], vn[r, hh, :],
                               start=True, stop=True)
                    m.then_inc(su_full, 1)
                project(GATE0 + 2 * c + 1)

            pe.wait_ge(s_ready, 4)
            for b in range(4):
                pe.wait_ge(ysq, b + 1)
                mm(ps[:, 4 + b, :], ones, MA_sq[:, b, :], start=True, stop=True).then_inc(ysum, 1)

            pe.wait_ge(gemm_out, UP0)
            for m_ in range(2):
                w = slot(B2 + UP0 + m_, 0).rearrange("p (k n c) -> p k n c", k=4, n=4)
                for n in range(4):
                    for k in range(4):
                        m = mm(ps[:, 2 * m_ + n // 2, (n % 2) * T:(n % 2 + 1) * T], w[:, k, n, :], yb[:, k, :],
                               start=k == 0, stop=k == 3)
                m.then_inc(slot_done, 1)
            for j in range(4):
                w = slot(B2 + UP0 + 2 + j, 0).rearrange("p (k n c) -> p k n c", k=8, n=2)
                if j == 0:
                    pe.wait_ge(yroot, 4)
                for n in range(2):
                    for k in range(DC):
                        if j == 0 and n == 0 and k % 2 == 0:
                            pe.wait_ge(ya_ready, k // 2 + 1)
                        m = mm(ps[:, 4 + j, n * T:(n + 1) * T], w[:, k, n, :], yo[:, k, :], start=k == 0, stop=k == DC - 1)
                m.then_inc(slot_done, 1)
            for j in range(4):
                w = slot(B2 + OUT2 + j, 0).rearrange("p (k n c) -> p k n c", k=8, n=2)
                for n in range(2):
                    for k in range(DC):
                        if j == 0 and n == 0 and k % 2 == 0:
                            pe.wait_ge(merged, k // 2 + 1)
                        m = mm(ps[:, j, n * T:(n + 1) * T], w[:, k, n, :], sga[:, k, :], start=k == 0, stop=k == DC - 1)
                m.then_inc(slot_done, 1)
            token_sums(2)
            pe.wait_ge(loaded2, 32)
            for t in range(2):
                for k in range(DC):
                    pe.wait_ge(hm_ready, DC + k + 1)
                    m = mm(ps[:, 6, t * EXPERTS:(t + 1) * EXPERTS], hm[:, k, t * P:(t + 1) * P], w_r[:, k, :],
                           start=k == 0, stop=k == DC - 1)
            m.then_inc(sc_full, 1)
            pe.wait_ge(comb_ready, 2)
            for t in range(2):
                m = nc.tensor.transpose(ps[0:EXPERTS, 5, t * P:(t + 1) * P], rt[:, 8 + t, 0:EXPERTS], ident)
            m.then_inc(ct_full, 1)

            def gate_up2(q, j0, turn0):
                for b in range(2):
                    w = slot(j0 + b, turn0).rearrange("p (k n c) -> p k n c", k=8, n=2)
                    for n in range(2):
                        for k in range(DC):
                            m = mm(ps[:, 2 * q + b, n * T:(n + 1) * T], w[:, k, n, :], hm[:, k, :],
                                   start=k == 0, stop=k == DC - 1)
                    m.then_inc(slot_done, 1)

            def down2(q, j, turn0):
                w = slot(j, turn0).rearrange("p (f n c) -> p f n c", f=2, n=8)
                for n in range(DC):
                    for f_ in range(2):
                        m = mm(ps[:, 4 + n // 2, (n % 2) * T:(n % 2 + 1) * T], w[:, f_, n, :], hid[:, q, f_, :],
                               start=False, stop=False, skip_group_check=True)
                m.then_inc(slot_done, 1)

            def spread(q, e):
                pe.wait_ge(row_ready, e + 1)
                pe.wait_ge(e_silu, e + 1)
                mm(ps[:, 2 * q, 0:T], ones[0:EXPERTS + 1, :], rhs_e[0:EXPERTS + 1, q, :], start=True, stop=True)\
                    .then_inc(cb_full, 1)

            ET, EJ = divmod(EX0, RING)
            gate_up2(0, EJ, ET)
            spread(0, 0)
            pe.wait_ge(zero_ready, 1)
            for b in range(4):
                mm(ps[:, 4 + b, :], zero_t, hm[:, 0:2, :], start=True, stop=False, skip_group_check=True)
            with pe.Fori(0, EXPERTS // 2) as t:
                for q in (1, 0):
                    first = EJ + 2 + (0 if q else 3)
                    n1 = 2 * t + (1 if q else 2)
                    pe.wait_ge(hid_primed, n1 + 1)
                    gate_up2(q, first, t + ET)
                    pe.wait_ge(hid_primed, n1 + 2)
                    down2(1 - q, first + 2, t + ET)
                    spread(q, n1)
            pe.wait_ge(hid_primed, EXPERTS + 3)
            down2(0, EJ + 2, ET + EXPERTS // 2)
            for b in range(4):
                m = mm(ps[:, 4 + b, :], zero_t, hm[:, 0:2, :], start=False, stop=True, skip_group_check=True)
            m.then_inc(y_full, 1)

        @block.scalar
        def _(act):
            f = nc.scalar.activation

            def squares(l, which, need):
                for g in range(2):
                    W(act, "h_added", need(g), l)
                    f(sq[:, 4 * g:4 * g + 4, :], h[:, 4 * g:4 * g + 4, :], ACT.Square).then_inc(sq_ready, 1)

            def root_of_mean(l, which, eps):
                W(act, "norm_sum", which + 1, l)
                f(root[:, 0, :], ps[:, 7, 0:L], ACT.Sqrt, bias=eps, scale=1.0 / D).then_inc(norm_root, 1)

            act.wait_ge(loaded, LOADS)
            act.wait_ge(zeroed, 4)
            f(cs[:, :], small[:, 40:48], ACT.Silu).then_inc(cs_ready, 1)
            with act.Fori(0, DEPTH) as l:
                def slot_out(s):
                    act.wait_ge(slot_done, l * LAYER_SLOTS + s + 1)

                def chunk_out(i):
                    W(act, "even_full", i // 2 + 1, l) if i % 2 == 0 else slot_out(i // 2)

                squares(l, 0, lambda g: 1)
                root_of_mean(l, 0, small[:, 60:61])
                W(act, "lam_sum", 1, l)
                f(small[:, 2:4], ps[:, 6, 0:2], ACT.Exp).then_inc(lam_exp, 1)
                W(act, "par_ready", 1, l)
                for c in range(CC):
                    slot_out(c)
                    f(sgl[:, c, :], ps[:, 2 * (c % 2) + 1, 0:L], ACT.Sigmoid, bias=par[:, PBG + 4 + c:PBG + 5 + c])\
                        .then_inc(glu_sig, 1)
                for j in range(8):
                    chunk_out(8 + j)
                    f(raw[:, j, :], ps[:, j % 4, 0:L], ACT.Copy).then_inc(raw_ready, 1)
                for j in range(HEADS + 2):
                    if j < HEADS:
                        chunk_out(16 + j)
                        f(vT[:, j, :], ps[:, j % 4, 0:L], ACT.Copy).then_inc(vT_ready, 1)
                    if j >= 2:
                        i = j - 2
                        W(act, "vt_full", i + 1, l)
                        bank = ps[:, 6 + i % 2, 0:3 * P].rearrange("p (t e) -> p t e", t=3)
                        f(V[:, 0:2, i, :], bank[:, 0:2, :], ACT.Copy).then_inc(v_ready, 1)
                        f(V[0:META, 2, i, :], bank[0:META, 2, :], ACT.Copy).then_inc(v_ready, 1)
                W(act, "xc_ready", 1, l)
                f(lsq[:, :, :], xc[:, :, :], ACT.Square).then_inc(lsq_ready, 1)
                W(act, "var_sum", 1, l)
                f(root[:, 1, :], ps[:, 1, 0:L], ACT.Sqrt, bias=small[:, 60:61], scale=1.0 / (CC * P)).then_inc(var_root, 1)

                W(act, "xn_ready", 1, l)
                for c in range(CC):
                    g, b = par[:, PLG + c:PLG + c + 1], par[:, PLB + c:PLB + c + 1]
                    f(lnv[:, c, :], xc[:, c, :], ACT.Identity, bias=b, scale=g).then_inc(ln_act, 1)
                    f(lns[:, c, :], xc[:, c, :], ACT.Sigmoid, bias=b, scale=g).then_inc(ln_act, 1)

                def exps(u):
                    head, t = UNITS[u]
                    q0, rows = Q_TILES[t]
                    W(act, "smax", u + 1, l)
                    if u >= 2:
                        W(act, "a_ready", u - 1, l)
                    for c in range(2):
                        m = f(Pr[0:rows, u % 2, c, 0:q0 + rows], Sm[0:rows, u % 2, c, 0:q0 + rows], ACT.Exp,
                              bias=small[0:rows, 8 + 4 * (u % 2) + c:9 + 4 * (u % 2) + c], scale=HD ** -0.5,
                              accum_out=small[0:rows, 16 + 4 * (u % 2) + c:17 + 4 * (u % 2) + c])
                        m.then_inc(exp_done, 1)

                def copy_probs(u):
                    head, t = UNITS[u]
                    rows = Q_TILES[t][1]
                    W(act, "at_full", u + 1, l)
                    bank = ps[:, u % 2, 0:3 * P].rearrange("p (t q) -> p t q", t=3)
                    full = min(t + 1, 2)
                    m = f(aT[:, u % 2, 0:full, 0:rows], bank[:, 0:full, 0:rows], ACT.Copy)
                    if t == 2:
                        m.then_inc(at_part, 1)
                        m = f(aT[0:META, u % 2, 2, 0:rows], bank[0:META, 2, 0:rows], ACT.Copy)
                    m.then_inc(at_ready, 1)

                def copy_out(head):
                    W(act, "o_full", head + 1, l)
                    f(oraw[:, head, :], ps[:, 2 + head % 2, 0:L], ACT.Copy).then_inc(o_copied, 1)
                    f(mod[:, ds(l * 24 + 6 * head, 6)], ps[:, 2 + head % 2, L:L + 6], ACT.Copy).then_inc(o_copied, 1)
                    f(sq[:, head, :], ps[:, 2 + head % 2, 0:L], ACT.Square).then_inc(osq_ready, 1)

                for u in range(12):
                    exps(u)
                    if u >= 1:
                        copy_probs(u - 1)
                    if u >= 3 and u % 3 == 0:
                        copy_out(u // 3 - 1)
                copy_probs(11)
                copy_out(3)
                W(act, "sub_sum", 1, l)
                f(root[:, :, :], ps[:, 4:8, 0:L], ACT.Sqrt, bias=small[:, 60:61], scale=1.0 / P).then_inc(sub_root, 1)

                squares(l, 1, lambda g: 1 + 4 * g + 4)
                root_of_mean(l, 1, small[:, 60:61])

                def silu_gate(i, q, need):
                    act.wait_ge(slot_done, l * LAYER_SLOTS + OUT0 + OUT_SLOTS + 1 + i)
                    if need is not None:
                        W(act, "hff_ready", need, l)
                    f(sgu[:, q, :], ps[:, 2 * q, 0:L], ACT.Silu).then_inc(gate_act, 1)

                for i in range(2):
                    silu_gate(i, i, None)
                with act.Fori(1, FC // 2) as t:
                    for q in range(2):
                        silu_gate(t * 2 + q, q, t * 2 + q - 1)
            squares(DEPTH, 0, lambda g: 1)
            root_of_mean(DEPTH, 0, small[:, 60:61])
            e2 = small[:, 59:60]

            def token_squares(which, need):
                for g in range(2):
                    act.wait_ge(x_ready, need(g))
                    f(sqx[:, 4 * g:4 * g + 4, :], x[:, 4 * g:4 * g + 4, :], ACT.Square).then_inc(sq_ready, 1)
                W(act, "norm_sum", which + 1, DEPTH)
                f(root[:, 0, 0:T], ps[:, 7, 0:T], ACT.Sqrt, bias=e2, scale=1.0 / D).then_inc(norm_root, 1)

            def shift(which, col):
                for c in range(DC):
                    act.wait_ge(hm_scaled, DC * which + c + 1)
                    f(hm[:, c, :], hm[:, c, :], ACT.Identity, bias=mod[:, col + c:col + c + 1]).then_inc(hm_ready, 1)

            token_squares(1, lambda g: 4 * g + 4)
            act.dma_start(c2, consts2).then_inc(loaded2, 16)
            shift(0, 0)

            def landed(i):
                act.wait_ge(slot_done, B2 + i + 1)

            def head_root(j, scale):
                act.wait_ge(msum, j + 1)
                if j >= 2:
                    act.wait_ge(mnorm, j - 1)
                f(root2[:, j % 2, :], ps[:, 2, :], ACT.Sqrt, bias=e2, scale=scale).then_inc(mroot, 1)

            def turned_out(full, value, bank, dest, a0, done):
                act.wait_ge(full, value)
                src = ps[:, bank, :].rearrange("p (a t e) -> p a t e", a=2, t=2)
                f(dest[:, :, a0:a0 + 2, :].rearrange("p t a e -> p a t e"), src, ACT.Copy).then_inc(done, 1)

            for i in range(DIL_SLOTS):
                landed(i)
                if i < 12:
                    f(dqk[:, 2 * i:2 * i + 2, :].rearrange("p a b -> p (a b)"), ps[:, i % 2, :], ACT.Copy).then_inc(chain_a, 1)
                    f(sqd[:, i % 2, :], ps[:, i % 2, :], ACT.Square).then_inc(gemm_out, 1)
                else:
                    f(vst[:, i % 2].rearrange("p a b -> p (a b)"), ps[:, i % 2, :], ACT.Copy).then_inc(gemm_out, 1)
                if 1 <= i <= 12:
                    head_root(i - 1, 1.0 / P)
                if i >= 13:
                    turned_out(dv_full, i - 12, 4 + (i - 1) % 2, dV, 2 * (i - 13), dv_out)
            turned_out(dv_full, 6, 5, dV, 10, dv_out)
            act.wait_ge(ba_full, 1)
            CA = [12]

            def alink(ins):
                CA[0] += 1
                ins.then_inc(chain_a, 1)
                act.wait_ge(chain_a, CA[0])

            g8 = region(16512, 4, T)
            alink(f(g8[0:GH, 0, :], ps[0:GH, 3, 0:T], ACT.Sigmoid))
            alink(f(g8[0:GH, 1, :], ps[0:GH, 3, T:2 * T], ACT.Identity, bias=par2[0:GH, QDT:QDT + 1]))
            alink(f(g8[0:GH, 2, :], g8[0:GH, 1, :], ACT.Abs))
            alink(f(g8[0:GH, 3, :], g8[0:GH, 2, :], ACT.Exp, scale=-1.0))
            f(small[0:GH, 48:49], par2[0:GH, QAL:QAL + 1], ACT.Exp).then_inc(gate_a1, 1)

            def dil_exps(d):
                hs, t = divmod(d, 2)
                act.wait_ge(dmax, d + 1)
                o = 16 * (d % 2)
                for g in range(DG):
                    f(dS[:, d % 2, g, 0:(t + 1) * P], dS[:, d % 2, g, 0:(t + 1) * P], ACT.Exp, scale=P ** -0.5,
                      bias=tiny[:, o + g:o + g + 1], accum_out=tiny[:, o + 4 + g:o + 5 + g]).then_inc(dexp, 1)
                f(tiny[:, o + 8:o + 11], tiny[:, o:o + 3], ACT.Exp, scale=-1.0, bias=tiny[:, o + 3:o + 4]).then_inc(dexp, 1)

            def dil_probs_out(d):
                t = d % 2
                act.wait_ge(dtp, d + 1)
                src = flat[:, 6 * 512:6 * 512 + 768].rearrange("p (g k q) -> p g k q", g=3, k=2)
                dst = dpT[:, d % 2].rearrange("p (g k) q -> p g k q", g=3)
                f(dst[:, :, 0:t + 1, :], src[:, :, 0:t + 1, :], ACT.Copy).then_inc(dpt_ready, 1)

            def dil_y_out(d):
                hs, t = divmod(d, 2)
                act.wait_ge(do_full, d + 1)
                f(yb[:, hs, t * P:(t + 1) * P], ps[:, 6, 0:P], ACT.Copy).then_inc(yb_ready, 1)

            act.wait_ge(padded, 1)
            for n in range(14):
                if n < 12:
                    landed(DIL_SLOTS + n)
                    if n >= 2:
                        act.wait_ge(gconv, n - 1)
                    f(gpad[:, n % 2, :, 3:], ps[:, n % 2, :].rearrange("p (a b) -> p a b", a=2), ACT.Copy).then_inc(gemm_out, 1)
                if n < 8:
                    dil_exps(n)
                if 1 <= n <= 8:
                    head_root(12 + n - 1, 1.0)
                    dil_probs_out(n - 1)
                if 4 <= n - 2 < 12:
                    k = n - 2
                    turned_out(x_full, k - 3, 3, gK if k < 8 else gV, 2 * (k - 4 if k < 8 else k - 8), x_out)
                if n < 12:
                    act.wait_ge(gconv, n + 1)
                    dst = gq[:, 2 * n:2 * n + 2, :] if n < 4 else gk[:, 2 * n - 8:2 * n - 6, :] if n < 8 else vst[:, n % 2]
                    f(dst, gacc[:, n % 2], ACT.Silu).then_inc(gsilu, 1)
                    if n < 8:
                        act.wait_ge(gsilu, n + 1)
                        f(sqd[:, n % 2, :], dst.rearrange("p a b -> p (a b)"), ACT.Square).then_inc(gsq, 1)
                if 1 <= n <= 8:
                    dil_y_out(n - 1)

            act.wait_ge(gate_v1, 1)
            f(gt_[0:GH, 2, :], gt_[0:GH, 1, :], ACT.Ln).then_inc(gate_a2, 1)

            def z_out(j):
                landed(Z0 + j)
                f(zs[:, 2 * j:2 * j + 2, :].rearrange("p a b -> p (a b)"), ps[:, (Z0 + j) % 2, :], ACT.Silu)\
                    .then_inc(gemm_out, 1)

            z_out(0)
            act.wait_ge(gb_full, 1)
            f(GB[:, :, :].rearrange("p a b -> p (a b)"), flat[:, 4 * 512:8 * 512], ACT.Copy).then_inc(gb_out, 1)
            f(tiny[:, 32:64], ps[:, 3, 0:32], ACT.Copy).then_inc(gb_out, 1)
            for i in range(2):
                m = [MA, MB][i]
                act.wait_ge(d_built, 2 * (i + 1))
                f(m[:, :, :, :], m[:, :, :, :], ACT.Exp).then_inc(d_exp, 1)
            act.wait_ge(d_built, 5)
            f(tiny[:, 64:80], tiny[:, 32:48], ACT.Exp).then_inc(gcols, 1)
            f(tiny[:, 96:112], tiny[:, 80:96], ACT.Exp).then_inc(gcols, 1)
            f(GB[:, :, :], GB[:, :, :], ACT.Exp).then_inc(d_exp, 1)
            for m_ in range(24):
                act.wait_ge(wt_full, m_ + 1)
                if m_ >= 2:
                    act.wait_ge(tu_full, m_ - 1)
                f(Wts[:, m_ % 2].rearrange("p a b -> p (a b)"), ps[:, 2 + 3 * (m_ % 2), :], ACT.Copy).then_inc(wt_copied, 1)
                if m_ in (5, 11, 17):
                    z_out(1 + m_ // 6)
            for b in range(4):
                act.wait_ge(u_full, b + 1)
                f(MA[:, b // 2, 4 * (b % 2):4 * (b % 2) + 4, :].rearrange("p a b -> p (a b)"), ps[:, 2 + b, :], ACT.Copy)\
                    .then_inc(u_out, 1)

            def gate_out(j):
                landed(GATE0 + j)
                dst = (sga if j < 4 else sgb)[:, 2 * (j % 4):2 * (j % 4) + 2, :]
                f(dst.rearrange("p a b -> p (a b)"), ps[:, (GATE0 + j) % 2, :], ACT.Sigmoid).then_inc(gemm_out, 1)

            for c in range(4):
                gate_out(2 * c)
                act.wait_ge(oc_full, c + 1)
                f(yo[:, :, c * CHUNK:(c + 1) * CHUNK], ps[:, 4 + c % 2, :].rearrange("p (a b) -> p a b", a=GH), ACT.Copy)\
                    .then_inc(oc_out, 1)
                gate_out(2 * c + 1)
            act.dma_start(w_r, w_router_d).then_inc(loaded2, 16)
            act.wait_ge(oc_out, 4)
            act.wait_ge(vn_ready, 4)
            for b in range(4):
                f(MA_sq[:, b, :], yo[:, 2 * b:2 * b + 2, :].rearrange("p a b -> p (a b)"), ACT.Square).then_inc(ysq, 1)
            for b in range(4):
                act.wait_ge(ysum, b + 1)
                f(MB_rt[:, b, :], ps[:, 4 + b, :], ACT.Sqrt, bias=e2, scale=1.0 / P).then_inc(yroot, 1)
            token_squares(2, lambda g: 8 + 4 * g + 4)
            shift(1, 24)
            act.wait_ge(sc_full, 1)
            f(rt[:, 0, :], ps[:, 6, 0:P], ACT.Sigmoid).then_inc(sc_ready, 1)
            act.wait_ge(ct_full, 1)
            f(combT[0:EXPERTS, :], ps[0:EXPERTS, 5, 0:T], ACT.Copy).then_inc(ct_out, 1)

            def silu_expert(q, e, b):
                act.wait_ge(slot_done, b)
                act.wait_ge(prod_primed, e + 1)
                f(esil[:, q, :], ps[:, 2 * q, :], ACT.Silu).then_inc(e_silu, 1)

            silu_expert(0, 0, EX0 + 1)
            with act.Fori(0, EXPERTS // 2) as t:
                silu_expert(1, 2 * t + 1, 6 * t + EX0 + 2 + 1)
                silu_expert(0, 2 * t + 2, 6 * t + EX0 + 5 + 1)

        @block.vector
        def _(dve):
            v = nc.vector

            class Chain:
                base, n = 0, 0

            def link(ins):
                Chain.n += 1
                ins.then_inc(chain_v, 1)
                dve.wait_ge(chain_v, Chain.base + Chain.n)

            v.memset(small[:, 59:60], EPS2).then_inc(zeroed, 1)
            v.memset(small[:, 60:61], EPS1).then_inc(zeroed, 1)
            v.memset(zpad[:, :, 0:PAD], 0.0).then_inc(zeroed, 1)
            dve.wait_ge(zeroed, 3)
            v.memset(small[:, 61:62], -1.0).then_inc(zeroed, 1)
            dve.wait_ge(zeroed, 4)
            v.memset(small[:, 62:63], -1.0).then_inc(h_added, 1)
            dve.wait_ge(loaded, LOADS)

            def normalize(l, which, gains):
                W(dve, "norm_root", which + 1, l)
                link(v.reciprocal(inv[:, 0, :], root[:, 0, :]))
                for c in range(DC):
                    v.scalar_tensor_tensor(hn[:, c, :], h[:, c, :], gains[:, c:c + 1], inv[:, 0, :],
                                           ALU.mult, ALU.mult).then_inc(hn_ready, 1)

            CHAIN = 186
            with dve.Fori(0, DEPTH) as l:
                Chain.base, Chain.n = l * CHAIN, 0
                dve.wait_ge(h_added, l * COUNT["h_added"] + 1)
                v.tensor_copy(par[:, :], par_all[:, ds(l, 1), :].rearrange("p a n -> p (a n)")).then_inc(par_ready, 1)
                W(dve, "par_ready", 1, l)
                v.tensor_tensor(small[0:HD, 0:2], par[0:HD, PLAM:PLAM + 4:2], par[0:HD, PLAM + 1:PLAM + 4:2], ALU.mult)\
                    .then_inc(lam_prod, 1)
                normalize(l, 0, par[:, PN1:PN1 + DC])

                taps = [(c, k) for c in range(CC) for k in range(TAPS)]

                def convolve(n):
                    for _ in range(min(n, len(taps))):
                        c, k = taps.pop(0)
                        z, g = zpad[:, c, k:k + L], par[:, PCW + c * TAPS + k:PCW + c * TAPS + k + 1]
                        if k == 0:
                            link(v.tensor_scalar(conv[:, c, :], z, g, par[:, PCB + c:PCB + c + 1], ALU.mult, ALU.add))
                        elif taps:
                            link(v.scalar_tensor_tensor(conv[:, c, :], z, g, conv[:, c, :], ALU.mult, ALU.add))
                        else:
                            v.scalar_tensor_tensor(conv[:, c, :], z, g, conv[:, c, :], ALU.mult, ALU.add)\
                                .then_inc(conv_ready, 1)

                for c in range(CC):
                    W(dve, "glu_sig", c + 1, l)
                    v.scalar_tensor_tensor(zpad[:, c, PAD:], ps[:, 2 * (c % 2), 0:L], par[:, PBG + c:PBG + c + 1],
                                           sgl[:, c, :], ALU.add, ALU.mult).then_inc(glu_done, 1)
                    W(dve, "glu_done", c + 1, l)
                    convolve(20)
                for j in range(8):
                    W(dve, "raw_ready", j + 1, l)
                    link(v.tensor_tensor(rt1[:, j % 2, :], raw[:, j, :], cos, ALU.mult))
                    W(dve, "rot_full", j + 1, l)
                    v.tensor_tensor(rt2[:, j % 2, :], ps[:, 4 + j % 2, 0:L], sin, ALU.mult).then_inc(rot_used, 1)
                    W(dve, "rot_used", j + 1, l)
                    v.tensor_tensor(qk[:, j, :], rt1[:, j % 2, :], rt2[:, j % 2, :], ALU.add).then_inc(qk_ready, 1)
                    convolve(6)
                assert not taps
                W(dve, "lam_exp", 1, l)
                link(v.tensor_tensor(small[:, 4:5], small[:, 3:4], small[:, 2:3], ALU.subtract))
                link(v.tensor_tensor(small[:, 5:6], small[:, 4:5], par[:, PLI:PLI + 1], ALU.subtract))
                link(v.tensor_tensor(small[:, 6:7], par[:, PSG:PSG + 1], par[:, PLO:PLO + 1], ALU.mult))
                W(dve, "mu_sum", 1, l)
                for c in range(CC):
                    m = v.scalar_tensor_tensor(xc[:, c, :], ps[:, 0, 0:L], -1.0 / (CC * P), conv[:, c, :], ALU.mult, ALU.add)
                m.then_inc(xc_ready, 1)

                def mask_max(u):
                    head, t = UNITS[u]
                    q0, rows = Q_TILES[t]
                    keys = q0 + rows
                    W(dve, "s_full", u + 1, l)
                    if u >= 2:
                        W(dve, "exp_done", 2 * (u - 1), l)
                    b = 4 + 2 * (u % 2)
                    m = causal[0:rows, t:t + 1, 0:keys].to_broadcast([rows, 2, keys])
                    v.tensor_tensor(Sm[0:rows, u % 2, :, 0:keys], ps[0:rows, b:b + 2, 0:keys], m, ALU.add)\
                        .then_inc(s_masked, 1)
                    W(dve, "s_masked", u + 1, l)
                    mx = small[0:rows, 24 + 4 * (u % 2):26 + 4 * (u % 2)]
                    link(v.tensor_reduce(mx, Sm[0:rows, u % 2, :, 0:keys], AX_X, ALU.max))
                    v.tensor_scalar(small[0:rows, 8 + 4 * (u % 2):10 + 4 * (u % 2)], mx, -HD ** -0.5, None, ALU.mult)\
                        .then_inc(smax, 1)

                def difference(u):
                    head, t = UNITS[u]
                    q0, rows = Q_TILES[t]
                    keys = q0 + rows
                    W(dve, "exp_done", 2 * (u + 1), l)
                    o = 32 + 4 * (u % 2)
                    link(v.reciprocal(small[0:rows, o:o + 2], small[0:rows, 16 + 4 * (u % 2):18 + 4 * (u % 2)]))
                    link(v.tensor_tensor(small[0:rows, o + 2:o + 3], small[0:rows, o + 1:o + 2], small[0:rows, 5:6], ALU.mult))
                    link(v.tensor_scalar(Pt[0:rows, u % 2, 0:keys], Pr[0:rows, u % 2, 1, 0:keys],
                                         small[0:rows, o + 2:o + 3], None, ALU.mult))
                    if u >= 2:
                        W(dve, "at_full", u - 1, l)
                    v.scalar_tensor_tensor(A[0:rows, u % 2, 0:keys], Pr[0:rows, u % 2, 0, 0:keys], small[0:rows, o:o + 1],
                                           Pt[0:rows, u % 2, 0:keys], ALU.mult, ALU.add).then_inc(a_ready, 1)

                mask_max(0)
                mask_max(1)
                W(dve, "var_root", 1, l)
                link(v.reciprocal(inv[:, 1, :], root[:, 1, :]))
                v.tensor_tensor(xc[:, :, :], xc[:, :, :], inv[:, 1:2, :].to_broadcast([P, CC, L]), ALU.mult)\
                    .then_inc(xn_ready, 1)
                for u in range(12):
                    difference(u)
                    if u + 2 < 12:
                        mask_max(u + 2)
                W(dve, "sub_root", 1, l)
                link(v.reciprocal(inv[:, :, :], root[:, :, :]))
                for head in range(HEADS):
                    v.scalar_tensor_tensor(cat[:, head, :], oraw[:, head, :], small[:, 6:7], inv[:, head, :],
                                           ALU.mult, ALU.mult).then_inc(attn_out, 1)
                for n in range(DC):
                    if n % 2 == 0:
                        W(dve, "even_full", IN_SLOTS + n // 2 + 1, l)
                    else:
                        dve.wait_ge(slot_done, l * LAYER_SLOTS + OUT0 + n // 2 + 1)
                    v.tensor_tensor(h[:, n, :], h[:, n, :], ps[:, n % 4, 0:L], ALU.add).then_inc(h_added, 1)
                W(dve, "h_added", 1 + DC, l)
                normalize(l, 1, par[:, PN2:PN2 + DC])
                with dve.Fori(0, FC // 2) as t:
                    for q in range(2):
                        W(dve, "gate_act", t * 2 + q + 1, l)
                        v.tensor_tensor(hff[:, ds(t * 2 + q, 1), :].rearrange("p a n -> p (a n)"), sgu[:, q, :],
                                        ps[:, 2 * q + 1, 0:L], ALU.mult).then_inc(hff_ready, 1)
                for half in range(2):
                    dve.wait_ge(slot_done, l * LAYER_SLOTS + OUT0 + OUT_SLOTS + GU_SLOTS + 6 * half + 6)
                    for n in range(4):
                        v.tensor_tensor(h[:, 4 * half + n, :], h[:, 4 * half + n, :], ps[:, 4 - 4 * half + n, 0:L], ALU.add)\
                            .then_inc(h_added, 1)
                assert Chain.n == CHAIN, Chain.n
            Chain.base, Chain.n = DEPTH * CHAIN, 0
            dve.wait_ge(h_added, DEPTH * COUNT["h_added"] + 1)
            W(dve, "norm_root", 1, DEPTH)
            link(v.reciprocal(inv[:, 0, :], root[:, 0, :]))
            for c in range(DC):
                v.scalar_tensor_tensor(h[:, c, :], h[:, c, :], fin_g[:, c:c + 1], inv[:, 0, :],
                                       ALU.mult, ALU.mult).then_inc(x_ready, 1)
            W(dve, "o_copied", 0, DEPTH)
            link(v.tensor_tensor(mod[:, :], mod[:, :], par2[:, QADA:QADA + 48], ALU.add))
            for o, g in ((0, QMIX), (24, QFFN)):
                link(v.scalar_tensor_tensor(mod[:, o + 8:o + 16], mod[:, o + 8:o + 16], 1.0, par2[:, g:g + DC],
                                            ALU.add, ALU.mult))

            def scale_tokens(which, col):
                W(dve, "norm_root", which + 1, DEPTH)
                link(v.reciprocal(inv[:, 0, 0:T], root[:, 0, 0:T]))
                for c in range(DC):
                    v.scalar_tensor_tensor(hm[:, c, :], x[:, c, :], mod[:, col + c:col + c + 1], inv[:, 0, 0:T],
                                           ALU.mult, ALU.mult).then_inc(hm_scaled, 1)

            dve.wait_ge(x_ready, 8)
            scale_tokens(1, 8)

            def head_norm(j, dst, gain):
                dve.wait_ge(mroot, j + 1)
                link(v.reciprocal(inv2[:, j % 2, :], root2[:, j % 2, :]))
                d = dst.rearrange("p a b -> p (a b)")
                v.scalar_tensor_tensor(d, d, gain, inv2[:, j % 2, :], ALU.mult, ALU.mult).then_inc(mnorm, 1)

            for i in range(12):
                g = QDQ if i < 6 else QDK
                head_norm(i, dqk[:, 2 * i:2 * i + 2, :], par2[:, g:g + 1])
            v.memset(gpad[:, :, :, 0:3], 0.0).then_inc(padded, 1)
            dve.wait_ge(loaded2, 16)

            def dil_mask(d):
                hs, t = divmod(d, 2)
                keys = (t + 1) * P
                o = 16 * (d % 2)
                dve.wait_ge(ds_full, d + 1)
                if d >= 2:
                    dve.wait_ge(dtp, d - 1)
                src = flat[:, 4 * 512:4 * 512 + 768].rearrange("p (g k) -> p g k", g=3)[:, :, 0:keys]
                k0 = (KD0, KD1)[t]
                mask = c2[:, k0:k0 + 3 * keys].rearrange("p (g k) -> p g k", g=3)
                s_ = dS[:, d % 2, :, 0:keys]
                v.tensor_tensor(s_, src, mask, ALU.add).then_inc(dmask, 1)
                dve.wait_ge(dmask, d + 1)
                link(v.tensor_reduce(tiny[:, o + 12:o + 15], s_, AX_X, ALU.max))
                link(v.tensor_scalar(tiny[:, o:o + 3], tiny[:, o + 12:o + 15], -P ** -0.5, None, ALU.mult))
                v.tensor_reduce(tiny[:, o + 3:o + 4], tiny[:, o:o + 3], AX_X, ALU.min).then_inc(dmax, 1)

            def dil_weights(d):
                hs, t = divmod(d, 2)
                keys = (t + 1) * P
                o, q = 16 * (d % 2), 112 + 16 * (d % 2)
                dve.wait_ge(dexp, 4 * (d + 1))
                link(v.tensor_tensor(tiny[:, q:q + 3], tiny[:, o + 4:o + 7], tiny[:, o + 8:o + 11], ALU.mult))
                link(v.tensor_reduce(tiny[:, q + 3:q + 4], tiny[:, q:q + 3], AX_X, ALU.add))
                link(v.reciprocal(tiny[:, q + 4:q + 5], tiny[:, q + 3:q + 4]))
                link(v.tensor_scalar(tiny[:, q + 8:q + 11], tiny[:, o + 8:o + 11], tiny[:, q + 4:q + 5], None, ALU.mult))
                s_ = dS[:, d % 2, :, 0:keys]
                c_ = tiny[:, q + 8:q + 11].rearrange("p (g a) -> p g a", a=1).to_broadcast([P, 3, keys])
                v.tensor_tensor(s_, s_, c_, ALU.mult).then_inc(dcoef, 1)

            def short_conv(n):
                dve.wait_ge(gemm_out, DIL_SLOTS + n + 1)
                if n >= 2:
                    dve.wait_ge(gsilu, n - 1)
                for k in range(4):
                    for a in range(2):
                        w = par2[:, QCW + 4 * (2 * n + a) + k:QCW + 4 * (2 * n + a) + k + 1]
                        z, y = gpad[:, n % 2, a, k:k + T], gacc[:, n % 2, a, :]
                        if k == 0:
                            m = v.tensor_scalar(y, z, w, None, ALU.mult)
                        else:
                            m = v.scalar_tensor_tensor(y, z, w, y, ALU.mult, ALU.add)
                        if k < 3:
                            m.then_inc(chain_v, 1)
                            Chain.n += 1
                            if a == 1:
                                dve.wait_ge(chain_v, Chain.base + Chain.n)
                m.then_inc(gconv, 1)

            for n in range(12):
                if n < 8:
                    dil_mask(n)
                short_conv(n)
                if n < 8:
                    dil_weights(n)
                if 1 <= n <= 8:
                    k = n - 1
                    dst = gq[:, 2 * k:2 * k + 2, :] if k < 4 else gk[:, 2 * k - 8:2 * k - 6, :]
                    head_norm(12 + k, dst, P ** -0.5 if k < 4 else 1.0)

            g8 = region(16512, 4, T)
            dve.wait_ge(gate_a1, 1)
            dve.wait_ge(yb_ready, 8)
            R = lambda i: gt_[0:GH, i, :]
            v.tensor_scalar(R(1), g8[0:GH, 3, :], 1.0, None, ALU.add).then_inc(gate_v1, 1)
            dve.wait_ge(gate_v1, 1)
            link(v.tensor_copy(R(0), g8[0:GH, 0, :]))
            link(v.tensor_scalar(R(3), R(1), -1.0, None, ALU.add))
            link(v.tensor_tensor(R(3), g8[0:GH, 3, :], R(3), ALU.subtract))
            link(v.reciprocal(R(4), R(1)))
            link(v.tensor_tensor(R(3), R(3), R(4), ALU.mult))
            link(v.tensor_scalar(R(4), g8[0:GH, 1, :], 0.0, None, ALU.max))
            link(v.tensor_tensor(R(3), R(3), R(4), ALU.add))
            dve.wait_ge(gate_a2, 1)
            link(v.tensor_tensor(R(3), R(3), R(2), ALU.add))
            link(v.tensor_scalar(R(4), R(3), small[0:GH, 48:49], -1.0, ALU.mult, ALU.mult))
            for c in range(4):
                cc = slice(c * CHUNK, (c + 1) * CHUNK)
                link(v.tensor_tensor_scan(gt_[0:GH, 5, cc], ones[0:GH, 0:CHUNK], gt_[0:GH, 4, cc], 0.0, ALU.mult, ALU.add))
            v.tensor_tensor(gdiag[0:GH, :, :], gt_[0:GH, 5:6, :].to_broadcast([GH, GH, T]),
                            ident[0:GH, 0:GH].rearrange("p (a b) -> p a b", b=1).to_broadcast([GH, GH, T]), ALU.mult)\
                .then_inc(gdiag_ready, 1)
            dve.wait_ge(gb_out, 2)
            low = c2[:, KLOW:KLOW + P].rearrange("p (a b) -> p a b", a=1).to_broadcast([P, GH, P])
            up = c2[:, KUP:KUP + P].rearrange("p (a b) -> p a b", a=1).to_broadcast([P, GH, P])

            def col(o, p):
                return tiny[:, o + GH * p:o + GH * p + GH].rearrange("p (a b) -> p a b", b=1).to_broadcast([P, GH, P])

            for p in range(2):
                link(v.tensor_tensor(MA[:, p], low, GB[:, :, p * P:(p + 1) * P], ALU.subtract))
            for p in range(2):
                v.tensor_tensor(MA[:, p], MA[:, p], col(32, p), ALU.add).then_inc(d_built, 1)
            for p in range(2):
                link(v.tensor_tensor(MB[:, p], up, GB[:, :, p * P:(p + 1) * P], ALU.add))
            for p in range(2):
                v.tensor_tensor(MB[:, p], MB[:, p], col(32, p), ALU.subtract).then_inc(d_built, 1)
            for p in range(2):
                for hf in range(2):
                    r = slice(64 * hf, 64 * hf + 64)
                    last = p * P + 64 * hf + 63
                    m = v.tensor_tensor(tiny[r, 80 + GH * p:88 + GH * p], GB[r, :, last:last + 1].rearrange("p a b -> p (a b)"),
                                        tiny[r, 32 + GH * p:40 + GH * p], ALU.subtract)
            m.then_inc(d_built, 1)
            dve.wait_ge(d_exp, 1)
            for b in range(4):
                dve.wait_ge(kk_full, b + 1)
                for i in range(4):
                    p, hh = b // 2, 4 * (b % 2) + i
                    m = v.scalar_tensor_tensor(MA[:, p, hh, :], ps[:, 4 + b, i * P:(i + 1) * P],
                                               tiny[:, 48 + GH * p + hh:49 + GH * p + hh], MA[:, p, hh, :], ALU.mult, ALU.mult)
                m.then_inc(l_ready, 1)
            dve.wait_ge(d_exp, 2)
            for b in range(4):
                dve.wait_ge(qk_full, b + 1)
                d = MB[:, b // 2, 4 * (b % 2):4 * (b % 2) + 4, :].rearrange("p a b -> p (a b)")
                v.tensor_tensor(d, ps[:, 4 + b, :], d, ALU.mult).then_inc(qkt_ready, 1)
            for m in (MT, MU):
                idb = ident.rearrange("p (a b) -> p a b", a=1).to_broadcast([P, 2 * GH, P])
                v.tensor_copy(m[:, :, :, :].rearrange("p a b c -> p (a b) c"), idb).then_inc(tu_init, 1)
            dve.wait_ge(tu_init, 2)
            dve.wait_ge(gcols, 2)
            link(v.tensor_tensor(tiny[:, 144:160], tiny[:, 48:64], tiny[:, 64:80], ALU.mult))
            dve.wait_ge(d_exp, 3)
            v.tensor_copy(tiny[:, 160:192].rearrange("p (c h) -> p h c", c=4), GB[:, :, 63:T:64]).then_inc(gtot_ready, 1)
            for m_ in range(24):
                b = m_ % 4
                dve.wait_ge(tu_full, m_ + 1)
                for o, mat in ((3, MT), (4, MU)):
                    d = mat[:, b // 2, 4 * (b % 2):4 * (b % 2) + 4, :].rearrange("p a b -> p (a b)")
                    m = v.tensor_tensor(d, d, ps[:, o + 3 * (m_ % 2), :], ALU.subtract)
                m.then_inc(tu_done, 1)
                if m_ < 20:
                    dve.wait_ge(tu_done, max(m_ - 2, 1))
            v.memset(St[:, :, :], 0.0).then_inc(s_ready, 1)
            dve.wait_ge(pool_scaled, 4)
            for b in range(4):
                dve.wait_ge(w_full, b + 1)
                v.tensor_copy(WT[:, b // 2, 4 * (b % 2):4 * (b % 2) + 4, :].rearrange("p a b -> p (a b)"),
                              ps[:, (6, 7, 2, 3)[b], :]).then_inc(w_out, 1)
            dve.wait_ge(u_out, 4)
            for c in range(4):
                p, r = c // 2, slice(CHUNK * (c % 2), CHUNK * (c % 2) + CHUNK)
                dve.wait_ge(vn_full, c + 1)
                v.tensor_tensor(vn[r, :, :].rearrange("p a b -> p (a b)"), MA[r, p, :, :].rearrange("p a b -> p (a b)"),
                                flat[r, 1024:2048], ALU.subtract).then_inc(vn_ready, 1)
                if c < 3:
                    dve.wait_ge(su_full, c + 1)
                    dve.wait_ge(s_ready, c + 1)
                    for hh in range(GH):
                        m = v.scalar_tensor_tensor(St[:, hh, :], St[:, hh, :], tiny[:, 160 + 8 * c + hh:161 + 8 * c + hh],
                                                   ps[:, 6 + hh // 4, (hh % 4) * P:(hh % 4 + 1) * P], ALU.mult, ALU.add)
                    m.then_inc(s_ready, 1)
            for b in range(4):
                dve.wait_ge(yroot, b + 1)
                link(v.reciprocal(MB_rt[:, b, :], MB_rt[:, b, :]))
                y = yo[:, 2 * b:2 * b + 2, :].rearrange("p a b -> p (a b)")
                link(v.scalar_tensor_tensor(y, y, par2[:, QGN:QGN + 1], MB_rt[:, b, :], ALU.mult, ALU.mult))
                v.tensor_tensor(y, y, zs[:, 2 * b:2 * b + 2, :].rearrange("p a b -> p (a b)"), ALU.mult).then_inc(ya_ready, 1)
            for m_ in range(2):
                dve.wait_ge(slot_done, B2 + UP0 + m_ + 1)
                d = sgb[:, 4 * m_:4 * m_ + 4, :].rearrange("p a b -> p (a b)")
                v.tensor_tensor(d, d, flat[:, 1024 * m_:1024 * m_ + 1024], ALU.mult).then_inc(up_out, 1)
            dve.wait_ge(up_out, 2)
            for j in range(4):
                dve.wait_ge(slot_done, B2 + UP0 + 2 + j + 1)
                d = sga[:, 2 * j:2 * j + 2, :].rearrange("p a b -> p (a b)")
                link(v.tensor_tensor(d, d, ps[:, 4 + j, :], ALU.mult))
                v.tensor_tensor(d, d, sgb[:, 2 * j:2 * j + 2, :].rearrange("p a b -> p (a b)"), ALU.add).then_inc(merged, 1)
            for j in range(4):
                dve.wait_ge(slot_done, B2 + OUT2 + j + 1)
                for n in range(2):
                    c = 2 * j + n
                    v.scalar_tensor_tensor(x[:, c, :], ps[:, j, n * T:(n + 1) * T], mod[:, 16 + c:17 + c], x[:, c, :],
                                           ALU.mult, ALU.add).then_inc(x_ready, 1)
            dve.wait_ge(x_ready, 16)
            scale_tokens(2, 32)

            sc = rt[:, 0, :].rearrange("p (t e) -> p t e", t=2)
            sel = rt[:, 1, :].rearrange("p (t e) -> p t e", t=2)
            bias = par2[:, QRB:QRB + EXPERTS].rearrange("p (a b) -> p a b", a=1).to_broadcast([P, 2, EXPERTS])
            link(v.memset(combT[EXPERTS:EXPERTS + 1, :], 1.0))
            link(v.memset(zero_t, 0.0))
            v.memset(rt[:, 15, 0:8], 0.0).then_inc(zero_ready, 1)
            dve.wait_ge(sc_ready, 1)
            link(v.tensor_tensor(sel, sc, bias, ALU.add))
            for t in range(2):
                for g in range(GROUPS):
                    m = v.max(rt[:, 2, 64 * t + 8 * g:64 * t + 8 * g + 8], rt[:, 1, 64 * t + 8 * g:64 * t + 8 * g + 8])
                link(m)
            top2 = rt[:, 2, :].rearrange("p (t g e) -> p t g e", t=2, g=GROUPS)
            gs = rt[:, 3, 0:16].rearrange("p (t g) -> p t g", t=2)
            link(v.tensor_tensor(gs, top2[:, :, :, 0], top2[:, :, :, 1], ALU.add))
            for t in range(2):
                a = rt[:, 3, 8 * t:8 * t + 8].rearrange("p (a b) -> p a b", a=1).to_broadcast([P, 8, 8])
                b = rt[:, 3, 8 * t:8 * t + 8].rearrange("p (a b) -> p a b", b=1).to_broadcast([P, 8, 8])
                gt8 = rt[:, 4, 64 * t:64 * t + 64].rearrange("p (a b) -> p a b", a=8)
                eq8 = rt[:, 5, 64 * t:64 * t + 64].rearrange("p (a b) -> p a b", a=8)
                link(v.tensor_tensor(gt8, a, b, ALU.is_gt))
                link(v.tensor_tensor(eq8, a, b, ALU.is_equal))
                link(v.tensor_tensor(eq8, eq8, cst[:, o_tie:o_tie + 64].rearrange("p (a b) -> p a b", a=8), ALU.mult))
                link(v.tensor_tensor(gt8, gt8, eq8, ALU.add))
                link(v.tensor_reduce(rt[:, 3, 16 + 8 * t:24 + 8 * t], gt8, AX_X, ALU.add))
            link(v.tensor_scalar(rt[:, 3, 32:48], rt[:, 3, 16:32], TOP_GROUPS - 0.5, None, ALU.is_lt))
            link(v.tensor_scalar(rt[:, 3, 48:64], rt[:, 3, 32:48], -NEG, NEG, ALU.mult, ALU.add))
            keep = [rt[:, 3, o:o + 16].rearrange("p (g b) -> p g b", b=1).to_broadcast([P, 16, 8]) for o in (32, 48)]
            s16 = rt[:, 1, :].rearrange("p (g e) -> p g e", g=16)
            link(v.tensor_tensor(s16, s16, keep[0], ALU.mult))
            link(v.tensor_tensor(s16, s16, keep[1], ALU.add))
            for t in range(2):
                s_ = rt[:, 1, 64 * t:64 * t + 64]
                link(v.max(rt[:, 6, 8 * t:8 * t + 8], s_))
                link(v.match_replace(rt[:, 7, 64 * t:64 * t + 64], rt[:, 6, 8 * t:8 * t + 8], s_, -3e38))
                link(v.tensor_scalar(rt[:, 7, 64 * t:64 * t + 64], rt[:, 7, 64 * t:64 * t + 64], -2e38, None, ALU.is_lt))
                link(v.tensor_tensor(rt[:, 7, 64 * t:64 * t + 64], rt[:, 7, 64 * t:64 * t + 64], rt[:, 0, 64 * t:64 * t + 64], ALU.mult))
                link(v.tensor_reduce(rt[:, 6, 32 + t:33 + t], rt[:, 7, 64 * t:64 * t + 64], AX_X, ALU.add))
                link(v.reciprocal(rt[:, 6, 34 + t:35 + t], rt[:, 6, 32 + t:33 + t]))
                v.tensor_scalar(rt[:, 8 + t, 0:EXPERTS], rt[:, 7, 64 * t:64 * t + 64], rt[:, 6, 34 + t:35 + t], ROUTE_SCALE,
                                ALU.mult, ALU.mult).then_inc(comb_ready, 1)

            E1 = EXPERTS + 1
            for i in range(2):
                v.memset(rt[:, 15, 8 + 16 * i:16 + 16 * i], 0.0).then_inc(hid_primed, 1)
                v.memset(rt[:, 15, 16 + 16 * i:24 + 16 * i], 0.0).then_inc(prod_primed, 1)
            dve.wait_ge(ct_out, 1)

            def row(q, e, column, primed=None):
                v.tensor_scalar(rhs_e[0:E1, q, :], combT[0:E1, :], column, None, ALU.mult).then_inc(row_ready, 1)

            def combine(q, e):
                dve.wait_ge(e_silu, e + 1)
                v.tensor_tensor(et[:, q, :], esil[:, q, :], ps[:, 2 * q + 1, :], ALU.mult).then_inc(prod_primed, 1)
                dve.wait_ge(prod_primed, e + 3)
                dve.wait_ge(cb_full, e + 1)
                cb = ps[:, 2 * q:2 * q + 1, 0:T].to_broadcast([P, 2, T])
                v.tensor_tensor(hid[:, q], et[:, q].rearrange("p (a b) -> p a b", a=2), cb, ALU.mult).then_inc(hid_primed, 1)

            row(0, 0, ident[0:E1, 0:1])
            dve.wait_ge(slot_done, EX0 + 2)
            combine(0, 0)
            with dve.Fori(0, EXPERTS // 2) as t:
                for q in (1, 0):
                    e = 2 * t + (1 if q else 2)
                    row(q, e, ident[0:E1, ds(e, 1)])
                    dve.wait_ge(slot_done, 6 * t + EX0 + (4 if q else 7))
                    combine(q, e)
            dve.wait_ge(y_full, 1)
            for c in range(DC):
                v.scalar_tensor_tensor(x[:, c, :], flat[:, 2048 + c * T:2048 + (c + 1) * T], mod[:, 40 + c:41 + c], x[:, c, :],
                                       ALU.mult, ALU.add).then_inc(x_ready, 1)

        @block.gpsimd
        def _(pool):
            with pool.Fori(0, DEPTH) as l:
                for c in range(CC):
                    W(pool, "ln_act", 2 * c + 2, l)
                    nc.gpsimd.tensor_tensor(cat[:, 4 + c, :], lnv[:, c, :], lns[:, c, :], ALU.mult).then_inc(conv_out, 1)
                W(pool, "conv_out", CC, l)
            tt = nc.gpsimd.tensor_tensor
            lev = [c2[:, KLEV + P * s_:KLEV + P * (s_ + 1)].rearrange("p (a b) -> p a b", a=1).to_broadcast([P, 4, P])
                   for s_ in range(6)]

            def col(o, p):
                return tiny[:, o + GH * p:o + GH * p + GH].rearrange("p (a b) -> p a b", b=1).to_broadcast([P, GH, P])

            def scale_step(i):
                if i == 0:
                    pool.wait_ge(x_out, 8)
                    for p in range(2):
                        m = tt(gV[:, p], gV[:, p], col(48, p), ALU.mult)
                elif i == 1:
                    pool.wait_ge(gtot_ready, 1)
                    for p in range(2):
                        m = tt(kbg[:, p], gK[:, p], col(144, p), ALU.mult)
                elif i == 2:
                    for p in range(2):
                        m = tt(gK[:, p], gK[:, p], col(96, p), ALU.mult)
                else:
                    m = tt(gq[:, :, :], gq[:, :, :], GB[:, :, :], ALU.mult)
                m.then_inc(pool_scaled, 1)
                pool.wait_ge(pool_scaled, i + 1)

            pool.wait_ge(loaded2, 16)
            for m_ in range(24):
                s_, b = divmod(m_, 4)
                if m_ < 4:
                    pool.wait_ge(l_ready, m_ + 1)
                if m_ >= 2:
                    pool.wait_ge(wt_full, m_ - 1)
                tt(Ms[:, m_ % 2], MA[:, b // 2, 4 * (b % 2):4 * (b % 2) + 4, :], lev[s_], ALU.mult).then_inc(m_ready, 1)
                if m_ % 4 == 3 and m_ // 4 < 4:
                    if m_ == 3:
                        pool.wait_ge(qk_full, 4)
                    scale_step(m_ // 4)


def chunk_pairs(w, order):
    v = w.reshape(DC, P, -1, P)
    return [v[:, :, list(pair), :].transpose(1, 0, 2, 3).reshape(1, P, SLOT) for pair in order]


def first_block_stream(x):
    parts = []
    for l in range(DEPTH):
        w = x["w_in"][l]
        pairs = [(12 + c, 16 + c) for c in range(4)] + [(2 * i, 2 * i + 1) for i in range(6)]
        parts += chunk_pairs(w, pairs)
        parts += chunk_pairs(x["w_ada_2"][0], [(24 * l + 2 * i, 24 * l + 2 * i + 1) for i in range(ADA_SLOTS)])
        parts += chunk_pairs(x["w_out"][l], [(2 * i, 2 * i + 1) for i in range(4)])
        parts += chunk_pairs(x["w_gate_up"][l], [(i, FC + i) for i in range(FC)])
        v = x["w_down"][l].reshape(FC, P, DC, P)
        for half in range(2):
            for g in range(6):
                part = v[4 * g:4 * g + 4, :, 4 * half:4 * half + 4, :].transpose(1, 0, 2, 3).reshape(P, -1)
                parts.append(np.concatenate([part, np.zeros((P, SLOT - part.shape[1]), np.float32)], 1)[None])
    return parts


def columns(v, n):
    return v.reshape(n, P).T


def layer_params(x, l):
    lam = np.zeros((P, 4), np.float32)
    for i, k in enumerate(("lam_q1", "lam_k1", "lam_q2", "lam_k2")):
        lam[:HD, i] = x[k][l]
    init = 0.8 - 0.6 * math.exp(-0.3 * l)
    return np.concatenate([
        columns(x["norm1_g"][l], 8), columns(x["b_glu"][l], 8),
        x["conv_w"][l].reshape(TAPS, CC, P).transpose(2, 1, 0).reshape(P, CC * TAPS),
        columns(x["conv_b"][l], CC), columns(x["conv_ln_g"][l], CC), columns(x["conv_ln_b"][l], CC),
        x["subln_g"][l].reshape(P, 1), columns(x["norm2_g"][l], 8), lam,
        np.full((P, 1), init, np.float32), np.full((P, 1), 1.0 - init, np.float32)], 1)


def constants():
    rot = np.zeros((P, P), np.float32)
    for b in range(0, P, HD):
        for d in range(HD // 2):
            rot[b + HD // 2 + d, b + d] = -1.0
            rot[b + d, b + HD // 2 + d] = 1.0
    inv = np.float32(10000.0) ** (-np.arange(0, HD, 2, dtype=np.float32) / np.float32(HD))
    ang = np.arange(L, dtype=np.float32)[:, None] * inv[None, :]
    ang = np.tile(ang, (1, 4)).T
    mask = np.zeros((P, 3, L), np.float32)
    for t, (q0, rows) in enumerate(Q_TILES):
        mask[:, t, :] = np.where(np.arange(L)[None, :] <= q0 + np.arange(P)[:, None], 0.0, -1e30)
    return np.concatenate([np.ones((P, P), np.float32), np.eye(P, dtype=np.float32), rot,
                           np.cos(ang), np.sin(ang), mask.reshape(P, -1),
                           np.broadcast_to(np.tril(np.ones((8, 8)), -1).reshape(1, 64), (P, 64))], 1).astype(np.float32)


def constants2():
    i, j = np.arange(P)[:, None], np.arange(P)[None, :]
    parts = []
    for t in range(2):
        q, k = t * P + np.arange(P)[:, None], np.arange((t + 1) * P)[None, :]
        for window, dil in WINDOW_DILATION:
            d = q - k
            parts.append(np.where((d >= 0) & (d % dil == 0) & (d // dil <= window // dil), 0.0, NEG))
    for s in (1, 2, 4, 8, 16, 32):
        parts.append(((i // (2 * s) == j // (2 * s)) & (i % (2 * s) >= s) & (j % (2 * s) < s)) * 1.0)
    same = i // CHUNK == j // CHUNK
    parts.append(np.where(same & (i >= j), 0.0, NEG))
    parts.append(np.where(same & (j >= i), 0.0, NEG))
    return np.concatenate(parts, 1).astype(np.float32)


def second_block_stream(x):
    parts = []
    w = x["w_in_2"][0]
    g = w[:, :4096]
    rest = w[:, 4112:]
    pairs = lambda n: [(2 * i, 2 * i + 1) for i in range(n)]
    parts += chunk_pairs(rest[:, :4608], pairs(18))
    parts += chunk_pairs(g, pairs(16))
    parts += chunk_pairs(rest[:, 4608:], pairs(8))
    v = x["w_up_dil_2"][0].reshape(4, P, DC, P)
    for m in range(2):
        parts.append(v[:, :, 4 * m:4 * m + 4, :].transpose(1, 0, 2, 3).reshape(1, P, SLOT))
    parts += chunk_pairs(x["w_up_gdn_2"][0], pairs(4))
    parts += chunk_pairs(x["w_out_2"][0], pairs(4))
    down = []
    for e in range(EXPERTS + 1):
        if e < EXPERTS:
            g, u, d = (x[f"w_exp_{k}_2"][0, e] for k in ("gate", "up", "down"))
        else:
            g, u, d = (x[f"w_sh_{k}_2"][0] for k in ("gate", "up", "down"))
        parts += chunk_pairs(g, [(0, 1)]) + chunk_pairs(u, [(0, 1)])
        if down:
            parts.append(down.pop())
        down.append(d.reshape(2, P, D).transpose(1, 0, 2).reshape(1, P, SLOT))
    return parts + down


def params2(x):
    def rows(a):
        return np.concatenate([a.reshape(GH, 1), np.zeros((P - GH, 1), np.float32)], 0)
    return np.concatenate([
        columns(x["g_mix_2"][0], 8), columns(x["g_ffn_2"][0], 8), columns(x["b_ada_2"][0], 48), columns(x["c_2"][0], 8),
        x["gdn_conv_w_2"][0].reshape(4, 24, P).transpose(2, 1, 0).reshape(P, 96),
        x["gdn_norm_g_2"][0].reshape(P, 1), x["dil_q_norm_g_2"][0].reshape(P, 1), x["dil_k_norm_g_2"][0].reshape(P, 1),
        rows(x["gdn_a_log_2"][0]), rows(x["gdn_dt_bias_2"][0]),
        np.broadcast_to(x["router_bias_2"][0][None, :], (P, EXPERTS))], 1)


def lay_out(x):
    tokens = np.concatenate([x["meta_tokens"], x["x"][0]], 0)
    return {
        "stream": np.concatenate(first_block_stream(x) + second_block_stream(x), 0),
        "par2": params2(x),
        "consts2": constants2(),
        "w_ba": x["w_in_2"][0][:, 4096:4112].reshape(DC, P, 16).transpose(1, 0, 2),
        "w_router": x["w_router_2"][0].reshape(DC, P, EXPERTS).transpose(1, 0, 2),
        "xT": tokens.T.reshape(DC, P, L).transpose(1, 0, 2),
        "par1": np.stack([layer_params(x, l) for l in range(DEPTH)], 1),
        "consts": constants(),
        "final_g": columns(x["final_g"], 8),
    }


def kernel(**inputs):
    import concourse.bacc as bacc
    from concourse.bass_utils import run_bass_kernel_spmd

    nc = bacc.Bacc("TRN2", target_bir_lowering=False, num_devices=1)
    arrays = {f"in_{n}": np.ascontiguousarray(a) for n, a in lay_out({k: np.asarray(a) for k, a in inputs.items()}).items()}
    args = {n[3:]: nc.dram_tensor(n, a.shape, F32, kind="ExternalInput").ap() for n, a in arrays.items()}
    args["out"] = nc.dram_tensor("out_xT", (P, DC, T), F32, kind="ExternalOutput").ap()
    build(nc, args)
    r = run_bass_kernel_spmd(nc, [arrays], core_ids=[0])
    return r.results[0]["out_xT"].transpose(2, 1, 0).reshape(1, T, D)
```

```python
from contextlib import ExitStack
import math

import numpy as np
import concourse.bass as bass
from concourse import mybir

ALU = mybir.AluOpType
ACT = mybir.ActivationFunctionType
F32 = mybir.dt.float32
F32R = mybir.dt.float32r
I32 = mybir.dt.int32
BF16 = mybir.dt.bfloat16
AX_X = mybir.AxisListType.X
ds = bass.ds

P = 128
D = 1024
DC = D // P

DEPTH = 2
SEQ = 256
META = 16
L = SEQ + META
HEADS = 4
HD = 64
FF = 2816
FC = FF // P
TAPS = 31
PAD = TAPS - 1
CC = 4
Q_TILES = [(0, 128), (128, 128), (256, 16)]
EPS1 = 1e-5
UNITS = [(h, t) for h in range(HEADS) for t in range(3)]

RING = 6
SLOT = 2048
IN_SLOTS, ADA_SLOTS, OUT_SLOTS, GU_SLOTS, DN_SLOTS = 10, 12, 4, FC, 12
OUT0 = IN_SLOTS + ADA_SLOTS
LAYER_SLOTS = OUT0 + OUT_SLOTS + GU_SLOTS + DN_SLOTS
assert LAYER_SLOTS % RING == 0

T = SEQ
GH = 8
CHUNK = 64
DG = 3
WINDOW_DILATION = ((128, 1), (512, 4), (2048, 16))
EXPERTS = 64
TOP = 8
GROUPS = 8
TOP_GROUPS = 4
EPS2 = 1e-6
NEG = -1e30
ROUTE_SCALE = 2.5
B2 = DEPTH * LAYER_SLOTS
DIL_SLOTS, GDN_SLOTS = 18, 12
Z0 = DIL_SLOTS + GDN_SLOTS
GATE0 = Z0 + 4
UP0 = GATE0 + 8
OUT2 = UP0 + 6
EX0 = B2 + OUT2 + 4
LOADS = 16 * 8
RB0 = EX0 + 3
BS = 64
MAX_BLOCKS = (TOP * T + (BS - 1) * EXPERTS) // BS
NBLK = (MAX_BLOCKS + 1) // 2 * 2 + 2
FAR = 16384

QMIX, QFFN, QADA, QC, QCW, QGN, QDQ, QDK, QAL, QDT, QRB = np.cumsum([0, 8, 8, 48, 8, 96, 1, 1, 1, 1, 1]).tolist()
NPAR2 = QRB + EXPERTS
KD0, KD1, KLEV, KLOW, KUP = np.cumsum([0, 3 * 128, 3 * 256, 6 * 128, 128]).tolist()
NCST2 = KUP + 128
KR0, KR1, KB, KFAR, KSLOT, KTHR, KE3 = np.cumsum([0, T, T, NBLK, NBLK, BS, T // BS]).tolist()
NCST3 = KE3 + 1
BIG0 = RING * SLOT + 2 * DC * L
OVERLAYS = [(f"wlo{j}", j * SLOT, SLOT) for j in range(RING)] + [
    ("yhi", BIG0 + 4096, D), ("ylo", BIG0 + 5120, D), ("STr", BIG0 + 6272, 2, T),
    ("whi3", BIG0 + 15616, SLOT), ("whi4", BIG0 + 15616 + SLOT, SLOT),
    ("whi0", BIG0 + 21104, SLOT), ("whi1", BIG0 + 21104 + SLOT, SLOT), ("whi2", BIG0 + 21104 + 2 * SLOT, SLOT),
    ("hghi", BIG0 + 27304, DC, BS), ("hglo", BIG0 + 27816, DC, BS),
    ("hThi", BIG0 + 28840, 2, BS), ("hTlo", BIG0 + 28968, 2, BS)]

PN1, PBG, PCW, PCB, PLG, PLB, PSG, PN2, PLAM, PLI, PLO = np.cumsum([0, 8, 8, CC * TAPS, CC, CC, CC, 1, 8, 4, 1]).tolist()
NPAR = PLO + 1


def build(nc, args, dbg=None):
    stream, xT, par1, consts, final_g, out = (args[k] for k in ("stream", "xT", "par1", "consts", "final_g", "out"))
    par2_d, consts2, w_ba_d, w_router_d = (args[k] for k in ("par2", "consts2", "w_ba", "w_router"))
    consts3_d = args["consts3"]
    NSLOT = stream.shape[0]
    TURNS = -(-NSLOT // RING)

    with ExitStack() as ctx:
        def sb(name, shape, dt=F32):
            return ctx.enter_context(nc.sbuf_tensor(name, shape, dt))

        rounded = {}
        with ExitStack() as over:
            upto = 0
            for name, o, *shape in OVERLAYS:
                if o > upto:
                    over.enter_context(nc.sbuf_tensor(f"before_{name}", [P, o - upto], F32))
                rounded[name] = over.enter_context(nc.sbuf_tensor(name, [P] + shape, F32R))
                upto = o + int(np.prod(shape))
        ring = sb("ring", [P, RING, SLOT])
        h = sb("h", [P, DC, L])
        hn = sb("hn", [P, DC, L])
        big = sb("big", [P, 30900])
        cst = sb("cst", [P, consts.shape[1]])
        ones, ident, rot = cst[:, 0:128], cst[:, 128:256], cst[:, 256:384]
        cos, sin = cst[:, 384:384 + L], cst[:, 384 + L:384 + 2 * L]
        o_tie = 384 + 5 * L
        o_mask = 384 + 2 * L
        causal = cst[:, o_mask:o_mask + 3 * L].rearrange("p (t k) -> p t k", t=3)
        par_all = sb("par_all", [P, DEPTH, NPAR])
        par = sb("par", [P, NPAR])
        fin_g = sb("fin_g", [P, DC])
        small = sb("small", [P, 64])
        root = sb("root", [P, HEADS, L])
        inv = sb("inv", [P, HEADS, L])

        at = [0]

        def carve(*shape):
            n = int(np.prod(shape))
            v = big[:, at[0]:at[0] + n]
            at[0] += n
            assert at[0] <= 30900, at
            if len(shape) == 2:
                v = v.rearrange("p (a b) -> p a b", a=shape[0])
            if len(shape) == 3:
                v = v.rearrange("p (a b c) -> p a b c", a=shape[0], b=shape[1])
            return v

        sq = carve(DC, L)
        zpad = carve(CC, PAD + L)
        conv = carve(CC, L)
        sgl = carve(CC, L)
        raw = carve(8, L)
        qk = carve(8, L)
        vT = carve(HEADS, L)
        V = carve(3, HEADS, P)
        rt1 = carve(2, L)
        rt2 = carve(2, L)
        after_w_in = at[0]
        Sm = carve(2, 2, L)
        Pr = carve(2, 2, L)
        Pt = carve(2, L)
        A = carve(2, L)
        aT = carve(2, 3, P)
        oraw = carve(HEADS, L)
        cat = carve(DC, L)
        xc = carve(CC, L)
        lsq = carve(CC, L)
        lnv = carve(CC, L)
        lns = carve(CC, L)
        attn_end = at[0]
        at[0] = PAD * CC + 2176 + CC * L
        hff = carve(FC, L)
        sgu = carve(2, L)
        at[0] = attn_end

        ps = ctx.enter_context(nc.psum_tensor("ps", [P, 8, 512], F32))
        par2 = sb("par2", [P, NPAR2])
        w_ba = sb("w_ba", [P, DC, 16])
        mod = sb("mod", [P, 48])
        cs = sb("cs", [P, DC])
        tiny = sb("tiny", [P, 192])
        lint = sb("lint", [1, NBLK + 1], I32)

        def region(o, *shape):
            n = int(np.prod(shape))
            v = big[:, o:o + n]
            names = "abcd"[:len(shape)]
            if len(shape) > 1:
                v = v.rearrange(f"p ({' '.join(names)}) -> p {' '.join(names)}", **dict(zip(names[:-1], shape[:-1])))
            return v

        x = h[:, :, META:L]
        hm = hn[:, :, 0:T]
        sqx = region(0, DC, T)
        c2 = region(0, NCST2)
        yb = region(2176, 4, T)
        dqk = region(3200, 24, T)
        zs = region(3200, GH, T)
        MA = region(5248, 2, GH, P)
        MB = region(7296, 2, GH, P)
        dV = region(9344, 2, 12, P)
        dS = region(12416, 2, 3, T)
        dpT = region(13952, 2, 6, P)
        vst = region(15488, 2, 2, T)
        GB = region(9344, GH, T)
        WT = region(9344, 2, GH, P)
        MT = region(11392, 2, GH, P)
        yo = region(11392, GH, T)
        gt_ = region(11392, 8, T)
        St = region(13440, GH, P)
        vn = region(14464, GH, P)
        MU = region(15488, 2, GH, P)
        sga = region(15488, GH, T)
        gdiag = region(17536, GH, T)
        kbg = region(17536, 2, GH, P)
        sgb = region(17536, GH, T)
        gq = region(19584, GH, T)
        gk = region(21632, GH, T)
        gV = region(23680, 2, GH, P)
        gK = region(25728, 2, GH, P)
        gpad = region(27776, 2, 2, T + 3)
        gacc = region(28812, 2, 2, T)
        sqd = region(29836, 2, 512)
        Ms = region(27776, 2, 4, P)
        Wts = region(28800, 2, 4, P)
        root2 = root[:, :, :].rearrange("p a b -> p (a b)")[:, 0:1024].rearrange("p (a b) -> p a b", a=2)
        inv2 = inv[:, :, :].rearrange("p a b -> p (a b)")[:, 0:1024].rearrange("p (a b) -> p a b", a=2)
        w_r = region(19584, DC, EXPERTS)
        cst3 = region(20096, NCST3)
        h2p = [region(1024 * i, D).bitcast(BF16).rearrange("p (t d) -> p t d", t=2) for i in range(3)]
        h2r = region(17664, 4, 512)
        yhi, ylo, STr = (rounded[n] for n in ("yhi", "ylo", "STr"))
        Sr = region(6144, BS).bitcast(BF16).rearrange("p (t s) -> p t s", t=2)
        ident_r = region(6784, P // 2).bitcast(BF16)
        SW = region(6912, 2, BS)
        whi = [[rounded[f"whi{r}"] for r in rs] for rs in ((0, 1, 2), (3, 4, 2))]
        wlo = [rounded[f"wlo{j}"] for j in range(RING)]
        hghi, hglo = rounded["hghi"], rounded["hglo"]
        gsil = region(28328, T)
        hidt = region(28584, T)
        hThi, hTlo = rounded["hThi"], rounded["hTlo"]
        wsc = region(7808, 2)
        nE, thr_hit, nblk, base, end, cpos = (region(7820 + 4 * i, 4) for i in range(6))
        E1 = region(8000, NBLK)
        E = region(8100, NBLK)
        posT = region(8200, T)
        pair_n = region(8456, 1)
        Pb = region(8500, 2, NBLK)
        Wb = region(8700, 2, NBLK)
        sel_T = region(8900, T)
        esil = region(9344, 512)
        hid = region(11392, 2, T)
        combT = region(12416, T)
        rt = region(13440, 16, 128)
        acc_sb = region(21104, 2, D)
        flat = ps[:, :, :].rearrange("p a b -> p (a b)")

        COUNT = {}
        SEM = {}

        def sem(name, per_layer=0):
            SEM[name] = ctx.enter_context(nc.semaphore(name))
            COUNT[name] = per_layer
            return SEM[name]

        loaded = sem("loaded")
        stepped = sem("stepped")
        out_done = sem("out_done")
        ring_full = [sem(f"ring_full{j}") for j in range(RING)]
        slot_done = sem("slot_done", LAYER_SLOTS)
        zeroed = sem("zeroed")
        h_added = sem("h_added", 16)
        par_ready = sem("par_ready", 1)
        sq_ready = sem("sq_ready", 4)
        norm_sum = sem("norm_sum", 2)
        norm_root = sem("norm_root", 2)
        hn_ready = sem("hn_ready", 16)
        lam_prod = sem("lam_prod", 1)
        lam_sum = sem("lam_sum", 1)
        lam_exp = sem("lam_exp", 1)
        even_full = sem("even_full", IN_SLOTS + OUT_SLOTS)
        glu_sig = sem("glu_sig", 4)
        glu_done = sem("glu_done", 4)
        raw_ready = sem("raw_ready", 8)
        rot_full = sem("rot_full", 8)
        rot_used = sem("rot_used", 8)
        qk_ready = sem("qk_ready", 8)
        vT_ready = sem("vT_ready", 4)
        vt_full = sem("vt_full", 4)
        v_ready = sem("v_ready", 8)
        conv_ready = sem("conv_ready", 1)
        mu_sum = sem("mu_sum", 1)
        xc_ready = sem("xc_ready", 1)
        lsq_ready = sem("lsq_ready", 1)
        var_sum = sem("var_sum", 1)
        var_root = sem("var_root", 1)
        xn_ready = sem("xn_ready", 1)
        ln_act = sem("ln_act", 8)
        conv_out = sem("conv_out", 4)
        s_full = sem("s_full", 12)
        s_masked = sem("s_masked", 12)
        smax = sem("smax", 12)
        exp_done = sem("exp_done", 24)
        a_ready = sem("a_ready", 12)
        at_full = sem("at_full", 12)
        at_ready = sem("at_ready", 12)
        o_full = sem("o_full", 4)
        o_copied = sem("o_copied", 8)
        osq_ready = sem("osq_ready", 4)
        sub_sum = sem("sub_sum", 1)
        sub_root = sem("sub_root", 1)
        attn_out = sem("attn_out", 4)
        gate_act = sem("gate_act", FC)
        hff_ready = sem("hff_ready", FC)
        at_part = sem("at_part", 4)
        chain_v = sem("chain_v")
        chain_a = sem("chain_a")
        cs_ready = sem("cs_ready")
        x_ready = sem("x_ready")
        hm_scaled = sem("hm_scaled")
        hm_ready = sem("hm_ready")
        loaded2 = sem("loaded2")
        padded = sem("padded")
        gemm_out = sem("gemm_out")
        msum = sem("msum")
        mroot = sem("mroot")
        mnorm = sem("mnorm")
        dv_full = sem("dv_full")
        dv_out = sem("dv_out")
        ba_full = sem("ba_full")
        ds_full = sem("ds_full")
        dmask = sem("dmask")
        dmax = sem("dmax")
        dexp = sem("dexp")
        dcoef = sem("dcoef")
        dtp = sem("dtp")
        dpt_ready = sem("dpt_ready")
        do_full = sem("do_full")
        yb_ready = sem("yb_ready")
        gconv = sem("gconv")
        gsilu = sem("gsilu")
        gsq = sem("gsq")
        x_full = sem("x_full")
        x_out = sem("x_out")
        gate_a1 = sem("gate_a1")
        gate_v1 = sem("gate_v1")
        gate_a2 = sem("gate_a2")
        gdiag_ready = sem("gdiag_ready")
        gb_full = sem("gb_full")
        gb_out = sem("gb_out")
        d_built = sem("d_built")
        d_exp = sem("d_exp")
        gcols = sem("gcols")
        kk_full = sem("kk_full")
        l_ready = sem("l_ready")
        qk_full = sem("qk_full")
        qkt_ready = sem("qkt_ready")
        tu_init = sem("tu_init")
        m_ready = sem("m_ready")
        wt_full = sem("wt_full")
        wt_copied = sem("wt_copied")
        tu_full = sem("tu_full")
        tu_done = sem("tu_done")
        pool_scaled = sem("pool_scaled")
        gtot_ready = sem("gtot_ready")
        u_full = sem("u_full")
        u_out = sem("u_out")
        w_full = sem("w_full")
        w_out = sem("w_out")
        vn_full = sem("vn_full")
        vn_ready = sem("vn_ready")
        oc_full = sem("oc_full")
        oc_out = sem("oc_out")
        su_full = sem("su_full")
        s_ready = sem("s_ready")
        ysq = sem("ysq")
        ysum = sem("ysum")
        yroot = sem("yroot")
        ya_ready = sem("ya_ready")
        up_out = sem("up_out")
        merged = sem("merged")
        sc_full = sem("sc_full")
        sc_ready = sem("sc_ready")
        comb_ready = sem("comb_ready")
        ct_full = sem("ct_full")
        ct_out = sem("ct_out")
        whi_ready = sem("whi_ready")
        wlo_ready = sem("wlo_ready")
        wlo_down = sem("wlo_down")
        hglo_ready = sem("hglo_ready")
        th_full = sem("th_full")
        thi_ready = sem("thi_ready")
        tlo_ready = sem("tlo_ready")
        tm_full = sem("tm_full")
        tm_hi = sem("tm_hi")
        tm_lo = sem("tm_lo")
        zero_ready = sem("zero_ready")
        sh_silu = sem("sh_silu")
        route_full = sem("route_full")
        route_ready = sem("route_ready")
        count_ready = sem("count_ready")
        place_ready = sem("place_ready")
        g_full = sem("g_full")
        hg_ready = sem("hg_ready")
        blk_silu = sem("blk_silu")
        blk_hid = sem("blk_hid")
        t_full = sem("t_full")
        t_out = sem("t_out")
        d_half = sem("d_half")
        yhi_ready = sem("yhi_ready")
        ylo_ready = sem("ylo_ready")
        acc_full = sem("acc_full")
        acc_out = sem("acc_out")
        y_full = sem("y_full")
        MA_sq = region(5248, 4, 512)
        MB_rt = region(7296, 4, 512)

        block = ctx.enter_context(nc.Block())

        def W(eng, name, value, l=0):
            eng.wait_ge(SEM[name], l * COUNT[name] + value)

        def W_alone(eng, name, value, l=0):
            W(eng, name, value, l)
            eng.sem_inc(stepped, 1)

        def after_layers(name, value):
            return DEPTH * COUNT[name] + value

        @block.sync
        def _(sp):
            sp.dma_start(h[:, :, :], xT).then_inc(loaded, 16)
            sp.dma_start(cst[:, :], consts).then_inc(loaded, 16)
            sp.dma_start(par_all[:, :, :], par1).then_inc(loaded, 16)
            sp.dma_start(fin_g[:, :], final_g).then_inc(loaded, 16)
            sp.dma_start(par2[:, :], par2_d).then_inc(loaded, 16)
            sp.dma_start(w_ba[:, :, :], w_ba_d).then_inc(loaded, 16)
            sp.dma_start(cs[:, :], par2_d[:, QC:QC + DC]).then_inc(loaded, 16)
            sp.dma_start(small[:, 40:48], par2_d[:, QC:QC + DC]).then_inc(loaded, 16)
            for j in range(RING):
                sp.dma_start(ring[:, j, :], stream[j, :, :]).then_inc(ring_full[j], 16)

            def refill(i, j):
                sp.wait_ge(slot_done, i - RING + 1)
                src = stream[i, :, :] if isinstance(i, int) else stream[ds(i, 1), :, :].rearrange("a p n -> (a p) n")
                sp.dma_start(ring[:, j, :], src).then_inc(ring_full[j], 16)

            with sp.Fori(1, RB0 // RING) as t:
                for j in range(RING):
                    refill(t * RING + j, j)
            for i in range(RB0 // RING * RING, RB0):
                refill(i, i % RING)
            sp.wait_ge(count_ready, 2)
            pairs = sp.value_load(lint[0:1, NBLK:NBLK + 1], min_val=1, max_val=NBLK // 2 - 1)

            def load_block(t, q, parts=3):
                first = sp.value_load(lint[0:1, ds(2 * t + q, 1)], min_val=RB0, max_val=NSLOT - 3)
                for r in range(parts):
                    sp.wait_ge(slot_done, 6 * t + RB0 + 3 * q + r - RING + 1)
                    sp.dma_start(ring[:, (RB0 + 3 * q + r) % RING, :],
                                 stream[ds(first + r, 1), :, :].rearrange("a p n -> (a p) n"))\
                        .then_inc(ring_full[(RB0 + 3 * q + r) % RING], 16)

            with sp.Fori(0, pairs) as t:
                for q in range(2):
                    load_block(t, q)
            load_block(pairs, 0, parts=2)
            sp.wait_ge(x_ready, 24)
            sp.dma_start(out, x).then_inc(out_done, 16)
            sp.wait_ge(out_done, 16)


        @block.tensor
        def _(pe):
            mm = nc.tensor.matmul

            def slot(s, turn0):
                pe.wait_ge(ring_full[s % RING], (turn0 + s // RING + 1) * 16)
                return ring[:, s % RING, :]

            def norm_sums(l, which):
                for c in range(DC):
                    if c % 4 == 0:
                        W(pe, "sq_ready", 2 * which + c // 4 + 1, l)
                    m = mm(ps[:, 7, 0:L], ones, sq[:, c, :], start=c == 0, stop=c == DC - 1)
                m.then_inc(norm_sum, 1)

            def pair(w, rhs, banks, order=range(DC), cols=L, wait=None, even=True):
                for n in range(2):
                    for q, k in enumerate(order):
                        if n == 0 and wait:
                            wait(k)
                        m = mm(ps[:, banks[n], 0:cols], w[:, k, n, :], rhs[:, k, 0:cols],
                               start=q == 0, stop=q == DC - 1)
                    if n == 0 and even:
                        m.then_inc(even_full, 1)
                m.then_inc(slot_done, 1)

            pe.wait_ge(loaded, LOADS)
            pe.wait_ge(cs_ready, 1)
            with pe.Fori(0, DEPTH) as l:
                turn = l * (LAYER_SLOTS // RING)

                def weights(s, t0=0):
                    return slot(s, turn + t0).rearrange("p (k n c) -> p k n c", k=8, n=2)

                norm_sums(l, 0)
                W(pe, "lam_prod", 1, l)
                mm(ps[:, 6, 0:2], ones[0:HD, :], small[0:HD, 0:2], start=True, stop=True).then_inc(lam_sum, 1)

                def rotate(j):
                    W(pe, "raw_ready", j + 1, l)
                    if j >= 2:
                        W(pe, "rot_used", j - 1, l)
                    mm(ps[:, 4 + j % 2, 0:L], rot, raw[:, j, :], start=True, stop=True).then_inc(rot_full, 1)

                def turn_v(j):
                    W(pe, "vT_ready", j + 1, l)
                    if j >= 2:
                        W(pe, "v_ready", 2 * (j - 1), l)
                    for t, (k0, kn) in enumerate(Q_TILES):
                        m = nc.tensor.transpose(ps[0:kn, 6 + j % 2, t * P:t * P + P], vT[:, j, k0:k0 + kn], ident)
                    m.then_inc(vt_full, 1)

                for s in range(IN_SLOTS):
                    w = weights(s)
                    if 2 <= s < 6:
                        W(pe, "glu_done", s - 1, l)
                    if 6 <= s < 8:
                        W(pe, "raw_ready", 2 * (s - 6) + 2, l)
                    if s >= 8:
                        W(pe, "raw_ready", 2 * (s - 6) + 2, l)
                    pair(w, hn, (2 * (s % 2), 2 * (s % 2) + 1),
                         wait=(lambda k: W(pe, "hn_ready", k + 1, l)) if s == 0 else None)
                    if s >= 5:
                        if s < 9:
                            rotate(2 * (s - 5))
                            rotate(2 * (s - 5) + 1)
                        else:
                            turn_v(0)
                            turn_v(1)
                turn_v(2)
                turn_v(3)

                def scores(u):
                    head, t = UNITS[u]
                    q0, rows = Q_TILES[t]
                    keys = q0 + rows
                    b = 4 + 2 * (u % 2)
                    if u < 2:
                        W(pe, "v_ready", 8, l)
                        W_alone(pe, "qk_ready", 8, l)
                    else:
                        W_alone(pe, "s_masked", u - 1, l)
                    for c in range(2):
                        r = slice(64 * c, 64 * c + 64)
                        m = mm(ps[0:rows, b + c, 0:keys], qk[r, head, q0:q0 + rows], qk[r, HEADS + head, 0:keys],
                               start=True, stop=True)
                    m.then_inc(s_full, 1)

                def turn_probs(u):
                    head, t = UNITS[u]
                    q0, rows = Q_TILES[t]
                    if u >= 2:
                        W(pe, "at_ready", u - 1, l)
                    W_alone(pe, "a_ready", u + 1, l)
                    for kt in range(t + 1):
                        k0, kn = Q_TILES[kt]
                        m = nc.tensor.transpose(ps[0:kn, u % 2, kt * P:kt * P + rows], A[0:rows, u % 2, k0:k0 + kn],
                                                ident[0:rows, 0:rows])
                    m.then_inc(at_full, 1)

                def modulate(u):
                    head, t = UNITS[u]
                    w = weights(IN_SLOTS + u)
                    for n in range(2):
                        for k in range(DC):
                            m = mm(ps[:, 2 + head % 2, L + 2 * t + n:L + 2 * t + n + 1], w[:, k, n, :], cs[:, k:k + 1],
                                   start=k == 0, stop=k == DC - 1)
                    m.then_inc(slot_done, 1)

                def weigh(u):
                    head, t = UNITS[u]
                    q0, rows = Q_TILES[t]
                    if head >= 2 and t == 0:
                        W(pe, "osq_ready", head - 1, l)
                    modulate(u)
                    W(pe, "at_ready", u + 1, l)
                    for kt in range(t + 1):
                        kn = Q_TILES[kt][1]
                        m = mm(ps[:, 2 + head % 2, q0:q0 + rows], V[0:kn, kt, head, :], aT[0:kn, u % 2, kt, 0:rows],
                               start=kt == 0, stop=kt == t)
                    if t == 2:
                        m.then_inc(o_full, 1)

                W(pe, "vT_ready", 4, l)
                W(pe, "conv_ready", 1, l)
                for c in range(CC):
                    m = mm(ps[:, 0, 0:L], ones, conv[:, c, :], start=c == 0, stop=c == CC - 1)
                m.then_inc(mu_sum, 1)
                scores(0)
                scores(1)
                W(pe, "lsq_ready", 1, l)
                for c in range(CC):
                    m = mm(ps[:, 1, 0:L], ones, lsq[:, c, :], start=c == 0, stop=c == CC - 1)
                m.then_inc(var_sum, 1)
                W(pe, "var_root", 1, l)
                for u in range(12):
                    turn_probs(u)
                    if u + 2 < 12:
                        scores(u + 2)
                    if u >= 1:
                        weigh(u - 1)
                weigh(11)
                W(pe, "s_masked", 12, l)
                for head in range(HEADS):
                    W(pe, "osq_ready", head + 1, l)
                    m = mm(ps[:, 4 + head, 0:L], ones, sq[:, head, :], start=True, stop=True)
                m.then_inc(sub_sum, 1)

                W(pe, "conv_out", 4, l)
                W(pe, "at_ready", 12, l)
                for n in range(OUT_SLOTS):
                    w = weights(OUT0 + n)
                    if n >= 2:
                        W(pe, "h_added", 1 + 2 * (n - 1), l)
                    pair(w, cat, (2 * (n % 2), 2 * (n % 2) + 1), order=[4, 5, 6, 7, 0, 1, 2, 3],
                         wait=(lambda k: W(pe, "attn_out", k % 4 + 1, l) if k < 4 else None) if n == 0 else None)
                norm_sums(l, 1)

                g0 = OUT0 + OUT_SLOTS

                def gate_up(i, s, t0=0, wait=None, need=None):
                    w = slot(s, turn + t0).rearrange("p (k n c) -> p k n c", k=8, n=2)
                    if need is not None:
                        W(pe, "hff_ready", need, l)
                    pair(w, hn, (2 * (i % 2), 2 * (i % 2) + 1), wait=wait, even=False)

                for i in range(4):
                    gate_up(i, g0 + i, need=i - 1 if i >= 2 else None,
                            wait=(lambda k: W(pe, "hn_ready", 8 + k + 1, l)) if i == 0 else None)
                with pe.Fori(0, (GU_SLOTS - 4) // RING) as t:
                    for i in range(RING):
                        gate_up(i, g0 + 4 + i, t0=t, need=t * RING + i + 3)

                d0 = g0 + GU_SLOTS
                for half in range(2):
                    for g in range(6):
                        s = d0 + 6 * half + g
                        w = slot(s, turn).rearrange("p (k n c) -> p k n c", k=4, n=4)
                        if half == 0:
                            W(pe, "hff_ready", min(4 * g + 4, FC), l)
                        for k in range(min(4, FC - 4 * g)):
                            for n in range(4):
                                m = mm(ps[:, 4 - 4 * half + n, 0:L], w[:, k, n, :], hff[:, 4 * g + k, :],
                                       start=g + k == 0, stop=4 * g + k == FC - 1)
                        m.then_inc(slot_done, 1)
            norm_sums(DEPTH, 0)

            def token_sums(which):
                for c in range(DC):
                    if c % 4 == 0:
                        W(pe, "sq_ready", 2 * which + c // 4 + 1, DEPTH)
                    m = mm(ps[:, 7, 0:T], ones, sqx[:, c, :], start=c == 0, stop=c == DC - 1)
                m.then_inc(norm_sum, 1)

            token_sums(1)

            def project(i, wait=None):
                w = slot(B2 + i, 0).rearrange("p (k n c) -> p k n c", k=8, n=2)
                if i >= 2:
                    pe.wait_ge(gemm_out, i - 1)
                for n in range(2):
                    for k in range(DC):
                        if wait and n == 0:
                            pe.wait_ge(hm_ready, k + 1)
                        m = mm(ps[:, i % 2, n * T:(n + 1) * T], w[:, k, n, :], hm[:, k, :], start=k == 0, stop=k == DC - 1)
                m.then_inc(slot_done, 1)

            def square_sum(j, ready, value):
                pe.wait_ge(ready, value)
                if j >= 1:
                    pe.wait_ge(mroot, j)
                mm(ps[:, 2, :], ones, sqd[:, j % 2, :], start=True, stop=True).then_inc(msum, 1)

            def turn4(bank, src):
                for a in range(2):
                    for t in range(2):
                        m = nc.tensor.transpose(ps[:, bank, (2 * a + t) * P:(2 * a + t + 1) * P],
                                                src[:, a, t * P:(t + 1) * P], ident)
                return m

            def turn_dv(i):
                pe.wait_ge(gemm_out, i + 1)
                if i >= 14:
                    pe.wait_ge(dv_out, i - 13)
                turn4(4 + i % 2, vst[:, i % 2]).then_inc(dv_full, 1)

            for i in range(DIL_SLOTS):
                project(i, wait=i == 0)
                if 1 <= i <= 12:
                    square_sum(i - 1, gemm_out, i)
                if i >= 13:
                    turn_dv(i - 1)
            turn_dv(17)
            for o in range(2):
                for k in range(DC):
                    m = mm(ps[0:GH, 3, o * T:(o + 1) * T], w_ba[:, k, o * GH:(o + 1) * GH], hm[:, k, :],
                           start=k == 0, stop=k == DC - 1)
            m.then_inc(ba_full, 1)

            def dil_scores(d):
                hs, t = divmod(d, 2)
                if d == 0:
                    pe.wait_ge(dv_out, 6)
                    pe.wait_ge(mnorm, 12)
                else:
                    pe.wait_ge(dmask, d)
                for g in range(DG):
                    m = mm(flat[:, 4 * 512 + g * T:4 * 512 + g * T + (t + 1) * P],
                           dqk[:, 4 * g + hs, t * P:(t + 1) * P], dqk[:, 12 + 4 * g + hs, 0:(t + 1) * P],
                           start=True, stop=True)
                m.then_inc(ds_full, 1)

            def dil_turn(d):
                t = d % 2
                pe.wait_ge(dcoef, d + 1)
                if d >= 1:
                    pe.wait_ge(yb_ready, d)
                for g in range(DG):
                    for kt in range(t + 1):
                        o = 6 * 512 + (2 * g + kt) * P
                        m = nc.tensor.transpose(flat[:, o:o + P], dS[:, d % 2, g, kt * P:(kt + 1) * P], ident)
                m.then_inc(dtp, 1)

            def dil_out(d):
                hs, t = divmod(d, 2)
                pe.wait_ge(dpt_ready, d + 1)
                n = 0
                for g in range(DG):
                    for kt in range(t + 1):
                        n += 1
                        m = mm(ps[:, 6, 0:P], dV[:, kt, 4 * g + hs, :], dpT[:, d % 2, 2 * g + kt, :],
                               start=n == 1, stop=n == DG * (t + 1))
                m.then_inc(do_full, 1)

            def turn_kv(n):
                if n < 8:
                    pe.wait_ge(mnorm, 12 + n + 1)
                    src = gk[:, 2 * (n - 4):2 * (n - 4) + 2, :]
                else:
                    pe.wait_ge(gsilu, n + 1)
                    src = vst[:, n % 2]
                pe.wait_ge(gate_a1, 1)
                if n > 4:
                    pe.wait_ge(x_out, n - 4)
                turn4(3, src).then_inc(x_full, 1)

            for n in range(14):
                if n < 12:
                    project(DIL_SLOTS + n)
                if n < 8:
                    dil_scores(n)
                if 1 <= n <= 8:
                    square_sum(12 + n - 1, gsq, n)
                    dil_turn(n - 1)
                if 4 <= n - 2 < 12:
                    turn_kv(n - 2)
                if 1 <= n <= 8:
                    dil_out(n - 1)

            project(Z0)
            pe.wait_ge(x_out, 8)
            pe.wait_ge(gdiag_ready, 1)
            for o, src in enumerate((gt_[:, 5, :], gt_[:, 0, :])):
                for t in range(2):
                    nc.tensor.transpose(ps[:, 3, (2 * o + t) * GH:(2 * o + t + 1) * GH], src[0:GH, t * P:(t + 1) * P],
                                        ident[0:GH, 0:GH])
            pe.wait_ge(yb_ready, 8)
            for b in range(4):
                m = mm(ps[:, 4 + b, :], ones[0:GH, :], gdiag[0:GH, 2 * b:2 * b + 2, :], start=True, stop=True)
            m.then_inc(gb_full, 1)
            pe.wait_ge(gb_out, 2)
            pe.wait_ge(mnorm, 20)

            def batch(b):
                return b // 2, range(4 * (b % 2), 4 * (b % 2) + 4)

            for b in range(4):
                p, heads = batch(b)
                for hh in heads:
                    kT = gk[:, hh, p * P:(p + 1) * P]
                    m = mm(ps[:, 4 + b, (hh % 4) * P:(hh % 4 + 1) * P], kT, kT, start=True, stop=True)
                m.then_inc(kk_full, 1)
            for b in range(4):
                p, heads = batch(b)
                pe.wait_ge(l_ready, b + 1)
                for hh in heads:
                    m = mm(ps[:, 4 + b, (hh % 4) * P:(hh % 4 + 1) * P], gk[:, hh, p * P:(p + 1) * P],
                           gq[:, hh, p * P:(p + 1) * P], start=True, stop=True)
                m.then_inc(qk_full, 1)

            def inv_w(m_):
                s_, b = divmod(m_, 4)
                p, heads = batch(b)
                pe.wait_ge(m_ready, m_ + 1)
                if m_ == 0:
                    pe.wait_ge(tu_init, 2)
                    pe.wait_ge(qkt_ready, 4)
                if s_ >= 1:
                    pe.wait_ge(tu_done, 4 * (s_ - 1) + b + 1)
                if m_ >= 2:
                    pe.wait_ge(wt_copied, m_ - 1)
                for hh in heads:
                    m = mm(ps[:, 2 + 3 * (m_ % 2), (hh % 4) * P:(hh % 4 + 1) * P], Ms[:, m_ % 2, hh % 4, :],
                           MU[:, p, hh, :], start=True, stop=True)
                m.then_inc(wt_full, 1)

            def inv_tu(m_):
                s_, b = divmod(m_, 4)
                p, heads = batch(b)
                pe.wait_ge(wt_copied, m_ + 1)
                if m_ >= 2:
                    pe.wait_ge(tu_done, m_ - 1)
                for hh in heads:
                    c = slice((hh % 4) * P, (hh % 4 + 1) * P)
                    mm(ps[:, 3 + 3 * (m_ % 2), c], Wts[:, m_ % 2, hh % 4, :], MT[:, p, hh, :], start=True, stop=True)
                    m = mm(ps[:, 4 + 3 * (m_ % 2), c], MT[:, p, hh, :], Wts[:, m_ % 2, hh % 4, :], start=True, stop=True)
                m.then_inc(tu_full, 1)

            inv_w(0)
            for m_ in range(24):
                if m_ in (5, 11, 17):
                    project(Z0 + 1 + m_ // 6)
                if m_ + 1 < 24:
                    inv_w(m_ + 1)
                inv_tu(m_)
            pe.wait_ge(tu_done, 24)
            for b in range(4):
                p, heads = batch(b)
                if b == 0:
                    pe.wait_ge(pool_scaled, 2)
                for hh in heads:
                    m = mm(ps[:, 2 + b, (hh % 4) * P:(hh % 4 + 1) * P], MU[:, p, hh, :], gV[:, p, hh, :],
                           start=True, stop=True)
                m.then_inc(u_full, 1)
            for b in range(4):
                p, heads = batch(b)
                bank = (6, 7, 2, 3)[b]
                if b >= 2:
                    pe.wait_ge(u_out, b - 1)
                for hh in heads:
                    m = mm(ps[:, bank, (hh % 4) * P:(hh % 4 + 1) * P], kbg[:, p, hh, :], MU[:, p, hh, :],
                           start=True, stop=True)
                m.then_inc(w_full, 1)
            pe.wait_ge(w_out, 4)
            pe.wait_ge(u_out, 4)
            pe.wait_ge(pool_scaled, 4)
            for c in range(4):
                p, r = c // 2, slice(CHUNK * (c % 2), CHUNK * (c % 2) + CHUNK)
                pe.wait_ge(s_ready, c + 1)
                for hh in range(GH):
                    m = mm(ps[r, 2 + hh // 4, (hh % 4) * P:(hh % 4 + 1) * P], WT[:, p, hh, r], St[:, hh, :],
                           start=True, stop=True)
                m.then_inc(vn_full, 1)
                project(GATE0 + 2 * c)
                pe.wait_ge(vn_ready, c + 1)
                if c >= 2:
                    pe.wait_ge(oc_out, c - 1)
                for hh in range(GH):
                    o = ps[:, 4 + c % 2, hh * CHUNK:(hh + 1) * CHUNK]
                    mm(o, St[:, hh, :], gq[:, hh, c * CHUNK:(c + 1) * CHUNK], start=True, stop=False)
                    m = mm(o, vn[r, hh, :], MB[r, p, hh, r], start=False, stop=True)
                m.then_inc(oc_full, 1)
                if c < 3:
                    for hh in range(GH):
                        m = mm(ps[:, 6 + hh // 4, (hh % 4) * P:(hh % 4 + 1) * P], gK[r, p, hh, :], vn[r, hh, :],
                               start=True, stop=True)
                    m.then_inc(su_full, 1)
                project(GATE0 + 2 * c + 1)

            pe.wait_ge(s_ready, 4)
            for b in range(4):
                pe.wait_ge(ysq, b + 1)
                mm(ps[:, 4 + b, :], ones, MA_sq[:, b, :], start=True, stop=True).then_inc(ysum, 1)

            pe.wait_ge(gemm_out, UP0)
            for m_ in range(2):
                w = slot(B2 + UP0 + m_, 0).rearrange("p (k n c) -> p k n c", k=4, n=4)
                for n in range(4):
                    for k in range(4):
                        m = mm(ps[:, 2 * m_ + n // 2, (n % 2) * T:(n % 2 + 1) * T], w[:, k, n, :], yb[:, k, :],
                               start=k == 0, stop=k == 3)
                m.then_inc(slot_done, 1)
            for j in range(4):
                w = slot(B2 + UP0 + 2 + j, 0).rearrange("p (k n c) -> p k n c", k=8, n=2)
                if j == 0:
                    pe.wait_ge(yroot, 4)
                for n in range(2):
                    for k in range(DC):
                        if j == 0 and n == 0 and k % 2 == 0:
                            pe.wait_ge(ya_ready, k // 2 + 1)
                        m = mm(ps[:, 4 + j, n * T:(n + 1) * T], w[:, k, n, :], yo[:, k, :], start=k == 0, stop=k == DC - 1)
                m.then_inc(slot_done, 1)
            for j in range(4):
                w = slot(B2 + OUT2 + j, 0).rearrange("p (k n c) -> p k n c", k=8, n=2)
                for n in range(2):
                    for k in range(DC):
                        if j == 0 and n == 0 and k % 2 == 0:
                            pe.wait_ge(merged, k // 2 + 1)
                        m = mm(ps[:, j, n * T:(n + 1) * T], w[:, k, n, :], sga[:, k, :], start=k == 0, stop=k == DC - 1)
                m.then_inc(slot_done, 1)
            token_sums(2)
            pe.wait_ge(loaded2, 48)
            for t in range(2):
                for k in range(DC):
                    pe.wait_ge(hm_ready, DC + k + 1)
                    m = mm(ps[:, 6, t * EXPERTS:(t + 1) * EXPERTS], hm[:, k, t * P:(t + 1) * P], w_r[:, k, :],
                           start=k == 0, stop=k == DC - 1)
            m.then_inc(sc_full, 1)
            for g in range(4):
                for i in range(4):
                    k = 4 * (g % 2) + i
                    m = nc.tensor.transpose(ps[:, (4, 7, 2, 3)[g], i * P:(i + 1) * P],
                                            hm[:, k, (g // 2) * P:(g // 2 + 1) * P], ident)
                m.then_inc(tm_full, 1)

            ET, EJ = divmod(EX0, RING)
            for b in range(2):
                w = slot(EJ + b, ET).rearrange("p (k n c) -> p k n c", k=8, n=2)
                for n in range(2):
                    for k in range(DC):
                        m = mm(ps[:, b, n * T:(n + 1) * T], w[:, k, n, :], hm[:, k, :], start=k == 0, stop=k == DC - 1)
                m.then_inc(slot_done, 1)
            pe.wait_ge(comb_ready, 2)
            pe.wait_ge(tm_lo, 4)
            for t in range(2):
                nc.tensor.transpose(ps[0:EXPERTS, 6, t * P:(t + 1) * P], rt[:, 8 + t, 0:EXPERTS], ident)
            for t in range(2):
                m = nc.tensor.transpose(ps[0:EXPERTS, 6, T + t * P:T + (t + 1) * P],
                                        rt[:, 10, t * EXPERTS:(t + 1) * EXPERTS], ident)
            m.then_inc(ct_full, 1)
            for t in range(2):
                m = mm(ps[0:EXPERTS, 3, 0:T], rt[:, 10, t * EXPERTS:(t + 1) * EXPERTS],
                       cst3[:, KR0 + t * T:KR0 + (t + 1) * T], start=t == 0, stop=t == 1)
            pe.wait_ge(zero_ready, 2)
            w_sh = slot(EJ + 2, ET).rearrange("p (f n) -> p f n", f=2)

            def shared_down(t):
                for half in range(2):
                    for f_ in range(2):
                        m = mm(ps[:, 4 + 2 * t + half, :], hid[:, f_, t * P:(t + 1) * P], w_sh[:, f_, half * 512:(half + 1) * 512],
                               start=f_ == 0, stop=False, skip_group_check=True)
                return m

            shared_down(0)
            pe.wait_ge(route_ready, 1)
            mm(ps[0:EXPERTS, 2, 0:1], cst3[0:EXPERTS, KR0:KR0 + EXPERTS], nblk[0:EXPERTS, 0:1], start=True, stop=True)\
                .then_inc(route_full, 1)
            pe.wait_ge(ct_out, 2)
            shared_down(1).then_inc(slot_done, 1)
            pe.wait_ge(route_ready, 2)
            for t in range(2):
                mm(ps[:, 3, t * NBLK:(t + 1) * NBLK], posT[0:EXPERTS, t * P:(t + 1) * P], E[0:EXPERTS, :], start=True, stop=True)
            for t in range(2):
                mm(ps[:, 3, (2 + t) * NBLK:(3 + t) * NBLK], combT[0:EXPERTS, t * P:(t + 1) * P], E[0:EXPERTS, :],
                   start=True, stop=True)
            mm(ps[0:1, 3, 4 * NBLK:5 * NBLK], cst3[0:EXPERTS, KE3:KE3 + 1], E[0:EXPERTS, :], start=True, stop=True)
            mm(ps[0:1, 2, 0:NBLK], ones[0:EXPERTS, 0:1], E[0:EXPERTS, :], start=True, stop=True).then_inc(route_full, 1)

            def gather(b):
                pe.wait_ge(place_ready, b + 1)
                if not isinstance(b, int):
                    pe.wait_ge(hglo_ready, b)
                for k in range(DC):
                    for t in range(2):
                        for i, part in enumerate(h2p):
                            m = mm(ps[:, 1, k * BS:(k + 1) * BS], part[:, t, k * P:(k + 1) * P], Sr[:, t, :],
                                   start=t + i == 0, stop=t + i == 3)
                m.then_inc(g_full, 1)

            def turn_places(b):
                for t in range(2):
                    mm(ps[0:BS, 0, t * P:(t + 1) * P], Sr[:, t, :], ident_r, start=True, stop=True)
                for t in range(2):
                    m = mm(ps[0:BS, 0, T:T + 1], SW[:, t, :], ones[:, 0:1], start=t == 0, stop=t == 1)
                m.then_inc(t_full, 1)

            def scatter(q, last=False):
                for t in range(2):
                    for half in range(2):
                        for i, part in enumerate((yhi, ylo)):
                            m = mm(ps[:, 4 + 2 * t + half, :], STr[0:BS, 1 - q, t * P:(t + 1) * P],
                                   part[0:BS, half * 512:(half + 1) * 512], start=False, stop=last and i == 1,
                                   skip_group_check=True)
                        if last:
                            m.then_inc(acc_full, 1)

            pe.wait_ge(tm_lo, 8)
            gather(0)
            pe.wait_ge(zero_ready, 1)
            turn_places(0)
            pe.wait_ge(count_ready, 2)
            pairs = pe.value_load(lint[0:1, NBLK:NBLK + 1], min_val=1, max_val=NBLK // 2 - 1)
            with pe.Fori(0, pairs) as tt_:
                for q in range(2):
                    b = 2 * tt_ + q
                    s0 = RB0 % RING + 3 * q
                    pe.wait_ge(hglo_ready, b + 1)
                    pe.wait_ge(t_out, b + 1)
                    for r in range(2):
                        pe.wait_ge(wlo_ready, 2 * b + r + 1)
                        w2 = [w.rearrange("p (k n) -> p k n", k=DC) for w in (whi[q][r][:, :], wlo[(s0 + r) % RING][:, :])]
                        for k in range(DC):
                            for i, (a, w) in enumerate(((hghi, w2[0]), (hghi, w2[1]), (hglo, w2[0]))):
                                m = mm(ps[0:BS, 0, r * T:(r + 1) * T], a[:, k, :], w[:, k, :],
                                       start=k + i == 0, stop=k == DC - 1 and i == 2)
                        m.then_inc(slot_done, 1)
                    gather(b + 1)
                    pe.wait_ge(ylo_ready, 2 * b + 2)
                    pe.wait_ge(blk_hid, b + 1)
                    pe.sem_inc(stepped, 1)
                    for f_ in range(2):
                        m = nc.tensor.transpose(ps[:, 2, f_ * BS:(f_ + 1) * BS], hidt[0:BS, f_ * P:(f_ + 1) * P], ident[0:BS, 0:BS])
                    m.then_inc(th_full, 1)
                    scatter(q)
                    turn_places(b + 1)
                    pe.wait_ge(wlo_down, b + 1)
                    pe.wait_ge(tlo_ready, b + 1)
                    w2 = [w.rearrange("p (f n) -> p f n", f=2) for w in (whi[q][2][:, :], wlo[(s0 + 2) % RING][:, :])]
                    for half in range(2):
                        o = slice(half * 512, (half + 1) * 512)
                        for f_ in range(2):
                            for i, (a, w) in enumerate(((hThi, w2[0]), (hThi, w2[1]), (hTlo, w2[0]))):
                                m = mm(ps[0:BS, 2 + half, :], a[:, f_, :], w[:, f_, o],
                                       start=f_ + i == 0, stop=f_ == 1 and i == 2)
                        m.then_inc(slot_done if half else d_half, 1)
            pe.wait_ge(ylo_ready, 4 * pairs + 2)
            scatter(0, last=True)
            pe.wait_ge(acc_out, 4)
            for k in range(DC):
                for t in range(2):
                    m = nc.tensor.transpose(ps[:, k // 2, (k % 2) * T + t * P:(k % 2) * T + (t + 1) * P],
                                            acc_sb[:, t, k * P:(k + 1) * P], ident)
                if k % 2:
                    m.then_inc(y_full, 1)

        @block.scalar
        def _(act):
            f = nc.scalar.activation

            def squares(l, which, need):
                for g in range(2):
                    W(act, "h_added", need(g), l)
                    f(sq[:, 4 * g:4 * g + 4, :], h[:, 4 * g:4 * g + 4, :], ACT.Square).then_inc(sq_ready, 1)

            def root_of_mean(l, which, eps):
                W(act, "norm_sum", which + 1, l)
                f(root[:, 0, :], ps[:, 7, 0:L], ACT.Sqrt, bias=eps, scale=1.0 / D).then_inc(norm_root, 1)

            act.wait_ge(loaded, LOADS)
            act.wait_ge(zeroed, 4)
            f(cs[:, :], small[:, 40:48], ACT.Silu).then_inc(cs_ready, 1)
            with act.Fori(0, DEPTH) as l:
                def slot_out(s):
                    act.wait_ge(slot_done, l * LAYER_SLOTS + s + 1)

                def chunk_out(i):
                    W(act, "even_full", i // 2 + 1, l) if i % 2 == 0 else slot_out(i // 2)

                squares(l, 0, lambda g: 1)
                root_of_mean(l, 0, small[:, 60:61])
                W(act, "lam_sum", 1, l)
                f(small[:, 2:4], ps[:, 6, 0:2], ACT.Exp).then_inc(lam_exp, 1)
                W(act, "par_ready", 1, l)
                for c in range(CC):
                    slot_out(c)
                    f(sgl[:, c, :], ps[:, 2 * (c % 2) + 1, 0:L], ACT.Sigmoid, bias=par[:, PBG + 4 + c:PBG + 5 + c])\
                        .then_inc(glu_sig, 1)
                for j in range(8):
                    chunk_out(8 + j)
                    f(raw[:, j, :], ps[:, j % 4, 0:L], ACT.Copy).then_inc(raw_ready, 1)
                for j in range(HEADS + 2):
                    if j < HEADS:
                        chunk_out(16 + j)
                        f(vT[:, j, :], ps[:, j % 4, 0:L], ACT.Copy).then_inc(vT_ready, 1)
                    if j >= 2:
                        i = j - 2
                        W(act, "vt_full", i + 1, l)
                        bank = ps[:, 6 + i % 2, 0:3 * P].rearrange("p (t e) -> p t e", t=3)
                        f(V[:, 0:2, i, :], bank[:, 0:2, :], ACT.Copy).then_inc(v_ready, 1)
                        f(V[0:META, 2, i, :], bank[0:META, 2, :], ACT.Copy).then_inc(v_ready, 1)
                W(act, "xc_ready", 1, l)
                f(lsq[:, :, :], xc[:, :, :], ACT.Square).then_inc(lsq_ready, 1)
                W(act, "var_sum", 1, l)
                f(root[:, 1, :], ps[:, 1, 0:L], ACT.Sqrt, bias=small[:, 60:61], scale=1.0 / (CC * P)).then_inc(var_root, 1)

                W(act, "xn_ready", 1, l)
                for c in range(CC):
                    g, b = par[:, PLG + c:PLG + c + 1], par[:, PLB + c:PLB + c + 1]
                    f(lnv[:, c, :], xc[:, c, :], ACT.Identity, bias=b, scale=g).then_inc(ln_act, 1)
                    f(lns[:, c, :], xc[:, c, :], ACT.Sigmoid, bias=b, scale=g).then_inc(ln_act, 1)

                def exps(u):
                    head, t = UNITS[u]
                    q0, rows = Q_TILES[t]
                    W(act, "smax", u + 1, l)
                    if u >= 2:
                        W(act, "a_ready", u - 1, l)
                    for c in range(2):
                        m = f(Pr[0:rows, u % 2, c, 0:q0 + rows], Sm[0:rows, u % 2, c, 0:q0 + rows], ACT.Exp,
                              bias=small[0:rows, 8 + 4 * (u % 2) + c:9 + 4 * (u % 2) + c], scale=HD ** -0.5,
                              accum_out=small[0:rows, 16 + 4 * (u % 2) + c:17 + 4 * (u % 2) + c])
                        m.then_inc(exp_done, 1)

                def copy_probs(u):
                    head, t = UNITS[u]
                    rows = Q_TILES[t][1]
                    W(act, "at_full", u + 1, l)
                    bank = ps[:, u % 2, 0:3 * P].rearrange("p (t q) -> p t q", t=3)
                    full = min(t + 1, 2)
                    m = f(aT[:, u % 2, 0:full, 0:rows], bank[:, 0:full, 0:rows], ACT.Copy)
                    if t == 2:
                        m.then_inc(at_part, 1)
                        m = f(aT[0:META, u % 2, 2, 0:rows], bank[0:META, 2, 0:rows], ACT.Copy)
                    m.then_inc(at_ready, 1)

                def copy_out(head):
                    W(act, "o_full", head + 1, l)
                    f(oraw[:, head, :], ps[:, 2 + head % 2, 0:L], ACT.Copy).then_inc(o_copied, 1)
                    f(mod[:, ds(l * 24 + 6 * head, 6)], ps[:, 2 + head % 2, L:L + 6], ACT.Copy).then_inc(o_copied, 1)
                    f(sq[:, head, :], ps[:, 2 + head % 2, 0:L], ACT.Square).then_inc(osq_ready, 1)

                for u in range(12):
                    exps(u)
                    if u >= 1:
                        copy_probs(u - 1)
                    if u >= 3 and u % 3 == 0:
                        copy_out(u // 3 - 1)
                copy_probs(11)
                copy_out(3)
                W(act, "sub_sum", 1, l)
                f(root[:, :, :], ps[:, 4:8, 0:L], ACT.Sqrt, bias=small[:, 60:61], scale=1.0 / P).then_inc(sub_root, 1)

                squares(l, 1, lambda g: 1 + 4 * g + 4)
                root_of_mean(l, 1, small[:, 60:61])

                def silu_gate(i, q, need):
                    act.wait_ge(slot_done, l * LAYER_SLOTS + OUT0 + OUT_SLOTS + 1 + i)
                    if need is not None:
                        W(act, "hff_ready", need, l)
                    f(sgu[:, q, :], ps[:, 2 * q, 0:L], ACT.Silu).then_inc(gate_act, 1)

                for i in range(2):
                    silu_gate(i, i, None)
                with act.Fori(1, FC // 2) as t:
                    for q in range(2):
                        silu_gate(t * 2 + q, q, t * 2 + q - 1)
            squares(DEPTH, 0, lambda g: 1)
            root_of_mean(DEPTH, 0, small[:, 60:61])
            e2 = small[:, 59:60]

            def token_squares(which, need):
                for g in range(2):
                    act.wait_ge(x_ready, need(g))
                    f(sqx[:, 4 * g:4 * g + 4, :], x[:, 4 * g:4 * g + 4, :], ACT.Square).then_inc(sq_ready, 1)
                W(act, "norm_sum", which + 1, DEPTH)
                f(root[:, 0, 0:T], ps[:, 7, 0:T], ACT.Sqrt, bias=e2, scale=1.0 / D).then_inc(norm_root, 1)

            def shift(which, col):
                for c in range(DC):
                    act.wait_ge(hm_scaled, DC * which + c + 1)
                    f(hm[:, c, :], hm[:, c, :], ACT.Identity, bias=mod[:, col + c:col + c + 1]).then_inc(hm_ready, 1)

            token_squares(1, lambda g: 4 * g + 4)
            act.dma_start(c2, consts2).then_inc(loaded2, 16)
            shift(0, 0)

            def landed(i):
                act.wait_ge(slot_done, B2 + i + 1)

            def head_root(j, scale):
                act.wait_ge(msum, j + 1)
                if j >= 2:
                    act.wait_ge(mnorm, j - 1)
                f(root2[:, j % 2, :], ps[:, 2, :], ACT.Sqrt, bias=e2, scale=scale).then_inc(mroot, 1)

            def turned_out(full, value, bank, dest, a0, done):
                act.wait_ge(full, value)
                src = ps[:, bank, :].rearrange("p (a t e) -> p a t e", a=2, t=2)
                f(dest[:, :, a0:a0 + 2, :].rearrange("p t a e -> p a t e"), src, ACT.Copy).then_inc(done, 1)

            for i in range(DIL_SLOTS):
                landed(i)
                if i < 12:
                    f(dqk[:, 2 * i:2 * i + 2, :].rearrange("p a b -> p (a b)"), ps[:, i % 2, :], ACT.Copy).then_inc(chain_a, 1)
                    f(sqd[:, i % 2, :], ps[:, i % 2, :], ACT.Square).then_inc(gemm_out, 1)
                else:
                    f(vst[:, i % 2].rearrange("p a b -> p (a b)"), ps[:, i % 2, :], ACT.Copy).then_inc(gemm_out, 1)
                if 1 <= i <= 12:
                    head_root(i - 1, 1.0 / P)
                if i >= 13:
                    turned_out(dv_full, i - 12, 4 + (i - 1) % 2, dV, 2 * (i - 13), dv_out)
            turned_out(dv_full, 6, 5, dV, 10, dv_out)
            act.wait_ge(ba_full, 1)
            CA = [12]

            def alink(ins):
                CA[0] += 1
                ins.then_inc(chain_a, 1)
                act.wait_ge(chain_a, CA[0])

            g8 = region(16512, 4, T)
            alink(f(g8[0:GH, 0, :], ps[0:GH, 3, 0:T], ACT.Sigmoid))
            alink(f(g8[0:GH, 1, :], ps[0:GH, 3, T:2 * T], ACT.Identity, bias=par2[0:GH, QDT:QDT + 1]))
            alink(f(g8[0:GH, 2, :], g8[0:GH, 1, :], ACT.Abs))
            alink(f(g8[0:GH, 3, :], g8[0:GH, 2, :], ACT.Exp, scale=-1.0))
            f(small[0:GH, 48:49], par2[0:GH, QAL:QAL + 1], ACT.Exp).then_inc(gate_a1, 1)

            def dil_exps(d):
                hs, t = divmod(d, 2)
                act.wait_ge(dmax, d + 1)
                o = 16 * (d % 2)
                for g in range(DG):
                    f(dS[:, d % 2, g, 0:(t + 1) * P], dS[:, d % 2, g, 0:(t + 1) * P], ACT.Exp, scale=P ** -0.5,
                      bias=tiny[:, o + g:o + g + 1], accum_out=tiny[:, o + 4 + g:o + 5 + g]).then_inc(dexp, 1)
                f(tiny[:, o + 8:o + 11], tiny[:, o:o + 3], ACT.Exp, scale=-1.0, bias=tiny[:, o + 3:o + 4]).then_inc(dexp, 1)

            def dil_probs_out(d):
                t = d % 2
                act.wait_ge(dtp, d + 1)
                src = flat[:, 6 * 512:6 * 512 + 768].rearrange("p (g k q) -> p g k q", g=3, k=2)
                dst = dpT[:, d % 2].rearrange("p (g k) q -> p g k q", g=3)
                f(dst[:, :, 0:t + 1, :], src[:, :, 0:t + 1, :], ACT.Copy).then_inc(dpt_ready, 1)

            def dil_y_out(d):
                hs, t = divmod(d, 2)
                act.wait_ge(do_full, d + 1)
                f(yb[:, hs, t * P:(t + 1) * P], ps[:, 6, 0:P], ACT.Copy).then_inc(yb_ready, 1)

            act.wait_ge(padded, 1)
            for n in range(14):
                if n < 12:
                    landed(DIL_SLOTS + n)
                    if n >= 2:
                        act.wait_ge(gconv, n - 1)
                    f(gpad[:, n % 2, :, 3:], ps[:, n % 2, :].rearrange("p (a b) -> p a b", a=2), ACT.Copy).then_inc(gemm_out, 1)
                if n < 8:
                    dil_exps(n)
                if 1 <= n <= 8:
                    head_root(12 + n - 1, 1.0)
                    dil_probs_out(n - 1)
                if 4 <= n - 2 < 12:
                    k = n - 2
                    turned_out(x_full, k - 3, 3, gK if k < 8 else gV, 2 * (k - 4 if k < 8 else k - 8), x_out)
                if n < 12:
                    act.wait_ge(gconv, n + 1)
                    dst = gq[:, 2 * n:2 * n + 2, :] if n < 4 else gk[:, 2 * n - 8:2 * n - 6, :] if n < 8 else vst[:, n % 2]
                    f(dst, gacc[:, n % 2], ACT.Silu).then_inc(gsilu, 1)
                    if n < 8:
                        act.wait_ge(gsilu, n + 1)
                        f(sqd[:, n % 2, :], dst.rearrange("p a b -> p (a b)"), ACT.Square).then_inc(gsq, 1)
                if 1 <= n <= 8:
                    dil_y_out(n - 1)

            act.wait_ge(gate_v1, 1)
            f(gt_[0:GH, 2, :], gt_[0:GH, 1, :], ACT.Ln).then_inc(gate_a2, 1)

            def z_out(j):
                landed(Z0 + j)
                f(zs[:, 2 * j:2 * j + 2, :].rearrange("p a b -> p (a b)"), ps[:, (Z0 + j) % 2, :], ACT.Silu)\
                    .then_inc(gemm_out, 1)

            z_out(0)
            act.wait_ge(gb_full, 1)
            f(GB[:, :, :].rearrange("p a b -> p (a b)"), flat[:, 4 * 512:8 * 512], ACT.Copy).then_inc(gb_out, 1)
            f(tiny[:, 32:64], ps[:, 3, 0:32], ACT.Copy).then_inc(gb_out, 1)
            for i in range(2):
                m = [MA, MB][i]
                act.wait_ge(d_built, 2 * (i + 1))
                f(m[:, :, :, :], m[:, :, :, :], ACT.Exp).then_inc(d_exp, 1)
            act.wait_ge(d_built, 5)
            f(tiny[:, 64:80], tiny[:, 32:48], ACT.Exp).then_inc(gcols, 1)
            f(tiny[:, 96:112], tiny[:, 80:96], ACT.Exp).then_inc(gcols, 1)
            f(GB[:, :, :], GB[:, :, :], ACT.Exp).then_inc(d_exp, 1)
            for m_ in range(24):
                act.wait_ge(wt_full, m_ + 1)
                if m_ >= 2:
                    act.wait_ge(tu_full, m_ - 1)
                f(Wts[:, m_ % 2].rearrange("p a b -> p (a b)"), ps[:, 2 + 3 * (m_ % 2), :], ACT.Copy).then_inc(wt_copied, 1)
                if m_ in (5, 11, 17):
                    z_out(1 + m_ // 6)
            for b in range(4):
                act.wait_ge(u_full, b + 1)
                f(MA[:, b // 2, 4 * (b % 2):4 * (b % 2) + 4, :].rearrange("p a b -> p (a b)"), ps[:, 2 + b, :], ACT.Copy)\
                    .then_inc(u_out, 1)

            def gate_out(j):
                landed(GATE0 + j)
                dst = (sga if j < 4 else sgb)[:, 2 * (j % 4):2 * (j % 4) + 2, :]
                f(dst.rearrange("p a b -> p (a b)"), ps[:, (GATE0 + j) % 2, :], ACT.Sigmoid).then_inc(gemm_out, 1)

            for c in range(4):
                gate_out(2 * c)
                act.wait_ge(oc_full, c + 1)
                f(yo[:, :, c * CHUNK:(c + 1) * CHUNK], ps[:, 4 + c % 2, :].rearrange("p (a b) -> p a b", a=GH), ACT.Copy)\
                    .then_inc(oc_out, 1)
                gate_out(2 * c + 1)
            act.dma_start(w_r, w_router_d).then_inc(loaded2, 16)
            act.dma_start(cst3, consts3_d).then_inc(loaded2, 16)
            act.wait_ge(oc_out, 4)
            act.wait_ge(vn_ready, 4)
            for b in range(4):
                f(MA_sq[:, b, :], yo[:, 2 * b:2 * b + 2, :].rearrange("p a b -> p (a b)"), ACT.Square).then_inc(ysq, 1)
            for b in range(4):
                act.wait_ge(ysum, b + 1)
                f(MB_rt[:, b, :], ps[:, 4 + b, :], ACT.Sqrt, bias=e2, scale=1.0 / P).then_inc(yroot, 1)
            token_squares(2, lambda g: 8 + 4 * g + 4)
            shift(1, 24)
            act.wait_ge(sc_full, 1)
            f(rt[:, 0, :], ps[:, 6, 0:P], ACT.Sigmoid).then_inc(sc_ready, 1)
            for g in range(4):
                act.wait_ge(tm_full, g + 1)
                f(h2p[0][:, g // 2, (g % 2) * 512:(g % 2 + 1) * 512], ps[:, (4, 7, 2, 3)[g], :], ACT.Copy).then_inc(tm_hi, 1)
            for g in range(4):
                act.wait_ge(tm_lo, g + 1)
                f(h2p[1][:, g // 2, (g % 2) * 512:(g % 2 + 1) * 512], h2r[:, g, :], ACT.Copy).then_inc(tm_hi, 1)
            act.wait_ge(slot_done, EX0 + 1)
            f(esil, ps[:, 0, :], ACT.Silu).then_inc(sh_silu, 1)
            act.wait_ge(ct_full, 1)
            f(combT[0:EXPERTS, :], ps[0:EXPERTS, 6, 0:T], ACT.Copy).then_inc(ct_out, 1)
            f(sel_T[0:EXPERTS, :], ps[0:EXPERTS, 6, T:2 * T], ACT.Copy).then_inc(ct_out, 1)

            def tokens_out():
                f(hghi[:, :, :].rearrange("p a b -> p (a b)"), ps[:, 1, :], ACT.Copy).then_inc(hg_ready, 1)

            def places_out(q):
                f(STr[0:BS, q, :], ps[0:BS, 0, 0:T], ACT.Copy)
                f(wsc[0:BS, q:q + 1], ps[0:BS, 0, T:T + 1], ACT.Copy).then_inc(t_out, 1)

            def split_weights(t, q, r):
                s = RB0 % RING + 3 * q + r
                act.wait_ge(ring_full[s % RING], (t + RB0 // RING + s // RING + 1) * 16)
                f(whi[q][r][:, :], ring[:, s % RING, :], ACT.Copy).then_inc(whi_ready, 1)

            act.wait_ge(g_full, 1)
            tokens_out()
            act.wait_ge(t_full, 1)
            places_out(0)
            for r in range(2):
                split_weights(0, 0, r)
            act.wait_ge(count_ready, 2)
            pairs = act.value_load(lint[0:1, NBLK:NBLK + 1], min_val=1, max_val=NBLK // 2 - 1)
            with act.Fori(0, pairs) as t:
                for q in range(2):
                    b = 2 * t + q
                    s0 = 6 * t + RB0 + 3 * q
                    n = (t, 1) if q == 0 else (t + 1, 0)
                    split_weights(*n, 0)
                    split_weights(t, q, 2)
                    act.wait_ge(slot_done, s0 + 2)
                    f(gsil[0:BS, :], ps[0:BS, 0, 0:T], ACT.Silu).then_inc(blk_silu, 1)
                    act.wait_ge(th_full, b + 1)
                    f(hThi[:, :, :].rearrange("p a b -> p (a b)"), ps[:, 2, 0:2 * BS], ACT.Copy).then_inc(thi_ready, 1)
                    tokens_out()
                    act.wait_ge(t_full, b + 2)
                    places_out(1 - q)
                    split_weights(*n, 1)
                    act.wait_ge(d_half, b + 1)
                    f(yhi[0:BS, 0:512], ps[0:BS, 2, :], ACT.Copy).then_inc(yhi_ready, 1)
                    act.wait_ge(slot_done, s0 + 3)
                    f(yhi[0:BS, 512:1024], ps[0:BS, 3, :], ACT.Copy).then_inc(yhi_ready, 1)
            for g in range(2):
                act.wait_ge(acc_full, g + 1)
                f(acc_sb[:, 0, g * 512:(g + 1) * 512], ps[:, 4 + g, :], ACT.Copy).then_inc(acc_out, 1)

        @block.vector
        def _(dve):
            v = nc.vector

            class Chain:
                base, n = 0, 0

            def link(ins):
                Chain.n += 1
                ins.then_inc(chain_v, 1)
                dve.wait_ge(chain_v, Chain.base + Chain.n)

            v.memset(small[:, 59:60], EPS2).then_inc(zeroed, 1)
            v.memset(small[:, 60:61], EPS1).then_inc(zeroed, 1)
            v.memset(zpad[:, :, 0:PAD], 0.0).then_inc(zeroed, 1)
            dve.wait_ge(zeroed, 3)
            v.memset(small[:, 61:62], -1.0).then_inc(zeroed, 1)
            dve.wait_ge(zeroed, 4)
            v.memset(small[:, 62:63], -1.0).then_inc(h_added, 1)
            dve.wait_ge(loaded, LOADS)

            def normalize(l, which, gains):
                W(dve, "norm_root", which + 1, l)
                link(v.reciprocal(inv[:, 0, :], root[:, 0, :]))
                for c in range(DC):
                    v.scalar_tensor_tensor(hn[:, c, :], h[:, c, :], gains[:, c:c + 1], inv[:, 0, :],
                                           ALU.mult, ALU.mult).then_inc(hn_ready, 1)

            CHAIN = 186
            with dve.Fori(0, DEPTH) as l:
                Chain.base, Chain.n = l * CHAIN, 0
                dve.wait_ge(h_added, l * COUNT["h_added"] + 1)
                v.tensor_copy(par[:, :], par_all[:, ds(l, 1), :].rearrange("p a n -> p (a n)")).then_inc(par_ready, 1)
                W(dve, "par_ready", 1, l)
                v.tensor_tensor(small[0:HD, 0:2], par[0:HD, PLAM:PLAM + 4:2], par[0:HD, PLAM + 1:PLAM + 4:2], ALU.mult)\
                    .then_inc(lam_prod, 1)
                normalize(l, 0, par[:, PN1:PN1 + DC])

                taps = [(c, k) for c in range(CC) for k in range(TAPS)]

                def convolve(n):
                    for _ in range(min(n, len(taps))):
                        c, k = taps.pop(0)
                        z, g = zpad[:, c, k:k + L], par[:, PCW + c * TAPS + k:PCW + c * TAPS + k + 1]
                        if k == 0:
                            link(v.tensor_scalar(conv[:, c, :], z, g, par[:, PCB + c:PCB + c + 1], ALU.mult, ALU.add))
                        elif taps:
                            link(v.scalar_tensor_tensor(conv[:, c, :], z, g, conv[:, c, :], ALU.mult, ALU.add))
                        else:
                            v.scalar_tensor_tensor(conv[:, c, :], z, g, conv[:, c, :], ALU.mult, ALU.add)\
                                .then_inc(conv_ready, 1)

                for c in range(CC):
                    W(dve, "glu_sig", c + 1, l)
                    v.scalar_tensor_tensor(zpad[:, c, PAD:], ps[:, 2 * (c % 2), 0:L], par[:, PBG + c:PBG + c + 1],
                                           sgl[:, c, :], ALU.add, ALU.mult).then_inc(glu_done, 1)
                    W(dve, "glu_done", c + 1, l)
                    convolve(20)
                for j in range(8):
                    W(dve, "raw_ready", j + 1, l)
                    link(v.tensor_tensor(rt1[:, j % 2, :], raw[:, j, :], cos, ALU.mult))
                    W(dve, "rot_full", j + 1, l)
                    v.tensor_tensor(rt2[:, j % 2, :], ps[:, 4 + j % 2, 0:L], sin, ALU.mult).then_inc(rot_used, 1)
                    W(dve, "rot_used", j + 1, l)
                    v.tensor_tensor(qk[:, j, :], rt1[:, j % 2, :], rt2[:, j % 2, :], ALU.add).then_inc(qk_ready, 1)
                    convolve(6)
                assert not taps
                W(dve, "lam_exp", 1, l)
                link(v.tensor_tensor(small[:, 4:5], small[:, 3:4], small[:, 2:3], ALU.subtract))
                link(v.tensor_tensor(small[:, 5:6], small[:, 4:5], par[:, PLI:PLI + 1], ALU.subtract))
                link(v.tensor_tensor(small[:, 6:7], par[:, PSG:PSG + 1], par[:, PLO:PLO + 1], ALU.mult))
                W(dve, "mu_sum", 1, l)
                for c in range(CC):
                    m = v.scalar_tensor_tensor(xc[:, c, :], ps[:, 0, 0:L], -1.0 / (CC * P), conv[:, c, :], ALU.mult, ALU.add)
                m.then_inc(xc_ready, 1)

                def mask_max(u):
                    head, t = UNITS[u]
                    q0, rows = Q_TILES[t]
                    keys = q0 + rows
                    W(dve, "s_full", u + 1, l)
                    if u >= 2:
                        W(dve, "exp_done", 2 * (u - 1), l)
                    b = 4 + 2 * (u % 2)
                    m = causal[0:rows, t:t + 1, 0:keys].to_broadcast([rows, 2, keys])
                    v.tensor_tensor(Sm[0:rows, u % 2, :, 0:keys], ps[0:rows, b:b + 2, 0:keys], m, ALU.add)\
                        .then_inc(s_masked, 1)
                    W(dve, "s_masked", u + 1, l)
                    mx = small[0:rows, 24 + 4 * (u % 2):26 + 4 * (u % 2)]
                    link(v.tensor_reduce(mx, Sm[0:rows, u % 2, :, 0:keys], AX_X, ALU.max))
                    v.tensor_scalar(small[0:rows, 8 + 4 * (u % 2):10 + 4 * (u % 2)], mx, -HD ** -0.5, None, ALU.mult)\
                        .then_inc(smax, 1)

                def difference(u):
                    head, t = UNITS[u]
                    q0, rows = Q_TILES[t]
                    keys = q0 + rows
                    W(dve, "exp_done", 2 * (u + 1), l)
                    o = 32 + 4 * (u % 2)
                    link(v.reciprocal(small[0:rows, o:o + 2], small[0:rows, 16 + 4 * (u % 2):18 + 4 * (u % 2)]))
                    link(v.tensor_tensor(small[0:rows, o + 2:o + 3], small[0:rows, o + 1:o + 2], small[0:rows, 5:6], ALU.mult))
                    link(v.tensor_scalar(Pt[0:rows, u % 2, 0:keys], Pr[0:rows, u % 2, 1, 0:keys],
                                         small[0:rows, o + 2:o + 3], None, ALU.mult))
                    if u >= 2:
                        W(dve, "at_full", u - 1, l)
                    v.scalar_tensor_tensor(A[0:rows, u % 2, 0:keys], Pr[0:rows, u % 2, 0, 0:keys], small[0:rows, o:o + 1],
                                           Pt[0:rows, u % 2, 0:keys], ALU.mult, ALU.add).then_inc(a_ready, 1)

                mask_max(0)
                mask_max(1)
                W(dve, "var_root", 1, l)
                link(v.reciprocal(inv[:, 1, :], root[:, 1, :]))
                v.tensor_tensor(xc[:, :, :], xc[:, :, :], inv[:, 1:2, :].to_broadcast([P, CC, L]), ALU.mult)\
                    .then_inc(xn_ready, 1)
                for u in range(12):
                    difference(u)
                    if u + 2 < 12:
                        mask_max(u + 2)
                W(dve, "sub_root", 1, l)
                link(v.reciprocal(inv[:, :, :], root[:, :, :]))
                for head in range(HEADS):
                    v.scalar_tensor_tensor(cat[:, head, :], oraw[:, head, :], small[:, 6:7], inv[:, head, :],
                                           ALU.mult, ALU.mult).then_inc(attn_out, 1)
                for n in range(DC):
                    if n % 2 == 0:
                        W(dve, "even_full", IN_SLOTS + n // 2 + 1, l)
                    else:
                        dve.wait_ge(slot_done, l * LAYER_SLOTS + OUT0 + n // 2 + 1)
                    v.tensor_tensor(h[:, n, :], h[:, n, :], ps[:, n % 4, 0:L], ALU.add).then_inc(h_added, 1)
                W(dve, "h_added", 1 + DC, l)
                normalize(l, 1, par[:, PN2:PN2 + DC])
                with dve.Fori(0, FC // 2) as t:
                    for q in range(2):
                        W(dve, "gate_act", t * 2 + q + 1, l)
                        v.tensor_tensor(hff[:, ds(t * 2 + q, 1), :].rearrange("p a n -> p (a n)"), sgu[:, q, :],
                                        ps[:, 2 * q + 1, 0:L], ALU.mult).then_inc(hff_ready, 1)
                for half in range(2):
                    dve.wait_ge(slot_done, l * LAYER_SLOTS + OUT0 + OUT_SLOTS + GU_SLOTS + 6 * half + 6)
                    for n in range(4):
                        v.tensor_tensor(h[:, 4 * half + n, :], h[:, 4 * half + n, :], ps[:, 4 - 4 * half + n, 0:L], ALU.add)\
                            .then_inc(h_added, 1)
                assert Chain.n == CHAIN, Chain.n
            Chain.base, Chain.n = DEPTH * CHAIN, 0
            dve.wait_ge(h_added, DEPTH * COUNT["h_added"] + 1)
            W(dve, "norm_root", 1, DEPTH)
            link(v.reciprocal(inv[:, 0, :], root[:, 0, :]))
            for c in range(DC):
                v.scalar_tensor_tensor(h[:, c, :], h[:, c, :], fin_g[:, c:c + 1], inv[:, 0, :],
                                       ALU.mult, ALU.mult).then_inc(x_ready, 1)
            W(dve, "o_copied", 0, DEPTH)
            link(v.tensor_tensor(mod[:, :], mod[:, :], par2[:, QADA:QADA + 48], ALU.add))
            for o, g in ((0, QMIX), (24, QFFN)):
                link(v.scalar_tensor_tensor(mod[:, o + 8:o + 16], mod[:, o + 8:o + 16], 1.0, par2[:, g:g + DC],
                                            ALU.add, ALU.mult))

            def scale_tokens(which, col):
                W(dve, "norm_root", which + 1, DEPTH)
                link(v.reciprocal(inv[:, 0, 0:T], root[:, 0, 0:T]))
                for c in range(DC):
                    v.scalar_tensor_tensor(hm[:, c, :], x[:, c, :], mod[:, col + c:col + c + 1], inv[:, 0, 0:T],
                                           ALU.mult, ALU.mult).then_inc(hm_scaled, 1)

            dve.wait_ge(x_ready, 8)
            scale_tokens(1, 8)

            def head_norm(j, dst, gain):
                dve.wait_ge(mroot, j + 1)
                link(v.reciprocal(inv2[:, j % 2, :], root2[:, j % 2, :]))
                d = dst.rearrange("p a b -> p (a b)")
                v.scalar_tensor_tensor(d, d, gain, inv2[:, j % 2, :], ALU.mult, ALU.mult).then_inc(mnorm, 1)

            for i in range(12):
                g = QDQ if i < 6 else QDK
                head_norm(i, dqk[:, 2 * i:2 * i + 2, :], par2[:, g:g + 1])
            v.memset(gpad[:, :, :, 0:3], 0.0).then_inc(padded, 1)
            dve.wait_ge(loaded2, 16)

            def dil_mask(d):
                hs, t = divmod(d, 2)
                keys = (t + 1) * P
                o = 16 * (d % 2)
                dve.wait_ge(ds_full, d + 1)
                if d >= 2:
                    dve.wait_ge(dtp, d - 1)
                src = flat[:, 4 * 512:4 * 512 + 768].rearrange("p (g k) -> p g k", g=3)[:, :, 0:keys]
                k0 = (KD0, KD1)[t]
                mask = c2[:, k0:k0 + 3 * keys].rearrange("p (g k) -> p g k", g=3)
                s_ = dS[:, d % 2, :, 0:keys]
                v.tensor_tensor(s_, src, mask, ALU.add).then_inc(dmask, 1)
                dve.wait_ge(dmask, d + 1)
                link(v.tensor_reduce(tiny[:, o + 12:o + 15], s_, AX_X, ALU.max))
                link(v.tensor_scalar(tiny[:, o:o + 3], tiny[:, o + 12:o + 15], -P ** -0.5, None, ALU.mult))
                v.tensor_reduce(tiny[:, o + 3:o + 4], tiny[:, o:o + 3], AX_X, ALU.min).then_inc(dmax, 1)

            def dil_weights(d):
                hs, t = divmod(d, 2)
                keys = (t + 1) * P
                o, q = 16 * (d % 2), 112 + 16 * (d % 2)
                dve.wait_ge(dexp, 4 * (d + 1))
                link(v.tensor_tensor(tiny[:, q:q + 3], tiny[:, o + 4:o + 7], tiny[:, o + 8:o + 11], ALU.mult))
                link(v.tensor_reduce(tiny[:, q + 3:q + 4], tiny[:, q:q + 3], AX_X, ALU.add))
                link(v.reciprocal(tiny[:, q + 4:q + 5], tiny[:, q + 3:q + 4]))
                link(v.tensor_scalar(tiny[:, q + 8:q + 11], tiny[:, o + 8:o + 11], tiny[:, q + 4:q + 5], None, ALU.mult))
                s_ = dS[:, d % 2, :, 0:keys]
                c_ = tiny[:, q + 8:q + 11].rearrange("p (g a) -> p g a", a=1).to_broadcast([P, 3, keys])
                v.tensor_tensor(s_, s_, c_, ALU.mult).then_inc(dcoef, 1)

            def short_conv(n):
                dve.wait_ge(gemm_out, DIL_SLOTS + n + 1)
                if n >= 2:
                    dve.wait_ge(gsilu, n - 1)
                for k in range(4):
                    for a in range(2):
                        w = par2[:, QCW + 4 * (2 * n + a) + k:QCW + 4 * (2 * n + a) + k + 1]
                        z, y = gpad[:, n % 2, a, k:k + T], gacc[:, n % 2, a, :]
                        if k == 0:
                            m = v.tensor_scalar(y, z, w, None, ALU.mult)
                        else:
                            m = v.scalar_tensor_tensor(y, z, w, y, ALU.mult, ALU.add)
                        if k < 3:
                            m.then_inc(chain_v, 1)
                            Chain.n += 1
                            if a == 1:
                                dve.wait_ge(chain_v, Chain.base + Chain.n)
                m.then_inc(gconv, 1)

            for n in range(12):
                if n < 8:
                    dil_mask(n)
                short_conv(n)
                if n < 8:
                    dil_weights(n)
                if 1 <= n <= 8:
                    k = n - 1
                    dst = gq[:, 2 * k:2 * k + 2, :] if k < 4 else gk[:, 2 * k - 8:2 * k - 6, :]
                    head_norm(12 + k, dst, P ** -0.5 if k < 4 else 1.0)

            g8 = region(16512, 4, T)
            dve.wait_ge(gate_a1, 1)
            dve.wait_ge(yb_ready, 8)
            R = lambda i: gt_[0:GH, i, :]
            v.tensor_scalar(R(1), g8[0:GH, 3, :], 1.0, None, ALU.add).then_inc(gate_v1, 1)
            dve.wait_ge(gate_v1, 1)
            link(v.tensor_copy(R(0), g8[0:GH, 0, :]))
            link(v.tensor_scalar(R(3), R(1), -1.0, None, ALU.add))
            link(v.tensor_tensor(R(3), g8[0:GH, 3, :], R(3), ALU.subtract))
            link(v.reciprocal(R(4), R(1)))
            link(v.tensor_tensor(R(3), R(3), R(4), ALU.mult))
            link(v.tensor_scalar(R(4), g8[0:GH, 1, :], 0.0, None, ALU.max))
            link(v.tensor_tensor(R(3), R(3), R(4), ALU.add))
            dve.wait_ge(gate_a2, 1)
            link(v.tensor_tensor(R(3), R(3), R(2), ALU.add))
            link(v.tensor_scalar(R(4), R(3), small[0:GH, 48:49], -1.0, ALU.mult, ALU.mult))
            for c in range(4):
                cc = slice(c * CHUNK, (c + 1) * CHUNK)
                link(v.tensor_tensor_scan(gt_[0:GH, 5, cc], ones[0:GH, 0:CHUNK], gt_[0:GH, 4, cc], 0.0, ALU.mult, ALU.add))
            v.tensor_tensor(gdiag[0:GH, :, :], gt_[0:GH, 5:6, :].to_broadcast([GH, GH, T]),
                            ident[0:GH, 0:GH].rearrange("p (a b) -> p a b", b=1).to_broadcast([GH, GH, T]), ALU.mult)\
                .then_inc(gdiag_ready, 1)
            dve.wait_ge(gb_out, 2)
            low = c2[:, KLOW:KLOW + P].rearrange("p (a b) -> p a b", a=1).to_broadcast([P, GH, P])
            up = c2[:, KUP:KUP + P].rearrange("p (a b) -> p a b", a=1).to_broadcast([P, GH, P])

            def col(o, p):
                return tiny[:, o + GH * p:o + GH * p + GH].rearrange("p (a b) -> p a b", b=1).to_broadcast([P, GH, P])

            for p in range(2):
                link(v.tensor_tensor(MA[:, p], low, GB[:, :, p * P:(p + 1) * P], ALU.subtract))
            for p in range(2):
                v.tensor_tensor(MA[:, p], MA[:, p], col(32, p), ALU.add).then_inc(d_built, 1)
            for p in range(2):
                link(v.tensor_tensor(MB[:, p], up, GB[:, :, p * P:(p + 1) * P], ALU.add))
            for p in range(2):
                v.tensor_tensor(MB[:, p], MB[:, p], col(32, p), ALU.subtract).then_inc(d_built, 1)
            for p in range(2):
                for hf in range(2):
                    r = slice(64 * hf, 64 * hf + 64)
                    last = p * P + 64 * hf + 63
                    m = v.tensor_tensor(tiny[r, 80 + GH * p:88 + GH * p], GB[r, :, last:last + 1].rearrange("p a b -> p (a b)"),
                                        tiny[r, 32 + GH * p:40 + GH * p], ALU.subtract)
            m.then_inc(d_built, 1)
            dve.wait_ge(d_exp, 1)
            for b in range(4):
                dve.wait_ge(kk_full, b + 1)
                for i in range(4):
                    p, hh = b // 2, 4 * (b % 2) + i
                    m = v.scalar_tensor_tensor(MA[:, p, hh, :], ps[:, 4 + b, i * P:(i + 1) * P],
                                               tiny[:, 48 + GH * p + hh:49 + GH * p + hh], MA[:, p, hh, :], ALU.mult, ALU.mult)
                m.then_inc(l_ready, 1)
            dve.wait_ge(d_exp, 2)
            for b in range(4):
                dve.wait_ge(qk_full, b + 1)
                d = MB[:, b // 2, 4 * (b % 2):4 * (b % 2) + 4, :].rearrange("p a b -> p (a b)")
                v.tensor_tensor(d, ps[:, 4 + b, :], d, ALU.mult).then_inc(qkt_ready, 1)
            for m in (MT, MU):
                idb = ident.rearrange("p (a b) -> p a b", a=1).to_broadcast([P, 2 * GH, P])
                v.tensor_copy(m[:, :, :, :].rearrange("p a b c -> p (a b) c"), idb).then_inc(tu_init, 1)
            dve.wait_ge(tu_init, 2)
            dve.wait_ge(gcols, 2)
            link(v.tensor_tensor(tiny[:, 144:160], tiny[:, 48:64], tiny[:, 64:80], ALU.mult))
            dve.wait_ge(d_exp, 3)
            v.tensor_copy(tiny[:, 160:192].rearrange("p (c h) -> p h c", c=4), GB[:, :, 63:T:64]).then_inc(gtot_ready, 1)
            for m_ in range(24):
                b = m_ % 4
                dve.wait_ge(tu_full, m_ + 1)
                for o, mat in ((3, MT), (4, MU)):
                    d = mat[:, b // 2, 4 * (b % 2):4 * (b % 2) + 4, :].rearrange("p a b -> p (a b)")
                    m = v.tensor_tensor(d, d, ps[:, o + 3 * (m_ % 2), :], ALU.subtract)
                m.then_inc(tu_done, 1)
                if m_ < 20:
                    dve.wait_ge(tu_done, max(m_ - 2, 1))
            v.memset(St[:, :, :], 0.0).then_inc(s_ready, 1)
            dve.wait_ge(pool_scaled, 4)
            for b in range(4):
                dve.wait_ge(w_full, b + 1)
                v.tensor_copy(WT[:, b // 2, 4 * (b % 2):4 * (b % 2) + 4, :].rearrange("p a b -> p (a b)"),
                              ps[:, (6, 7, 2, 3)[b], :]).then_inc(w_out, 1)
            dve.wait_ge(u_out, 4)
            for c in range(4):
                p, r = c // 2, slice(CHUNK * (c % 2), CHUNK * (c % 2) + CHUNK)
                dve.wait_ge(vn_full, c + 1)
                v.tensor_tensor(vn[r, :, :].rearrange("p a b -> p (a b)"), MA[r, p, :, :].rearrange("p a b -> p (a b)"),
                                flat[r, 1024:2048], ALU.subtract).then_inc(vn_ready, 1)
                if c < 3:
                    dve.wait_ge(su_full, c + 1)
                    dve.wait_ge(s_ready, c + 1)
                    for hh in range(GH):
                        m = v.scalar_tensor_tensor(St[:, hh, :], St[:, hh, :], tiny[:, 160 + 8 * c + hh:161 + 8 * c + hh],
                                                   ps[:, 6 + hh // 4, (hh % 4) * P:(hh % 4 + 1) * P], ALU.mult, ALU.add)
                    m.then_inc(s_ready, 1)
            for b in range(4):
                dve.wait_ge(yroot, b + 1)
                link(v.reciprocal(MB_rt[:, b, :], MB_rt[:, b, :]))
                y = yo[:, 2 * b:2 * b + 2, :].rearrange("p a b -> p (a b)")
                link(v.scalar_tensor_tensor(y, y, par2[:, QGN:QGN + 1], MB_rt[:, b, :], ALU.mult, ALU.mult))
                v.tensor_tensor(y, y, zs[:, 2 * b:2 * b + 2, :].rearrange("p a b -> p (a b)"), ALU.mult).then_inc(ya_ready, 1)
            for m_ in range(2):
                dve.wait_ge(slot_done, B2 + UP0 + m_ + 1)
                d = sgb[:, 4 * m_:4 * m_ + 4, :].rearrange("p a b -> p (a b)")
                v.tensor_tensor(d, d, flat[:, 1024 * m_:1024 * m_ + 1024], ALU.mult).then_inc(up_out, 1)
            dve.wait_ge(up_out, 2)
            for j in range(4):
                dve.wait_ge(slot_done, B2 + UP0 + 2 + j + 1)
                d = sga[:, 2 * j:2 * j + 2, :].rearrange("p a b -> p (a b)")
                link(v.tensor_tensor(d, d, ps[:, 4 + j, :], ALU.mult))
                v.tensor_tensor(d, d, sgb[:, 2 * j:2 * j + 2, :].rearrange("p a b -> p (a b)"), ALU.add).then_inc(merged, 1)
            for j in range(4):
                dve.wait_ge(slot_done, B2 + OUT2 + j + 1)
                for n in range(2):
                    c = 2 * j + n
                    v.scalar_tensor_tensor(x[:, c, :], ps[:, j, n * T:(n + 1) * T], mod[:, 16 + c:17 + c], x[:, c, :],
                                           ALU.mult, ALU.add).then_inc(x_ready, 1)
            dve.wait_ge(x_ready, 16)
            scale_tokens(2, 32)

            sc = rt[:, 0, :].rearrange("p (t e) -> p t e", t=2)
            sel = rt[:, 1, :].rearrange("p (t e) -> p t e", t=2)
            bias = par2[:, QRB:QRB + EXPERTS].rearrange("p (a b) -> p a b", a=1).to_broadcast([P, 2, EXPERTS])
            v.memset(yhi[0:BS, :].bitcast(F32), 0.0)
            v.memset(ylo[0:BS, :].bitcast(F32), 0.0)
            v.memset(STr[0:BS, 1, :].bitcast(F32), 0.0)
            v.tensor_copy(ident_r, ident).then_inc(zero_ready, 1)
            dve.wait_ge(sc_ready, 1)
            link(v.tensor_tensor(sel, sc, bias, ALU.add))
            for t in range(2):
                for g in range(GROUPS):
                    m = v.max(rt[:, 2, 64 * t + 8 * g:64 * t + 8 * g + 8], rt[:, 1, 64 * t + 8 * g:64 * t + 8 * g + 8])
                link(m)
            top2 = rt[:, 2, :].rearrange("p (t g e) -> p t g e", t=2, g=GROUPS)
            gs = rt[:, 3, 0:16].rearrange("p (t g) -> p t g", t=2)
            link(v.tensor_tensor(gs, top2[:, :, :, 0], top2[:, :, :, 1], ALU.add))
            for t in range(2):
                a = rt[:, 3, 8 * t:8 * t + 8].rearrange("p (a b) -> p a b", a=1).to_broadcast([P, 8, 8])
                b = rt[:, 3, 8 * t:8 * t + 8].rearrange("p (a b) -> p a b", b=1).to_broadcast([P, 8, 8])
                gt8 = rt[:, 4, 64 * t:64 * t + 64].rearrange("p (a b) -> p a b", a=8)
                eq8 = rt[:, 5, 64 * t:64 * t + 64].rearrange("p (a b) -> p a b", a=8)
                link(v.tensor_tensor(gt8, a, b, ALU.is_gt))
                link(v.tensor_tensor(eq8, a, b, ALU.is_equal))
                link(v.tensor_tensor(eq8, eq8, cst[:, o_tie:o_tie + 64].rearrange("p (a b) -> p a b", a=8), ALU.mult))
                link(v.tensor_tensor(gt8, gt8, eq8, ALU.add))
                link(v.tensor_reduce(rt[:, 3, 16 + 8 * t:24 + 8 * t], gt8, AX_X, ALU.add))
            link(v.tensor_scalar(rt[:, 3, 32:48], rt[:, 3, 16:32], TOP_GROUPS - 0.5, None, ALU.is_lt))
            link(v.tensor_scalar(rt[:, 3, 48:64], rt[:, 3, 32:48], -NEG, NEG, ALU.mult, ALU.add))
            keep = [rt[:, 3, o:o + 16].rearrange("p (g b) -> p g b", b=1).to_broadcast([P, 16, 8]) for o in (32, 48)]
            s16 = rt[:, 1, :].rearrange("p (g e) -> p g e", g=16)
            link(v.tensor_tensor(s16, s16, keep[0], ALU.mult))
            link(v.tensor_tensor(s16, s16, keep[1], ALU.add))
            for t in range(2):
                s_ = rt[:, 1, 64 * t:64 * t + 64]
                link(v.max(rt[:, 6, 8 * t:8 * t + 8], s_))
                link(v.match_replace(rt[:, 7, 64 * t:64 * t + 64], rt[:, 6, 8 * t:8 * t + 8], s_, -3e38))
                link(v.tensor_scalar(rt[:, 7, 64 * t:64 * t + 64], rt[:, 7, 64 * t:64 * t + 64], -2e38, None, ALU.is_lt))
                v.tensor_copy(rt[:, 10, 64 * t:64 * t + 64], rt[:, 7, 64 * t:64 * t + 64])
                link(v.tensor_tensor(rt[:, 7, 64 * t:64 * t + 64], rt[:, 7, 64 * t:64 * t + 64], rt[:, 0, 64 * t:64 * t + 64], ALU.mult))
                link(v.tensor_reduce(rt[:, 6, 32 + t:33 + t], rt[:, 7, 64 * t:64 * t + 64], AX_X, ALU.add))
                link(v.reciprocal(rt[:, 6, 34 + t:35 + t], rt[:, 6, 32 + t:33 + t]))
                v.tensor_scalar(rt[:, 8 + t, 0:EXPERTS], rt[:, 7, 64 * t:64 * t + 64], rt[:, 6, 34 + t:35 + t], ROUTE_SCALE,
                                ALU.mult, ALU.mult).then_inc(comb_ready, 1)

            for g in range(4):
                dve.wait_ge(tm_hi, g + 1)
                o = slice((g % 2) * 512, (g % 2 + 1) * 512)
                v.tensor_tensor(h2r[:, g, :], ps[:, (4, 7, 2, 3)[g], :], h2p[0][:, g // 2, o], ALU.subtract).then_inc(tm_lo, 1)
            for g in range(4):
                dve.wait_ge(tm_hi, 4 + g + 1)
                o = slice((g % 2) * 512, (g % 2 + 1) * 512)
                v.tensor_tensor(h2p[2][:, g // 2, o], h2r[:, g, :], h2p[1][:, g // 2, o], ALU.subtract).then_inc(tm_lo, 1)
            dve.wait_ge(slot_done, EX0 + 2)
            dve.wait_ge(sh_silu, 1)
            v.tensor_tensor(hid[:, :, :].rearrange("p a b -> p (a b)"), esil, ps[:, 1, :], ALU.mult).then_inc(zero_ready, 1)
            X = slice(0, EXPERTS)
            dve.wait_ge(ct_out, 2)
            link(v.tensor_reduce(nE[X, 0:1], sel_T[X, :], AX_X, ALU.add))
            link(v.tensor_scalar(thr_hit[X, 0:4], cst3[X, KTHR:KTHR + 4], nE[X, 0:1], None, ALU.is_lt))
            v.tensor_reduce(nblk[X, 0:1], thr_hit[X, 0:4], AX_X, ALU.add).then_inc(route_ready, 1)
            dve.wait_ge(route_ready, 1)
            dve.wait_ge(route_full, 1)
            link(v.tensor_copy(base[X, 0:1], ps[X, 2, 0:1]))
            link(v.tensor_tensor(end[X, 0:1], base[X, 0:1], nblk[X, 0:1], ALU.add))
            link(v.tensor_scalar(cpos[X, 0:1], base[X, 0:1], float(BS), float(FAR), ALU.mult, ALU.add))
            link(v.tensor_scalar(E1[X, :], cst3[X, KB:KB + NBLK], base[X, 0:1], None, ALU.is_ge))
            link(v.scalar_tensor_tensor(E[X, :], cst3[X, KB:KB + NBLK], end[X, 0:1], E1[X, :], ALU.is_lt, ALU.mult))
            v.scalar_tensor_tensor(posT[X, :], ps[X, 3, 0:T], cpos[X, 0:1], sel_T[X, :], ALU.add, ALU.mult).then_inc(route_ready, 1)
            dve.wait_ge(route_full, 2)
            v.tensor_scalar(lint[0:1, 0:NBLK], ps[0:1, 3, 4 * NBLK:5 * NBLK], float(RB0), None, ALU.add).then_inc(count_ready, 1)
            link(v.tensor_reduce(pair_n[0:1, :], ps[0:1, 2, 0:NBLK:2], AX_X, ALU.add))
            v.tensor_copy(lint[0:1, NBLK:NBLK + 1], pair_n[0:1, :]).then_inc(count_ready, 1)
            far = cst3[:, KFAR:KFAR + NBLK].rearrange("p (a b) -> p a b", a=1).to_broadcast([P, 2, NBLK])
            v.tensor_tensor(Pb[:, :, :], ps[:, 3, 0:2 * NBLK].rearrange("p (a b) -> p a b", a=2), far, ALU.subtract)
            link(v.tensor_copy(Wb[:, :, :], ps[:, 3, 2 * NBLK:4 * NBLK].rearrange("p (a b) -> p a b", a=2)))

            def places(b):
                c = slice(b, b + 1) if isinstance(b, int) else ds(b, 1)
                for t in range(2):
                    v.tensor_scalar(Sr[:, t, :], cst3[:, KSLOT:KSLOT + BS], Pb[:, t, c], None, ALU.is_equal)
                for t in range(2):
                    m = v.tensor_scalar(SW[:, t, :], cst3[:, KSLOT:KSLOT + BS], Pb[:, t, c], Wb[:, t, c],
                                        ALU.is_equal, ALU.mult)
                m.then_inc(place_ready, 1)

            def rest_of_weights(b, q, r):
                dve.wait_ge(whi_ready, r + 1 if isinstance(b, int) else 3 * b + 2 * r)
                j = (RB0 + 3 * q + r) % RING
                v.tensor_tensor(wlo[j][:, :], ring[:, j, :], whi[q][r][:, :], ALU.subtract).then_inc(wlo_ready, 1)

            def rest_of_tokens(b):
                dve.wait_ge(hg_ready, b + 1)
                v.tensor_tensor(hglo[:, :, :].rearrange("p a b -> p (a b)"), ps[:, 1, :], hghi[:, :, :].rearrange("p a b -> p (a b)"),
                                ALU.subtract).then_inc(hglo_ready, 1)

            places(0)
            rest_of_tokens(0)
            for r in range(2):
                rest_of_weights(0, 0, r)
            dve.wait_ge(t_full, 1)
            places(1)
            v.memset(rt[0:1, 15, 0:8], 0.0).then_inc(ylo_ready, 2)
            dve.wait_ge(count_ready, 2)
            pairs = dve.value_load(lint[0:1, NBLK:NBLK + 1], min_val=1, max_val=NBLK // 2 - 1)
            with dve.Fori(0, pairs) as t:
                for q in range(2):
                    b = 2 * t + q
                    rest_of_weights(b + 1, 1 - q, 0)
                    dve.wait_ge(blk_silu, b + 1)
                    v.scalar_tensor_tensor(hidt[0:BS, :], gsil[0:BS, :], wsc[0:BS, q:q + 1], ps[0:BS, 0, T:2 * T],
                                           ALU.mult, ALU.mult).then_inc(blk_hid, 1)
                    dve.wait_ge(thi_ready, b + 1)
                    v.tensor_tensor(hTlo[:, :, :].rearrange("p a b -> p (a b)"), ps[:, 2, 0:2 * BS],
                                    hThi[:, :, :].rearrange("p a b -> p (a b)"), ALU.subtract).then_inc(tlo_ready, 1)
                    rest_of_tokens(b + 1)
                    dve.wait_ge(t_full, b + 2)
                    places(b + 2)
                    rest_of_weights(b + 1, 1 - q, 1)
                    for half in range(2):
                        o = slice(half * 512, half * 512 + 512)
                        dve.wait_ge(yhi_ready, 2 * b + half + 1)
                        v.tensor_tensor(ylo[0:BS, o], ps[0:BS, 2 + half, :], yhi[0:BS, o], ALU.subtract).then_inc(ylo_ready, 1)
            for g in range(2, 4):
                dve.wait_ge(acc_full, g + 1)
                v.tensor_copy(acc_sb[:, 1, (g - 2) * 512:(g - 1) * 512], ps[:, 4 + g, :]).then_inc(acc_out, 1)
            for c in range(DC):
                if c % 2 == 0:
                    dve.wait_ge(y_full, c // 2 + 1)
                v.scalar_tensor_tensor(x[:, c, :], flat[:, c * T:(c + 1) * T], mod[:, 40 + c:41 + c], x[:, c, :],
                                       ALU.mult, ALU.add).then_inc(x_ready, 1)

        @block.gpsimd
        def _(pool):
            with pool.Fori(0, DEPTH) as l:
                for c in range(CC):
                    W(pool, "ln_act", 2 * c + 2, l)
                    nc.gpsimd.tensor_tensor(cat[:, 4 + c, :], lnv[:, c, :], lns[:, c, :], ALU.mult).then_inc(conv_out, 1)
                W(pool, "conv_out", CC, l)
            tt = nc.gpsimd.tensor_tensor
            lev = [c2[:, KLEV + P * s_:KLEV + P * (s_ + 1)].rearrange("p (a b) -> p a b", a=1).to_broadcast([P, 4, P])
                   for s_ in range(6)]

            def col(o, p):
                return tiny[:, o + GH * p:o + GH * p + GH].rearrange("p (a b) -> p a b", b=1).to_broadcast([P, GH, P])

            def scale_step(i):
                if i == 0:
                    pool.wait_ge(x_out, 8)
                    for p in range(2):
                        m = tt(gV[:, p], gV[:, p], col(48, p), ALU.mult)
                elif i == 1:
                    pool.wait_ge(gtot_ready, 1)
                    for p in range(2):
                        m = tt(kbg[:, p], gK[:, p], col(144, p), ALU.mult)
                elif i == 2:
                    for p in range(2):
                        m = tt(gK[:, p], gK[:, p], col(96, p), ALU.mult)
                else:
                    m = tt(gq[:, :, :], gq[:, :, :], GB[:, :, :], ALU.mult)
                m.then_inc(pool_scaled, 1)
                pool.wait_ge(pool_scaled, i + 1)

            pool.wait_ge(loaded2, 16)
            for m_ in range(24):
                s_, b = divmod(m_, 4)
                if m_ < 4:
                    pool.wait_ge(l_ready, m_ + 1)
                if m_ >= 2:
                    pool.wait_ge(wt_full, m_ - 1)
                tt(Ms[:, m_ % 2], MA[:, b // 2, 4 * (b % 2):4 * (b % 2) + 4, :], lev[s_], ALU.mult).then_inc(m_ready, 1)
                if m_ % 4 == 3 and m_ // 4 < 4:
                    if m_ == 3:
                        pool.wait_ge(qk_full, 4)
                    scale_step(m_ // 4)

            def rest_of_down(b, q):
                pool.wait_ge(whi_ready, 3 * b + 4)
                j = (RB0 + 3 * q + 2) % RING
                tt(wlo[j][:, :], ring[:, j, :], whi[q][2][:, :], ALU.subtract).then_inc(wlo_down, 1)

            pool.wait_ge(count_ready, 2)
            pairs = pool.value_load(lint[0:1, NBLK:NBLK + 1], min_val=1, max_val=NBLK // 2 - 1)
            with pool.Fori(0, pairs) as t:
                for q in range(2):
                    rest_of_down(2 * t + q, q)


def chunk_pairs(w, order):
    v = w.reshape(DC, P, -1, P)
    return [v[:, :, list(pair), :].transpose(1, 0, 2, 3).reshape(1, P, SLOT) for pair in order]


def first_block_stream(x):
    parts = []
    for l in range(DEPTH):
        w = x["w_in"][l]
        pairs = [(12 + c, 16 + c) for c in range(4)] + [(2 * i, 2 * i + 1) for i in range(6)]
        parts += chunk_pairs(w, pairs)
        parts += chunk_pairs(x["w_ada_2"][0], [(24 * l + 2 * i, 24 * l + 2 * i + 1) for i in range(ADA_SLOTS)])
        parts += chunk_pairs(x["w_out"][l], [(2 * i, 2 * i + 1) for i in range(4)])
        parts += chunk_pairs(x["w_gate_up"][l], [(i, FC + i) for i in range(FC)])
        v = x["w_down"][l].reshape(FC, P, DC, P)
        for half in range(2):
            for g in range(6):
                part = v[4 * g:4 * g + 4, :, 4 * half:4 * half + 4, :].transpose(1, 0, 2, 3).reshape(P, -1)
                parts.append(np.concatenate([part, np.zeros((P, SLOT - part.shape[1]), np.float32)], 1)[None])
    return parts


def columns(v, n):
    return v.reshape(n, P).T


def layer_params(x, l):
    lam = np.zeros((P, 4), np.float32)
    for i, k in enumerate(("lam_q1", "lam_k1", "lam_q2", "lam_k2")):
        lam[:HD, i] = x[k][l]
    init = 0.8 - 0.6 * math.exp(-0.3 * l)
    return np.concatenate([
        columns(x["norm1_g"][l], 8), columns(x["b_glu"][l], 8),
        x["conv_w"][l].reshape(TAPS, CC, P).transpose(2, 1, 0).reshape(P, CC * TAPS),
        columns(x["conv_b"][l], CC), columns(x["conv_ln_g"][l], CC), columns(x["conv_ln_b"][l], CC),
        x["subln_g"][l].reshape(P, 1), columns(x["norm2_g"][l], 8), lam,
        np.full((P, 1), init, np.float32), np.full((P, 1), 1.0 - init, np.float32)], 1)


def constants():
    rot = np.zeros((P, P), np.float32)
    for b in range(0, P, HD):
        for d in range(HD // 2):
            rot[b + HD // 2 + d, b + d] = -1.0
            rot[b + d, b + HD // 2 + d] = 1.0
    inv = np.float32(10000.0) ** (-np.arange(0, HD, 2, dtype=np.float32) / np.float32(HD))
    ang = np.arange(L, dtype=np.float32)[:, None] * inv[None, :]
    ang = np.tile(ang, (1, 4)).T
    mask = np.zeros((P, 3, L), np.float32)
    for t, (q0, rows) in enumerate(Q_TILES):
        mask[:, t, :] = np.where(np.arange(L)[None, :] <= q0 + np.arange(P)[:, None], 0.0, -1e30)
    return np.concatenate([np.ones((P, P), np.float32), np.eye(P, dtype=np.float32), rot,
                           np.cos(ang), np.sin(ang), mask.reshape(P, -1),
                           np.broadcast_to(np.tril(np.ones((8, 8)), -1).reshape(1, 64), (P, 64))], 1).astype(np.float32)


def constants2():
    i, j = np.arange(P)[:, None], np.arange(P)[None, :]
    parts = []
    for t in range(2):
        q, k = t * P + np.arange(P)[:, None], np.arange((t + 1) * P)[None, :]
        for window, dil in WINDOW_DILATION:
            d = q - k
            parts.append(np.where((d >= 0) & (d % dil == 0) & (d // dil <= window // dil), 0.0, NEG))
    for s in (1, 2, 4, 8, 16, 32):
        parts.append(((i // (2 * s) == j // (2 * s)) & (i % (2 * s) >= s) & (j % (2 * s) < s)) * 1.0)
    same = i // CHUNK == j // CHUNK
    parts.append(np.where(same & (i >= j), 0.0, NEG))
    parts.append(np.where(same & (j >= i), 0.0, NEG))
    return np.concatenate(parts, 1).astype(np.float32)


def constants3():
    i = np.arange(P)[:, None]
    before = (i < np.arange(P)[None, :]) * 1.0
    b = np.arange(NBLK)[None, :]
    rows = [before, np.ones((P, P)), np.zeros((P, P)), before, b, b * BS + FAR, np.arange(BS)[None, :],
            np.arange(T // BS)[None, :] * BS, 3 * i]
    return np.concatenate([np.broadcast_to(r, (P, r.shape[1])) for r in rows], 1).astype(np.float32)


def second_block_stream(x):
    parts = []
    w = x["w_in_2"][0]
    g = w[:, :4096]
    rest = w[:, 4112:]
    pairs = lambda n: [(2 * i, 2 * i + 1) for i in range(n)]
    parts += chunk_pairs(rest[:, :4608], pairs(18))
    parts += chunk_pairs(g, pairs(16))
    parts += chunk_pairs(rest[:, 4608:], pairs(8))
    v = x["w_up_dil_2"][0].reshape(4, P, DC, P)
    for m in range(2):
        parts.append(v[:, :, 4 * m:4 * m + 4, :].transpose(1, 0, 2, 3).reshape(1, P, SLOT))
    parts += chunk_pairs(x["w_up_gdn_2"][0], pairs(4))
    parts += chunk_pairs(x["w_out_2"][0], pairs(4))
    sets = [[x[f"w_sh_{k}_2"][0] for k in ("gate", "up", "down")]]
    sets += [[x[f"w_exp_{k}_2"][0, e] for k in ("gate", "up", "down")] for e in range(EXPERTS)]
    for g, u, d in sets:
        parts += chunk_pairs(g, [(0, 1)]) + chunk_pairs(u, [(0, 1)])
        parts.append(d.reshape(2, P, D).transpose(1, 0, 2).reshape(1, P, SLOT))
    return parts


def params2(x):
    def rows(a):
        return np.concatenate([a.reshape(GH, 1), np.zeros((P - GH, 1), np.float32)], 0)
    return np.concatenate([
        columns(x["g_mix_2"][0], 8), columns(x["g_ffn_2"][0], 8), columns(x["b_ada_2"][0], 48), columns(x["c_2"][0], 8),
        x["gdn_conv_w_2"][0].reshape(4, 24, P).transpose(2, 1, 0).reshape(P, 96),
        x["gdn_norm_g_2"][0].reshape(P, 1), x["dil_q_norm_g_2"][0].reshape(P, 1), x["dil_k_norm_g_2"][0].reshape(P, 1),
        rows(x["gdn_a_log_2"][0]), rows(x["gdn_dt_bias_2"][0]),
        np.broadcast_to(x["router_bias_2"][0][None, :], (P, EXPERTS))], 1)


def lay_out(x):
    tokens = np.concatenate([x["meta_tokens"], x["x"][0]], 0)
    return {
        "stream": np.concatenate(first_block_stream(x) + second_block_stream(x), 0),
        "par2": params2(x),
        "consts2": constants2(),
        "consts3": constants3(),
        "w_ba": x["w_in_2"][0][:, 4096:4112].reshape(DC, P, 16).transpose(1, 0, 2),
        "w_router": x["w_router_2"][0].reshape(DC, P, EXPERTS).transpose(1, 0, 2),
        "xT": tokens.T.reshape(DC, P, L).transpose(1, 0, 2),
        "par1": np.stack([layer_params(x, l) for l in range(DEPTH)], 1),
        "consts": constants(),
        "final_g": columns(x["final_g"], 8),
    }


def kernel(**inputs):
    import concourse.bacc as bacc
    from concourse.bass_utils import run_bass_kernel_spmd

    nc = bacc.Bacc("TRN2", target_bir_lowering=False, num_devices=1)
    arrays = {f"in_{n}": np.ascontiguousarray(a) for n, a in lay_out({k: np.asarray(a) for k, a in inputs.items()}).items()}
    args = {n[3:]: nc.dram_tensor(n, a.shape, F32, kind="ExternalInput").ap() for n, a in arrays.items()}
    args["out"] = nc.dram_tensor("out_xT", (P, DC, T), F32, kind="ExternalOutput").ap()
    build(nc, args)
    r = run_bass_kernel_spmd(nc, [arrays], core_ids=[0])
    return r.results[0]["out_xT"].transpose(2, 1, 0).reshape(1, T, D)
```
